# Optimizing a Trainium2 kernel written in Bass

```python
import jax, jax.numpy as jnp
from jax import lax
import numpy as np

D_MODEL = 1024
BATCH = 1
SEQ = 512
DEPTH = 2

LRU_WIDTH = D_MODEL
LRU_BLOCKS = 8
LRU_BLOCK_W = LRU_WIDTH // LRU_BLOCKS
CONV_W = 4
LRU_C = 8.0
MLA_HEADS = 8
QK_NOPE = 128
QK_ROPE = 64
QK_HEAD = QK_NOPE + QK_ROPE
V_HEAD = D_MODEL // MLA_HEADS
Q_RANK = 256
KV_RANK = 128
ROPE_THETA = 10000.0
Q_BLOCK = 128
D_FF = -(-8 * D_MODEL // (3 * 256)) * 256
EPS = 1e-6
D_IN = LRU_WIDTH + Q_RANK + KV_RANK + QK_ROPE + 2 * D_MODEL
IN_SPLIT_POINTS = (LRU_WIDTH,
                   LRU_WIDTH + Q_RANK,
                   LRU_WIDTH + Q_RANK + KV_RANK,
                   LRU_WIDTH + Q_RANK + KV_RANK + QK_ROPE,
                   LRU_WIDTH + Q_RANK + KV_RANK + QK_ROPE + D_MODEL)


def rms_norm(x, gain=None):
    xf = x.astype(jnp.float32)
    y = xf * lax.rsqrt(jnp.mean(xf * xf, axis=-1, keepdims=True) + EPS)
    if gain is not None:
        y = y * gain.astype(jnp.float32)
    return y.astype(x.dtype)

def rope_tables(positions):
    inv_freq = ROPE_THETA ** (-jnp.arange(0, QK_ROPE, 2, dtype=jnp.float32) / QK_ROPE)
    ang = positions.astype(jnp.float32)[..., None] * inv_freq
    return jnp.cos(ang), jnp.sin(ang)

def apply_rope(x, cos, sin):
    half = QK_ROPE // 2
    xf = x.astype(jnp.float32)
    x1, x2 = xf[..., :half], xf[..., half:]
    return jnp.concatenate([x1 * cos - x2 * sin, x2 * cos + x1 * sin], axis=-1).astype(x.dtype)

def causal_depthwise_conv(x, w, b):
    y = lax.conv_general_dilated(x, w[:, None, :].astype(x.dtype), window_strides=(1,),
                                 padding=((CONV_W - 1, 0),),
                                 dimension_numbers=('NWC', 'WIO', 'NWC'),
                                 feature_group_count=x.shape[-1])
    return y + b

def rg_lru(x, positions, w_a, b_a, w_x, b_x, a_param):
    B, S, _ = x.shape
    xf = x.astype(jnp.float32)
    xb = xf.reshape(B, S, LRU_BLOCKS, LRU_BLOCK_W)
    r = jax.nn.sigmoid(jnp.einsum('bsni,nij->bsnj', xb, w_a.astype(jnp.float32))
                       + b_a.astype(jnp.float32)).reshape(B, S, LRU_WIDTH)
    i = jax.nn.sigmoid(jnp.einsum('bsni,nij->bsnj', xb, w_x.astype(jnp.float32))
                       + b_x.astype(jnp.float32)).reshape(B, S, LRU_WIDTH)
    log_a = -LRU_C * r * jax.nn.softplus(-a_param.astype(jnp.float32))
    reset = (positions == 0)[..., None]
    a = jnp.where(reset, 0.0, jnp.exp(log_a))
    mult = jnp.where(reset, 1.0, jnp.sqrt(-jnp.expm1(2.0 * log_a)))
    b_in = xf * i * mult

    def combine(left, right):
        return (left[0] * right[0], right[0] * left[1] + right[1])

    _, h = lax.associative_scan(combine, (a, b_in), axis=1)
    return h.astype(x.dtype)

def causal_block_attention(q, k, v):
    B, S, H, Dk = q.shape
    nb = S // Q_BLOCK
    scale = QK_HEAD ** -0.5
    qb = q.reshape(B, nb, Q_BLOCK, H, Dk).transpose(1, 0, 2, 3, 4)
    k_idx = jnp.arange(S)

    def one_block(args):
        q_blk, blk = args
        s = jnp.einsum('bqhd,bkhd->bhqk', q_blk, k, preferred_element_type=jnp.float32) * scale
        q_idx = blk * Q_BLOCK + jnp.arange(Q_BLOCK)
        s = jnp.where(k_idx[None, :] <= q_idx[:, None], s, -jnp.inf)
        p = jax.nn.softmax(s, axis=-1)
        o = jnp.einsum('bhqk,bkhd->bqhd', p.astype(v.dtype), v, preferred_element_type=jnp.float32)
        return o.astype(v.dtype)

    o = lax.map(one_block, (qb, jnp.arange(nb)))
    return o.transpose(1, 0, 2, 3, 4).reshape(B, S, H, v.shape[-1])

def mla(q_down, kv_down, k_rope, cos, sin, q_norm_g, kv_norm_g, w_uq, w_ukv):
    B, S, _ = q_down.shape
    c_q = rms_norm(q_down, q_norm_g)
    q = jnp.einsum('bsr,rhd->bshd', c_q, w_uq)
    q = jnp.concatenate([q[..., :QK_NOPE],
                         apply_rope(q[..., QK_NOPE:], cos[:, :, None, :], sin[:, :, None, :])], axis=-1)
    c_kv = rms_norm(kv_down, kv_norm_g)
    kv = jnp.einsum('bsr,rhd->bshd', c_kv, w_ukv)
    k_pe = apply_rope(k_rope, cos, sin)
    k = jnp.concatenate([kv[..., :QK_NOPE],
                         jnp.broadcast_to(k_pe[:, :, None, :], (B, S, MLA_HEADS, QK_ROPE))], axis=-1)
    v = kv[..., QK_NOPE:]
    o = causal_block_attention(q, k, v)
    return o.reshape(B, S, MLA_HEADS * V_HEAD)

def hybrid_layer(x, c, positions, cos, sin, w_ada, b_ada, w_in, conv_w, conv_b,
                 lru_wa, lru_ba, lru_wx, lru_bx, lru_a_param, q_norm_g, kv_norm_g,
                 w_uq, w_ukv, w_out, w_ffn_in, w_ffn_out):
    mod = (c @ w_ada + b_ada)[:, None, :]
    sh_m, sc_m, g_m, sh_f, sc_f, g_f = jnp.split(mod, 6, axis=-1)
    h = rms_norm(x) * (1 + sc_m) + sh_m
    proj = h @ w_in
    x_lru, q_down, kv_down, k_rope, gate_a, gate_b = jnp.split(proj, IN_SPLIT_POINTS, axis=-1)
    y_a = rg_lru(causal_depthwise_conv(x_lru, conv_w, conv_b), positions,
                 lru_wa, lru_ba, lru_wx, lru_bx, lru_a_param)
    y_b = mla(q_down, kv_down, k_rope, cos, sin, q_norm_g, kv_norm_g, w_uq, w_ukv)
    y = jax.nn.sigmoid(gate_a) * y_a + jax.nn.sigmoid(gate_b) * y_b
    x = x + g_m * (y @ w_out)
    h = rms_norm(x) * (1 + sc_f) + sh_f
    gate, up = jnp.split(h @ w_ffn_in, 2, axis=-1)
    x = x + g_f * ((jax.nn.silu(gate) * up) @ w_ffn_out)
    return x

def first_inputs(seed: int = 0) -> dict:
    key = jax.random.key(seed)
    ks = jax.random.split(key, 24)
    f32 = jnp.float32
    x = jax.random.normal(ks[0], (BATCH, SEQ, D_MODEL), f32)
    c = jax.random.normal(ks[1], (BATCH, D_MODEL), f32)
    positions = jnp.broadcast_to(jnp.arange(SEQ, dtype=jnp.int32)[None, :], (BATCH, SEQ))
    w_ada = jax.random.normal(ks[2], (DEPTH, D_MODEL, 6 * D_MODEL), f32) * (0.3 * D_MODEL ** -0.5)
    b_ada = jax.random.normal(ks[3], (DEPTH, 6 * D_MODEL), f32) * 0.02
    w_in = jax.random.normal(ks[4], (DEPTH, D_MODEL, D_IN), f32) * D_MODEL ** -0.5
    conv_w = jax.random.normal(ks[5], (DEPTH, CONV_W, LRU_WIDTH), f32) * CONV_W ** -0.5
    conv_b = jax.random.normal(ks[6], (DEPTH, LRU_WIDTH), f32) * 0.01
    lru_wa = jax.random.normal(ks[7], (DEPTH, LRU_BLOCKS, LRU_BLOCK_W, LRU_BLOCK_W), f32) * LRU_BLOCK_W ** -0.5
    lru_ba = jax.random.normal(ks[8], (DEPTH, LRU_BLOCKS, LRU_BLOCK_W), f32) * 0.01
    lru_wx = jax.random.normal(ks[9], (DEPTH, LRU_BLOCKS, LRU_BLOCK_W, LRU_BLOCK_W), f32) * LRU_BLOCK_W ** -0.5
    lru_bx = jax.random.normal(ks[10], (DEPTH, LRU_BLOCKS, LRU_BLOCK_W), f32) * 0.01
    rad = jax.random.uniform(ks[11], (DEPTH, LRU_WIDTH), f32, minval=0.9, maxval=0.999)
    a0 = rad ** (1.0 / LRU_C)
    lru_a_param = jnp.log(a0) - jnp.log1p(-a0)
    q_norm_g = 1.0 + 0.01 * jax.random.normal(ks[12], (DEPTH, Q_RANK), f32)
    kv_norm_g = 1.0 + 0.01 * jax.random.normal(ks[13], (DEPTH, KV_RANK), f32)
    w_uq = jax.random.normal(ks[14], (DEPTH, Q_RANK, MLA_HEADS, QK_HEAD), f32) * Q_RANK ** -0.5
    w_ukv = jax.random.normal(ks[15], (DEPTH, KV_RANK, MLA_HEADS, QK_NOPE + V_HEAD), f32) * KV_RANK ** -0.5
    w_out = jax.random.normal(ks[16], (DEPTH, D_MODEL, D_MODEL), f32) * D_MODEL ** -0.5
    w_ffn_in = jax.random.normal(ks[17], (DEPTH, D_MODEL, 2 * D_FF), f32) * D_MODEL ** -0.5
    w_ffn_out = jax.random.normal(ks[18], (DEPTH, D_FF, D_MODEL), f32) * D_FF ** -0.5
    final_norm_g = 1.0 + 0.01 * jax.random.normal(ks[19], (D_MODEL,), f32)
    return {'x': x, 'c': c, 'positions': positions, 'w_ada': w_ada, 'b_ada': b_ada,
            'w_in': w_in, 'conv_w': conv_w, 'conv_b': conv_b, 'lru_wa': lru_wa,
            'lru_ba': lru_ba, 'lru_wx': lru_wx, 'lru_bx': lru_bx, 'lru_a_param': lru_a_param,
            'q_norm_g': q_norm_g, 'kv_norm_g': kv_norm_g, 'w_uq': w_uq, 'w_ukv': w_ukv,
            'w_out': w_out, 'w_ffn_in': w_ffn_in, 'w_ffn_out': w_ffn_out,
            'final_norm_g': final_norm_g}

def first_block(x, c, positions, w_ada, b_ada, w_in, conv_w, conv_b, lru_wa, lru_ba, lru_wx,
              lru_bx, lru_a_param, q_norm_g, kv_norm_g, w_uq, w_ukv, w_out, w_ffn_in,
              w_ffn_out, final_norm_g):
    cos, sin = rope_tables(positions)
    for l in range(DEPTH):
        x = hybrid_layer(x, c, positions, cos, sin, w_ada[l], b_ada[l], w_in[l], conv_w[l],
                         conv_b[l], lru_wa[l], lru_ba[l], lru_wx[l], lru_bx[l], lru_a_param[l],
                         q_norm_g[l], kv_norm_g[l], w_uq[l], w_ukv[l], w_out[l],
                         w_ffn_in[l], w_ffn_out[l])
    return rms_norm(x, final_norm_g)


DEPTH_2 = 1

D_MIX = D_MODEL
MLSTM_WIDTH = D_MIX // 2
MLSTM_HEADS = 4
MLSTM_HEAD_DIM = MLSTM_WIDTH // MLSTM_HEADS
MLSTM_CHUNK = 64
CONV_WIDTH = 4
POOL_WIDTH = D_MIX - MLSTM_WIDTH
POOL_WINDOWS = (2, 4, 8, 16)
POOL_GROUPS = len(POOL_WINDOWS)
POOL_GROUP_DIM = POOL_WIDTH // POOL_GROUPS
N_IN = 4 * MLSTM_WIDTH + 2 * MLSTM_HEADS + POOL_WIDTH
N_EXPERTS = 32
TOP_K = 4
D_FF_2 = D_MODEL
SWIGLU_LIMIT = 7.0
SWIGLU_ALPHA = 1.702
EXPERT_BLOCK = 128
EPS_2 = 1e-5


def rmsnorm(x, g):
    xf = x.astype(jnp.float32)
    y = xf * lax.rsqrt(jnp.mean(xf * xf, axis=-1, keepdims=True) + EPS_2)
    return (y * g.astype(jnp.float32)).astype(x.dtype)

def causal_depthwise_conv_2(u, w):
    k = w.shape[0]
    return lax.conv_general_dilated(
        u, w[:, None, :].astype(u.dtype), window_strides=(1,), padding=[(k - 1, 0)],
        dimension_numbers=("NWC", "WIO", "NWC"), feature_group_count=u.shape[-1])

def mlstm_chunkwise(q, k, v, ig, lf):
    B, H, S, Dh = q.shape
    L = MLSTM_CHUNK
    NC = S // L
    q = q.reshape(B, H, NC, L, Dh)
    k = k.reshape(B, H, NC, L, Dh)
    v = v.reshape(B, H, NC, L, Dh)
    ig = ig.reshape(B, H, NC, L)
    lf = lf.reshape(B, H, NC, L)
    b = jnp.cumsum(lf, axis=-1)
    b_tot = b[..., -1]

    g = b_tot[..., None] - b + ig
    m_loc = jnp.max(g, axis=-1)
    w_loc = jnp.exp(g - m_loc[..., None])
    C_loc = jnp.einsum("bhclk,bhclv->bhckv", w_loc[..., None] * k, v)
    n_loc = jnp.einsum("bhcl,bhclk->bhck", w_loc, k)

    def step(carry, inp):
        C, n, m = carry
        C_l, n_l, m_l, bt = inp
        m_new = jnp.maximum(bt + m, m_l)
        s_old = jnp.exp(bt + m - m_new)
        s_loc = jnp.exp(m_l - m_new)
        C_new = s_old[..., None, None] * C + s_loc[..., None, None] * C_l
        n_new = s_old[..., None] * n + s_loc[..., None] * n_l
        return (C_new, n_new, m_new), (C, n, m)

    init = (jnp.zeros((B, H, Dh, Dh), jnp.float32),
            jnp.zeros((B, H, Dh), jnp.float32),
            jnp.zeros((B, H), jnp.float32))
    xs = (jnp.moveaxis(C_loc, 2, 0), jnp.moveaxis(n_loc, 2, 0),
          jnp.moveaxis(m_loc, 2, 0), jnp.moveaxis(b_tot, 2, 0))
    _, (C_in, n_in, m_in) = lax.scan(step, init, xs)
    C_in = jnp.moveaxis(C_in, 0, 2)
    n_in = jnp.moveaxis(n_in, 0, 2)
    m_in = jnp.moveaxis(m_in, 0, 2)

    causal = jnp.tril(jnp.ones((L, L), dtype=bool))
    log_d = b[..., :, None] - b[..., None, :] + ig[..., None, :]
    log_d = jnp.where(causal, log_d, -jnp.inf)
    a = b + m_in[..., None]
    m_out = jnp.maximum(a, jnp.max(log_d, axis=-1))
    s = jnp.einsum("bhcld,bhcrd->bhclr", q, k) * jnp.exp(log_d - m_out[..., None])
    inter = jnp.exp(a - m_out)
    num = (jnp.einsum("bhclr,bhcrv->bhclv", s, v)
           + inter[..., None] * jnp.einsum("bhcld,bhcdv->bhclv", q, C_in))
    den = jnp.sum(s, axis=-1) + inter * jnp.einsum("bhcld,bhcd->bhcl", q, n_in)
    h = num / jnp.maximum(jnp.abs(den), jnp.exp(-m_out))[..., None]
    return h.reshape(B, H, S, Dh)

def multiscale_pool(u, pool_w, pool_scale):
    B, S, _ = u.shape
    uf = u.astype(jnp.float32).reshape(B, S, POOL_GROUPS, POOL_GROUP_DIM)
    cs = jnp.concatenate([jnp.zeros((B, 1, POOL_GROUPS, POOL_GROUP_DIM), jnp.float32),
                          jnp.cumsum(uf, axis=1)], axis=1)
    t = jnp.arange(S)
    pooled = []
    for gi, w in enumerate(POOL_WINDOWS):
        c = cs[:, :, gi]
        c_lo = jnp.concatenate([jnp.zeros((B, w - 1, POOL_GROUP_DIM), jnp.float32),
                                c[:, :S - w + 1]], axis=1)
        cnt = jnp.minimum(t + 1, w).astype(jnp.float32)
        pooled.append((c[:, 1:] - c_lo) / cnt[None, :, None])
    pooled = jnp.stack(pooled, axis=2) - uf
    mixed = jnp.einsum("bsgc,gcd->bsgd", pooled, pool_w.astype(jnp.float32))
    mixed = mixed.reshape(B, S, POOL_WIDTH) * pool_scale.astype(jnp.float32)
    return mixed.astype(u.dtype)

def hybrid_mixer(h, w_in, ig_b, fg_b, conv_w, head_norm_g, pool_w, pool_scale, w_out):
    B, S, _ = h.shape
    W, H, Dh = MLSTM_WIDTH, MLSTM_HEADS, MLSTM_HEAD_DIM
    p = h @ w_in
    qk = p[..., :2 * W]
    v = p[..., 2 * W:3 * W]
    o = p[..., 3 * W:4 * W]
    gates = p[..., 4 * W:4 * W + 2 * H].astype(jnp.float32)
    u = p[..., 4 * W + 2 * H:]

    qk = jax.nn.silu(causal_depthwise_conv_2(qk, conv_w))

    def to_heads(t):
        return t.reshape(B, S, H, Dh).transpose(0, 2, 1, 3).astype(jnp.float32)

    q = to_heads(qk[..., :W])
    k = to_heads(qk[..., W:]) * (Dh ** -0.5)
    vh = to_heads(v)
    ig = (gates[..., :H] + ig_b.astype(jnp.float32)).transpose(0, 2, 1)
    lf = jax.nn.log_sigmoid(gates[..., H:] + fg_b.astype(jnp.float32)).transpose(0, 2, 1)
    hm = mlstm_chunkwise(q, k, vh, ig, lf)
    mu = jnp.mean(hm, axis=-1, keepdims=True)
    var = jnp.mean(jnp.square(hm - mu), axis=-1, keepdims=True)
    hm = (hm - mu) * lax.rsqrt(var + EPS_2)
    hm = hm.transpose(0, 2, 1, 3).reshape(B, S, W) * head_norm_g.astype(jnp.float32)
    y_m = (jax.nn.sigmoid(o.astype(jnp.float32)) * hm).astype(h.dtype)

    y_p = multiscale_pool(u, pool_w, pool_scale)

    return jnp.concatenate([y_m, y_p], axis=-1) @ w_out

def moe_ffn(h, w_router, b_router, w_gate, b_gate, w_up, b_up, w_down, b_down):
    B, S, D = h.shape
    T = B * S
    xt = h.reshape(T, D)
    logits = (xt @ w_router + b_router).astype(jnp.float32)
    top_vals, top_idx = lax.top_k(logits, TOP_K)
    top_gates = jax.nn.softmax(top_vals, axis=-1)

    A = T * TOP_K
    flat_expert = top_idx.reshape(A)
    flat_token = jnp.repeat(jnp.arange(T, dtype=jnp.int32), TOP_K)
    flat_gate = top_gates.reshape(A)
    order = jnp.argsort(flat_expert)
    s_expert = flat_expert[order]
    s_token = flat_token[order]
    s_gate = flat_gate[order]

    counts = jax.ops.segment_sum(jnp.ones((A,), jnp.int32), flat_expert, num_segments=N_EXPERTS)
    group_start = jnp.cumsum(counts) - counts
    padded = ((counts + EXPERT_BLOCK - 1) // EXPERT_BLOCK) * EXPERT_BLOCK
    padded_end = jnp.cumsum(padded)
    padded_start = padded_end - padded
    rank = jnp.arange(A, dtype=jnp.int32) - group_start[s_expert]
    dest = padded_start[s_expert] + rank

    n_blocks = -(-A // EXPERT_BLOCK) + N_EXPERTS
    P = n_blocks * EXPERT_BLOCK
    tok_buf = jnp.full((P,), T, jnp.int32).at[dest].set(s_token)
    gate_buf = jnp.zeros((P,), jnp.float32).at[dest].set(s_gate)
    block_start = jnp.arange(n_blocks, dtype=jnp.int32) * EXPERT_BLOCK
    block_expert = jnp.minimum(jnp.searchsorted(padded_end, block_start, side="right"),
                               N_EXPERTS - 1).astype(jnp.int32)

    x_pad = jnp.concatenate([xt, jnp.zeros((1, D), xt.dtype)], axis=0)
    x_buf = x_pad[tok_buf].reshape(n_blocks, EXPERT_BLOCK, D)

    def expert_block(args):
        xb, e = args
        gate = xb @ w_gate[e] + b_gate[e]
        up = xb @ w_up[e] + b_up[e]
        gate = jnp.minimum(gate, SWIGLU_LIMIT)
        up = jnp.clip(up, -SWIGLU_LIMIT, SWIGLU_LIMIT)
        glu = gate * jax.nn.sigmoid(SWIGLU_ALPHA * gate)
        return (glu * (up + 1.0)) @ w_down[e] + b_down[e]

    y_buf = lax.map(expert_block, (x_buf, block_expert)).reshape(P, D)
    y_buf = y_buf * gate_buf[:, None].astype(y_buf.dtype)
    out = jax.ops.segment_sum(y_buf, tok_buf, num_segments=T + 1)[:T]
    return out.reshape(B, S, D).astype(h.dtype)

def second_inputs(seed: int = 0) -> dict:
    key = jax.random.key(seed)
    ks = jax.random.split(key, 20)
    f32 = jnp.float32
    L_, D, E, F, H = DEPTH_2, D_MODEL, N_EXPERTS, D_FF_2, MLSTM_HEADS
    nrm = lambda k, shape, s: jax.random.normal(k, shape, f32) * s
    x = jax.random.normal(ks[0], (BATCH, SEQ, D), f32)
    norm1_g = 1.0 + nrm(ks[1], (L_, D), 0.02)
    w_in = nrm(ks[2], (L_, D, N_IN), D ** -0.5)
    ig_b = nrm(ks[3], (L_, H), 0.1)
    fg_b = jnp.broadcast_to(jnp.linspace(3.0, 6.0, H, dtype=f32), (L_, H)) + nrm(ks[4], (L_, H), 0.1)
    conv_w = nrm(ks[5], (L_, CONV_WIDTH, 2 * MLSTM_WIDTH), CONV_WIDTH ** -0.5)
    head_norm_g = 1.0 + nrm(ks[6], (L_, MLSTM_WIDTH), 0.02)
    pool_w = nrm(ks[7], (L_, POOL_GROUPS, POOL_GROUP_DIM, POOL_GROUP_DIM), POOL_GROUP_DIM ** -0.5)
    pool_scale = 1.0 + nrm(ks[8], (L_, POOL_WIDTH), 0.02)
    w_out = nrm(ks[9], (L_, D_MIX, D), D_MIX ** -0.5)
    norm2_g = 1.0 + nrm(ks[10], (L_, D), 0.02)
    w_router = nrm(ks[11], (L_, D, E), D ** -0.5)
    b_router = nrm(ks[12], (L_, E), 0.01)
    w_gate = nrm(ks[13], (L_, E, D, F), D ** -0.5)
    b_gate = nrm(ks[14], (L_, E, F), 0.01)
    w_up = nrm(ks[15], (L_, E, D, F), D ** -0.5)
    b_up = nrm(ks[16], (L_, E, F), 0.01)
    w_down = nrm(ks[17], (L_, E, F, D), F ** -0.5)
    b_down = nrm(ks[18], (L_, E, D), 0.01)
    normf_g = 1.0 + nrm(ks[19], (D,), 0.02)
    return {"x": x, "norm1_g": norm1_g, "w_in": w_in, "ig_b": ig_b, "fg_b": fg_b,
            "conv_w": conv_w, "head_norm_g": head_norm_g, "pool_w": pool_w,
            "pool_scale": pool_scale, "w_out": w_out, "norm2_g": norm2_g,
            "w_router": w_router, "b_router": b_router, "w_gate": w_gate,
            "b_gate": b_gate, "w_up": w_up, "b_up": b_up, "w_down": w_down,
            "b_down": b_down, "normf_g": normf_g}

def second_block(x, norm1_g, w_in, ig_b, fg_b, conv_w, head_norm_g, pool_w, pool_scale,
              w_out, norm2_g, w_router, b_router, w_gate, b_gate, w_up, b_up,
              w_down, b_down, normf_g):
    for l in range(DEPTH_2):
        h = rmsnorm(x, norm1_g[l])
        x = x + hybrid_mixer(h, w_in[l], ig_b[l], fg_b[l], conv_w[l], head_norm_g[l],
                             pool_w[l], pool_scale[l], w_out[l])
        h = rmsnorm(x, norm2_g[l])
        x = x + moe_ffn(h, w_router[l], b_router[l], w_gate[l], b_gate[l], w_up[l],
                        b_up[l], w_down[l], b_down[l])
    return rmsnorm(x, normf_g)


def setup_inputs(seed=0):
    out = dict(first_inputs(seed))
    for name, value in second_inputs(seed + 1).items():
        if name != "x":
            out[name + "_2"] = value
    return out


def reference(
    x, c, positions, w_ada, b_ada, w_in, conv_w, conv_b, lru_wa, lru_ba, lru_wx, lru_bx,
    lru_a_param, q_norm_g, kv_norm_g, w_uq, w_ukv, w_out, w_ffn_in, w_ffn_out, final_norm_g,
    norm1_g_2, w_in_2, ig_b_2, fg_b_2, conv_w_2, head_norm_g_2, pool_w_2, pool_scale_2, w_out_2,
    norm2_g_2, w_router_2, b_router_2, w_gate_2, b_gate_2, w_up_2, b_up_2, w_down_2, b_down_2,
    normf_g_2,
):
    x = first_block(
        x, c, positions, w_ada, b_ada, w_in, conv_w, conv_b, lru_wa, lru_ba, lru_wx, lru_bx,
        lru_a_param, q_norm_g, kv_norm_g, w_uq, w_ukv, w_out, w_ffn_in, w_ffn_out, final_norm_g,
    )
    return second_block(
        x, norm1_g_2, w_in_2, ig_b_2, fg_b_2, conv_w_2, head_norm_g_2, pool_w_2, pool_scale_2,
        w_out_2, norm2_g_2, w_router_2, b_router_2, w_gate_2, b_gate_2, w_up_2, b_up_2,
        w_down_2, b_down_2, normf_g_2,
    )


_drawn_inputs = setup_inputs


def setup_inputs(seed=0):
    import zlib

    import numpy as np

    out = dict(_drawn_inputs(seed))
    spreads = {}
    factors = {'lru_ba': 8.0,
     'lru_bx': 4.388,
     'q_norm_g': 8.0,
     'kv_norm_g': 5.631,
     'ig_b_2': 64.0,
     'b_gate_2': 8.0,
     'b_up_2': 24.771,
     'b_down_2': 8.0,
     'head_norm_g_2': 2.855}
    for name, (base, spread) in spreads.items():
        noise = np.random.default_rng([zlib.crc32(name.encode()), seed]).standard_normal(out[name].shape)
        drawn = base * np.exp(spread * noise) if base else spread * noise
        out[name] = __import__('jax').numpy.asarray(drawn.astype(out[name].dtype))
    for name, factor in factors.items():
        out[name] = (out[name] * factor).astype(out[name].dtype)
    return out
```

```python
from contextlib import ExitStack
import numpy as np
import concourse.bass as bass
from concourse import mybir

F32 = mybir.dt.float32
F32R = mybir.dt.float32r
BF16 = mybir.dt.bfloat16
I32 = mybir.dt.int32
U32 = mybir.dt.uint32
ACT = mybir.ActivationFunctionType
ALU = mybir.AluOpType
AX = mybir.AxisListType

P = 128
D = 1024
S = 512
KD = D // P
NT = S // P
DEPTH = 2
HEADS = 8
NOPE, ROPE = 128, 64
QR, KVR = 256, 128
DFF = 2816
NF = DFF // P // 2
C_Q = D
C_KV = D + QR
C_KR = C_KV + KVR
C_GA = C_KR + ROPE
C_GB = C_GA + D
KB = 1024
LRU_C = 8.0
EPS = 1e-6

V_BADA, V_CW, V_CB, V_BA, V_BX, V_AP, V_QG, V_KVG = 0, 48, 80, 88, 96, 104, 112, 114
NVEC = 115
K_ID, K_J2, K_ONE = 0, 128, 256
K_INVF, K_SG, K_PH, K_E6, K_E5, K_MOD = 384, 385, 386, 387, 388, 389
K_KEPT = 390
K_MASK, K_TRI, K_LT = 390, 518, 646
K_INV, K_I32, K_I48 = 774, 790, 822
K_I128 = 872
NK = 1000

RAW_SLOTS, W_SLOTS = 4, 3
SLOT = 2048


class Signals:

    def __init__(self, nc, ctx, names, at):
        self.sem = {n: ctx.enter_context(nc.semaphore(n)) for n in names.split()}
        self.count = {n: 0 for n in self.sem}
        self.at, self.known = at, dict(at)

    def inc(self, name, number=None, also=(), n=1):
        self.count[name] += n
        for key in [(name, number), *also]:
            self.at[key] = (name, self.count[name])
        return self.sem[name], n

    def event(self, name, number=None):
        sem, value = self.known[name, number] if self.known else (next(iter(self.sem)), 1)
        return self.sem[sem], value

    def last(self, name):
        return self.sem[name], self.count[name]


def layer_chunks():
    out = [("ada", i, False) for i in range(8)]
    out += [("lru", i, True) for i in range(4)]
    out += [("q", 0, True), ("kv", 0, True)]
    out += [("ga", i, True) for i in range(4)] + [("gb", i, True) for i in range(4)]
    out += [("uq", 0, True), ("uq", 1, True), ("ukv", 0, True)]
    out += [("ada", i, False) for i in range(8, 24)]
    out += [("out", i, True) for i in range(4)]
    for half in range(2):
        out += [("fi", half * NF + j, True) for j in range(NF)]
        out += [("fo", half * KD + j, True) for j in range(KD)]
    return out


CHUNKS = layer_chunks()
W_CHUNKS = [c for c in CHUNKS if c[2]]
W_INDEX = {(k, i): n for n, (k, i, _) in enumerate(W_CHUNKS)}
POSITION = {(k, i): n for n, (k, i, _) in enumerate(CHUNKS)}
GROUPS_OF = {"lru": 2, "q": 2, "kv": 2, "ga": 2, "gb": 2, "uq": 0, "ukv": 8, "out": 2, "fi": 2, "fo": 1}


def first_groups():
    first, g = {}, 0
    for kind, i, _ in W_CHUNKS:
        first[kind, i] = g
        g += GROUPS_OF[kind]
    return first


FIRST_GROUP = first_groups()
P_AT = [0, 128, 384, 768]
T_AT = [0, 512, 896, 1152]


def split3(pe, out, lhi, llo, rhi, rlo, start, stop):
    pe.matmul(out, lhi, rhi, start=start, stop=False)
    pe.matmul(out, lhi, rlo, start=False, stop=False)
    return pe.matmul(out, llo, rhi, start=False, stop=stop)

def log1p(v, sg, sem, out, u, s, p):
    v.tensor_scalar(s, u, 2.0, None, ALU.add).then_inc(*sg.inc(sem))
    v.wait_ge(*sg.last(sem))
    v.reciprocal(s, s).then_inc(*sg.inc(sem))
    v.wait_ge(*sg.last(sem))
    v.tensor_tensor(s, s, u, ALU.mult).then_inc(*sg.inc(sem))
    v.wait_ge(*sg.last(sem))
    v.tensor_tensor(p, s, s, ALU.mult).then_inc(*sg.inc(sem))
    v.wait_ge(*sg.last(sem))
    v.tensor_scalar(out, p, 1.0 / 17, 1.0 / 15, ALU.mult, ALU.add).then_inc(*sg.inc(sem))
    v.wait_ge(*sg.last(sem))
    for n in (13, 11, 9, 7, 5, 3, 1):
        v.tensor_tensor(out, out, p, ALU.mult).then_inc(*sg.inc(sem))
        v.wait_ge(*sg.last(sem))
        v.tensor_scalar(out, out, 1.0 / n, None, ALU.add).then_inc(*sg.inc(sem))
        v.wait_ge(*sg.last(sem))
    v.scalar_tensor_tensor(out, out, 2.0, s, ALU.mult, ALU.mult).then_inc(*sg.inc(sem))
    v.wait_ge(*sg.last(sem))


LAYER_SIGNALS = """step_act step_dve raw_in0 raw_in1 raw_in2 raw_in3 vec_in lruw_in raw_used w_hi pe_step
    act_free dve_free act_out dve_out act_sq act_root act_hi dve_h dve_lo act_exp act_pt act_qk
    dve_max dve_p dve_qa dve_pt dve_y ada_out parted"""


def layer_loads(sp, l, sg, m, W):
    sp.dma_start(m["vec"][:], W["vecs"][l]).then_inc(*sg.inc("vec_in", n=16))
    for i, name in enumerate(("lru_wa", "lru_wx")):
        sp.dma_start(m["lruw"][:, 8 * i:8 * i + 8, :], W[name][l].rearrange("g i j -> i g j")).then_inc(*sg.inc("lruw_in", i, n=16))
    by_k = lambda name: W[name][l].rearrange("(k p) n -> p k n", p=P)
    w_in, w_ada, w_out = by_k("w_in"), by_k("w_ada"), by_k("w_out")
    w_fi, w_fo = by_k("w_ffn_in"), by_k("w_ffn_out")
    w_uq = W["w_uq"][l].rearrange("(k p) h d -> p k h d", p=P)
    w_ukv = W["w_ukv"][l]
    h = ROPE // 2
    for n, (kind, i, _) in enumerate(CHUNKS):
        slot = n % RAW_SLOTS
        if n >= RAW_SLOTS:
            sp.wait_ge(*sg.event("raw_used", n - RAW_SLOTS))
        raw = m["RAW"][:, slot, :]
        by256 = raw.rearrange("p (k n) -> p k n", k=KD)
        if kind == "ada":
            parts = [(by256, w_ada[:, :, i * 256:(i + 1) * 256])]
        elif kind in ("lru", "q", "ga", "gb"):
            c = {"lru": 0, "q": C_Q, "ga": C_GA, "gb": C_GB}[kind] + i * 256
            parts = [(by256, w_in[:, :, c:c + 256])]
        elif kind == "kv":
            parts = [(by256[:, :, 0:192], w_in[:, :, C_KV:C_KV + 192]),
                     (by256[:, :, 192:192 + h], w_in[:, :, C_KR + h:C_KR + ROPE]),
                     (by256[:, :, 192 + h:256], w_in[:, :, C_KR:C_KR + h])]
        elif kind == "uq":
            parts = []
            for k in range(2):
                dst = raw[:, k * 1024:(k + 1) * 1024].rearrange("p (h n) -> p h n", h=4)
                src = w_uq[:, k, 4 * i:4 * i + 4, :]
                parts += [(dst[:, :, 0:192], src), (dst[:, :, 192:192 + h], src[:, :, 160:192]),
                          (dst[:, :, 192 + h:256], src[:, :, 128:160])]
        elif kind == "ukv":
            parts = [(raw[:, 0:1024].rearrange("p (h n) -> p h n", h=HEADS), w_ukv[:, :, 0:128]),
                     (raw[:, 1024:2048].rearrange("p (h n) -> p h n", h=HEADS), w_ukv[:, :, 128:256])]
        elif kind == "out":
            parts = [(by256, w_out[:, :, i * 256:(i + 1) * 256])]
        elif kind == "fi":
            parts = [(by256[:, :, 0:128], w_fi[:, :, i * P:(i + 1) * P]),
                     (by256[:, :, 128:256], w_fi[:, :, DFF + i * P:DFF + (i + 1) * P])]
        else:
            half, j = divmod(i, KD)
            parts = [(raw[:, 0:NF * P].rearrange("p (k n) -> p k n", k=NF),
                      w_fo[:, half * NF:(half + 1) * NF, j * P:(j + 1) * P])]
        for dst, src in parts:
            sp.dma_start(dst, src).then_inc(*sg.inc(f"raw_in{slot}", also=[("raw", n)], n=16))


def score_bank(b, q):
    w = (q + 1) * P
    return {3: b[0][:, 0:w], 2: b[1][:, 0:w], 0: b[1][:, 384:512], 1: b[2][:, 0:w]}[q]


Q_ORDER = (1, 0, 2, 3)
FLOATS = {"fo": NF * P}
SCALE = (NOPE + ROPE) ** -0.5


def layer_act(act, sg, m, b, chunks=None):
    K, X, HH = m["K"], m["X"], m["HH"]

    fed = [0]

    def feed(upto):
        while fed[0] <= min(upto, len(W_CHUNKS) - 1):
            n = fed[0]
            kind, i, _ = W_CHUNKS[n]
            c, size = POSITION[kind, i], FLOATS.get(kind, SLOT)
            act.wait_ge(*sg.event("raw", c))
            if n >= W_SLOTS:
                act.wait_ge(*sg.event("w_used", n - W_SLOTS))
            act.activation(m["WHI"][:, n % W_SLOTS, 0:size], m["RAW"][:, c % RAW_SLOTS, 0:size], ACT.Copy).then_inc(*sg.inc("w_hi", n))
            fed[0] += 1

    def norm(t, eps):
        for k in range(KD):
            if (t, k) >= (0, 2):
                act.wait_ge(*sg.event("sq_used", (t, k - 2) if k >= 2 else (t - 1, KD - 2 + k)))
            act.activation(m["sq"][:, k % 2, :], X[:, k, :], ACT.Square).then_inc(*sg.inc("act_sq", (t, k)))
        act.wait_ge(*sg.event("stat", t))
        act.activation(m["rstd"][:], b[4][:], ACT.Sqrt, bias=K[:, eps:eps + 1], scale=1.0 / D).then_inc(*sg.inc("act_root", t))
        for k in range(KD):
            act.wait_ge(*sg.event("h", (t, k)))
            act.activation(HH[:, k, :], m["nh"][:, k % 2, :], ACT.Copy).then_inc(*sg.inc("act_hi", ("h", t, k)))

    act.wait_ge(*sg.event("absa"))
    act.activation(m["sm"][:, 8:16], m["sm"][:, 0:8], ACT.Exp, scale=-1.0).then_inc(*sg.inc("act_out", "expa"))
    norm(0, K_E6)
    feed(1)

    def lru_tail(i):
        act.wait_ge(*sg.event("gate_pre", i))
        if i:
            act.wait_ge(*sg.event("lru_done", i - 1))
        act.wait_ge(*sg.event("hb"))
        hb = m["hb"]
        for n in range(2):
            blk = 2 * i + n
            act.activation(m["tr"][:, n, :], b[4 + 2 * n][:], ACT.Tanh, scale=0.5, bias=hb[:, blk:blk + 1])
            ins = act.activation(m["ti"][:, n, :], b[5 + 2 * n][:], ACT.Tanh, scale=0.5, bias=hb[:, 8 + blk:9 + blk])
        ins.then_inc(*sg.inc("act_out", ("lru_tanh", i)))
        act.wait_ge(*sg.event("act_out", ("lru_tanh", i)))
        for n in range(2):
            r = hb[:, 16 + 2 * i + n:17 + 2 * i + n]
            ins = act.activation(m["la"][:, n, :], m["tr"][:, n, :], ACT.Exp, scale=r, bias=r)
        ins.then_inc(*sg.inc("step_act"))
        act.wait_ge(*sg.last("step_act"))
        for n in range(2):
            r = hb[:, 24 + 2 * i + n:25 + 2 * i + n]
            act.activation(m["tr"][:, n, :], m["tr"][:, n, :], ACT.Tanh, scale=r, bias=r)
            ins = act.activation(m["sq2"][:, n, :], m["la"][:, n, :], ACT.Square)
        ins.then_inc(*sg.inc("act_out", ("lru_square", i)))
        act.wait_ge(*sg.event("lru_var", i))
        for n in range(2):
            ins = act.activation(m["tr"][:, n, :], m["tr"][:, n, :], ACT.Sqrt)
        ins.then_inc(*sg.inc("act_out", ("lru_root", i)))

    for n, (kind, i, _) in enumerate(W_CHUNKS):
        if kind == "uq":
            break
        feed(n + 2)
        g = FIRST_GROUP[kind, i]
        if kind == "lru":
            for j in range(2):
                act.wait_ge(*sg.event("acc", g + j))
                if i:
                    act.wait_ge(*sg.event("xc", 2 * i + j - 2))
                act.activation(m["xpad"][:, j, 3:3 + S], b[(g + j) % 4][:], ACT.Copy).then_inc(*sg.inc("act_free", g + j, also=[("free", g + j)]))
            if i:
                lru_tail(i - 1)
        elif kind == "q":
            for j in range(2):
                act.wait_ge(*sg.event("acc", g + j))
                act.activation(m["qraw"][:, j, :], b[(g + j) % 4][:], ACT.Copy).then_inc(*sg.inc("act_free", g + j, also=[("free", g + j)]))
            lru_tail(3)
        elif kind == "kv":
            act.wait_ge(*sg.event("acc", g))
            act.activation(m["kvraw"][:], b[g % 4][:], ACT.Copy).then_inc(*sg.inc("act_free", g, also=[("free", g)]))
            act.wait_ge(*sg.event("act_free", g))
            act.wait_ge(*sg.event("lru_done", 3))
            for j in range(2):
                act.activation(m["sq2"][:, j, :], m["qraw"][:, j, :], ACT.Square)
            act.activation(m["ti"][:, 0, :], m["kvraw"][:], ACT.Square).then_inc(*sg.inc("act_sq", "qkv"))
        elif kind == "ga":
            for j in range(2):
                act.wait_ge(*sg.event("acc", g + j))
                if i:
                    act.wait_ge(*sg.event("ga_used", 2 * i + j - 2))
                act.activation(m["tg"][:, j, :], b[(g + j) % 4][:], ACT.Tanh, scale=0.5).then_inc(*sg.inc("act_free", g + j, also=[("free", g + j)]))
            if i == 1:
                act.wait_ge(*sg.event("stat", "qkv"))
                act.activation(m["rq"][:, 0, :], b[4][:], ACT.Sqrt, bias=K[:, K_E6:K_E6 + 1], scale=1.0 / QR)
                act.activation(m["rq"][:, 1, :], b[5][:], ACT.Sqrt, bias=K[:, K_E6:K_E6 + 1], scale=1.0 / KVR).then_inc(*sg.inc("act_root", "qkv"))
                act.wait_ge(*sg.event("cq"))
                act.activation(m["cqh"][:], m["qraw"][:], ACT.Copy)
                act.activation(m["ckvh"][:], m["kvraw"][:], ACT.Copy).then_inc(*sg.inc("act_hi", "cq"))
        elif kind == "gb":
            act.wait_ge(*sg.event("gate_pre", 3))
            for j in range(2):
                act.wait_ge(*sg.event("acc", g + j))
                act.activation(m["tgb"][:, 2 * i + j, :], b[(g + j) % 4][:], ACT.Tanh, scale=0.5).then_inc(*sg.inc("act_free", g + j, also=[("free", g + j)]))

    feed(W_INDEX["ukv", 0])
    g = FIRST_GROUP["ukv", 0]
    for j in range(8):
        act.wait_ge(*sg.event("acc", g + j))
        act.activation(m["V"][:, j // 2, (j % 2) * 512:(j % 2 + 1) * 512], b[(g + j) % 4][:], ACT.Copy).then_inc(*sg.inc("act_free", g + j, also=[("free", g + j)]))

    for h in range(-2, HEADS):
        if 0 <= h + 1 < HEADS:
            for q in Q_ORDER:
                n, w = 4 * (h + 1) + q, (q + 1) * P
                act.wait_ge(*sg.event("max", n))
                if h >= 1:
                    act.wait_ge(*sg.event("t", (h - 1, 3)))
                act.activation(m["P2"][:, (h + 1) % 2, P_AT[q]:P_AT[q] + w], score_bank(b, q), ACT.Exp,
                                       bias=m["nm"][:, n % 8:n % 8 + 1], scale=SCALE,
                                       accum_out=m["sum"][:, n % 8:n % 8 + 1]).then_inc(*sg.inc("act_exp", n))
        if h + 2 < HEADS:
            a = h + 2
            act.wait_ge(*sg.event("qn_acc", a))
            if a >= 2:
                act.wait_ge(*sg.event("s", 4 * (a - 2) + 3))
            act.activation(m["qn"][:, a % 2, :], b[3][:], ACT.Copy).then_inc(*sg.inc("act_qk", ("qn", a)))
            act.wait_ge(*sg.event("kn_acc", a))
            act.activation(m["kn"][:, a % 2, :], b[3][:], ACT.Copy).then_inc(*sg.inc("act_qk", ("kn", a)))
        if h >= 0:
            for kb in (0, 1):
                w = (4 - kb) * P
                act.wait_ge(*sg.event("t", (h, kb)))
                if h:
                    act.wait_ge(*sg.event("o", h - 1))
                act.activation(m["PT"][:, T_AT[kb]:T_AT[kb] + w], b[5 + kb % 2][:, 0:w], ACT.Copy).then_inc(*sg.inc("act_pt", (h, kb), also=[("pt", (h, kb))]))
    act.wait_ge(*sg.event("o", HEADS - 1))
    for k in range(KD):
        act.wait_ge(*sg.event("y", k))
        act.activation(HH[:, k, :], m["ya"][:, k, :], ACT.Copy).then_inc(*sg.inc("act_hi", ("y", k)))
    for i in range(4):
        feed(W_INDEX["out", i] + 2)
    act.wait_ge(*sg.event("x"))
    norm(1, K_E6)
    for q in range(2 * NF):
        half, j = divmod(q, NF)
        feed(W_INDEX["fi", q] + 2)
        g = FIRST_GROUP["fi", q]
        act.wait_ge(*sg.event("acc", g))
        if q >= 2:
            act.wait_ge(*sg.event("ff_hid", q - 2))
        act.activation(m["fth"][:, q % 2, :], b[g % 4][:], ACT.Tanh, scale=0.5).then_inc(*sg.inc("act_out", ("ff_tanh", q)))
        act.wait_ge(*sg.event("ff_hid", q))
        act.activation(m["hidh"][:, j, :], m["fh"][:, q % 2, :], ACT.Copy).then_inc(*sg.inc("act_hi", ("ff", q)))
        if j == NF - 1:
            for jj in range(KD):
                feed(W_INDEX["fo", half * KD + jj] + 2)


def layer_dve(v, sg, m, b):
    f = lambda t: t.bitcast(F32)
    K, X, HH, HL, vec, mod = m["K"], m["X"], m["HH"], m["HL"], m["vec"], m["mod"]

    fed, nw = [0], [0]

    def ada():
        c, i = fed[0], CHUNKS[fed[0]][1]
        v.wait_ge(*sg.event("raw", c))
        if i >= 2:
            v.wait_ge(*sg.event("ada_col", i - 2))
        acc, raw = m["acc"][:, i % 2, :], m["RAW"][:, c % RAW_SLOTS, :]
        v.tensor_scalar(acc, raw[:, 0:256], m["c"][:, 0:1], None, ALU.mult).then_inc(*sg.inc("step_dve"))
        v.wait_ge(*sg.last("step_dve"))
        for k in range(1, KD):
            ins = v.scalar_tensor_tensor(acc, raw[:, k * 256:(k + 1) * 256], m["c"][:, k:k + 1], acc, ALU.mult, ALU.add)
            if k < KD - 1:
                ins.then_inc(*sg.inc("step_dve"))
                v.wait_ge(*sg.last("step_dve"))
        ins.then_inc(*sg.inc("raw_used", c, also=[("ada_acc", i)]))
        fed[0] += 1

    def ada_column(i):
        v.wait_ge(*sg.event("ada_col", i))
        src = b[6][:, 400:402] if i >= 8 else b[6][:, 2 * i:2 * i + 2]
        v.tensor_tensor(mod[:, 2 * i:2 * i + 2], src, vec[:, V_BADA + 2 * i:V_BADA + 2 * i + 2], ALU.add).then_inc(*sg.inc("ada_out", i))

    def feed(upto):
        while nw[0] <= min(upto, len(W_CHUNKS) - 1) and CHUNKS[fed[0]][2]:
            n, c = nw[0], fed[0]
            size = FLOATS.get(W_CHUNKS[n][0], SLOT)
            v.wait_ge(*sg.event("w_hi", n))
            v.tensor_tensor(m["WLO"][:, n % W_SLOTS, 0:size], m["RAW"][:, c % RAW_SLOTS, 0:size],
                                    f(m["WHI"])[:, n % W_SLOTS, 0:size], ALU.subtract).then_inc(*sg.inc("raw_used", c, also=[("w", n)]))
            nw[0] += 1
            fed[0] += 1

    def norm(t, scale, shift):
        v.wait_ge(*sg.event("act_root", t))
        v.reciprocal(m["rstd"][:], m["rstd"][:]).then_inc(*sg.inc("step_dve"))
        v.wait_ge(*sg.last("step_dve"))
        for k in range(KD):
            v.tensor_tensor(m["nt"][:, k % 2, :], X[:, k, :], m["rstd"][:], ALU.mult).then_inc(*sg.inc("step_dve"))
            v.wait_ge(*sg.last("step_dve"))
            if k >= 2:
                v.wait_ge(*sg.event("act_hi", ("h", t, k - 2)))
            v.tensor_scalar(m["nh"][:, k % 2, :], m["nt"][:, k % 2, :], scale(k), shift(k), ALU.mult, ALU.add).then_inc(*sg.inc("dve_h", ("h", t, k), also=[("h", (t, k))]))
            v.wait_ge(*sg.event("dve_h", ("h", t, k)))
            v.wait_ge(*sg.event("act_hi", ("h", t, k)))
            v.tensor_tensor(HL[:, k, :], m["nh"][:, k % 2, :], f(HH)[:, k, :], ALU.subtract).then_inc(*sg.inc("dve_lo", ("h", t, k), also=[("hl", (t, k))]))

    v.wait_ge(*sg.event("vec_in"))
    sm, hb = m["sm"], m["hb"]
    v.tensor_scalar(hb[:, 0:16], vec[:, V_BA:V_BA + 16], 0.5, None, ALU.mult).then_inc(*sg.inc("step_dve"))
    v.wait_ge(*sg.last("step_dve"))
    ap = vec[:, V_AP:V_AP + 8]
    v.tensor_scalar(sm[:, 16:24], ap, -1.0, None, ALU.mult).then_inc(*sg.inc("step_dve"))
    v.wait_ge(*sg.last("step_dve"))
    v.tensor_tensor(sm[:, 0:8], ap, sm[:, 16:24], ALU.max).then_inc(*sg.inc("dve_out", "absa", also=[("absa", None)]))
    v.wait_ge(*sg.event("act_out", "expa"))
    log1p(v, sg, "step_dve", sm[:, 24:32], sm[:, 8:16], sm[:, 32:40], sm[:, 40:48])
    v.tensor_scalar(sm[:, 16:24], sm[:, 16:24], 0.0, None, ALU.max).then_inc(*sg.inc("step_dve"))
    v.wait_ge(*sg.last("step_dve"))
    v.tensor_tensor(sm[:, 24:32], sm[:, 24:32], sm[:, 16:24], ALU.add).then_inc(*sg.inc("step_dve"))
    v.wait_ge(*sg.last("step_dve"))
    v.tensor_scalar(hb[:, 16:24], sm[:, 24:32], -LRU_C / 2, None, ALU.mult)
    v.tensor_scalar(hb[:, 24:32], sm[:, 24:32], LRU_C / 2, None, ALU.mult).then_inc(*sg.inc("dve_out", "hb", also=[("hb", None)]))
    for i in range(8):
        ada()
        if i:
            ada_column(i - 1)
    ada_column(7)
    v.wait_ge(*sg.event("ada_out", 7))
    v.tensor_scalar(mod[:, 8:16], mod[:, 8:16], 1.0, None, ALU.add).then_inc(*sg.inc("step_dve"))
    v.wait_ge(*sg.last("step_dve"))
    norm(0, lambda k: mod[:, 8 + k:9 + k], lambda k: mod[:, k:k + 1])
    feed(1)

    def lru_head(i):
        g = FIRST_GROUP["lru", i]
        for j in range(2):
            blk = 2 * i + j
            xc, pad = m["xc"][:, blk % 4, :], m["xpad"][:, j, :]
            cw = lambda t: vec[:, V_CW + 8 * t + blk:V_CW + 8 * t + blk + 1]
            v.wait_ge(*sg.event("act_free", g + j))
            if blk >= 4:
                v.wait_ge(*sg.event("gate_pre", i - 2))
            v.tensor_scalar(xc, pad[:, 0:S], cw(0), vec[:, V_CB + blk:V_CB + blk + 1], ALU.mult, ALU.add).then_inc(*sg.inc("step_dve"))
            v.wait_ge(*sg.last("step_dve"))
            v.scalar_tensor_tensor(xc, pad[:, 1:1 + S], cw(1), xc, ALU.mult, ALU.add).then_inc(*sg.inc("step_dve"))
            v.wait_ge(*sg.last("step_dve"))
            v.scalar_tensor_tensor(xc, pad[:, 2:2 + S], cw(2), xc, ALU.mult, ALU.add).then_inc(*sg.inc("step_dve"))
            v.wait_ge(*sg.last("step_dve"))
            v.scalar_tensor_tensor(xc, pad[:, 3:3 + S], cw(3), xc, ALU.mult, ALU.add).then_inc(*sg.inc("dve_out", ("xc", blk), also=[("xc", blk)]))

    def lru_tail(i):
        tr, ti, la, sq2, rs = m["tr"], m["ti"], m["la"], m["sq2"], m["rs"]
        v.wait_ge(*sg.event("act_out", ("lru_square", i)))
        for n in range(2):
            v.scalar_tensor_tensor(tr[:, n, :], sq2[:, n, :], 1.0, tr[:, n, :], ALU.add, ALU.mult).then_inc(*sg.inc("step_dve"))
            v.wait_ge(*sg.last("step_dve"))
            ins = v.tensor_tensor(tr[:, n, :], tr[:, n, :], rs[:], ALU.max)
        ins.then_inc(*sg.inc("dve_out", ("lru_var", i), also=[("lru_var", i)]))
        v.wait_ge(*sg.event("dve_out", ("xc", 2 * i + 1)))
        for n in range(2):
            v.scalar_tensor_tensor(ti[:, n, :], ti[:, n, :], 1.0, m["xc"][:, (2 * i + n) % 4, :], ALU.add, ALU.mult)
            ins = v.scalar_tensor_tensor(la[:, n, :], rs[:], 0.0, la[:, n, :], ALU.is_equal, ALU.mult)
        ins.then_inc(*sg.inc("step_dve"))
        v.wait_ge(*sg.last("step_dve"))
        v.wait_ge(*sg.event("act_out", ("lru_root", i)))
        for n in range(2):
            v.scalar_tensor_tensor(ti[:, n, :], ti[:, n, :], 0.5, tr[:, n, :], ALU.mult, ALU.mult).then_inc(*sg.inc("step_dve"))
            v.wait_ge(*sg.last("step_dve"))
            ins = v.tensor_tensor_scan(m["ya"][:, 2 * i + n, :], la[:, n, :], ti[:, n, :], 0.0, ALU.mult, ALU.add)
        ins.then_inc(*sg.inc("dve_out", ("lru_done", i), also=[("lru_done", i)]))

    for n, (kind, i, _) in enumerate(W_CHUNKS):
        if kind == "uq":
            break
        feed(n + 2)
        g = FIRST_GROUP[kind, i]
        if kind == "lru":
            lru_head(i)
            if i:
                lru_tail(i - 1)
        elif kind == "q":
            lru_tail(3)
            v.wait_ge(*sg.event("lru_done", 3))
        elif kind == "kv":
            v.wait_ge(*sg.event("acc", g + 1))
            v.tensor_tensor(m["Ak"][:], b[(g + 1) % 4][:], m["T"][:], ALU.mult).then_inc(*sg.inc("dve_free", g + 1, also=[("free", g + 1), ("ak", None)]))
        elif kind == "ga":
            for j in range(2):
                blk = 2 * i + j
                v.wait_ge(*sg.event("act_free", g + j))
                v.scalar_tensor_tensor(m["ya"][:, blk, :], m["tg"][:, j, :], 1.0, m["ya"][:, blk, :], ALU.add, ALU.mult).then_inc(*sg.inc("dve_out", ("ga", blk), also=[("ga_used", blk)]))
            if i == 1:
                v.wait_ge(*sg.event("act_root", "qkv"))
                v.reciprocal(m["rq"][:], m["rq"][:]).then_inc(*sg.inc("step_dve"))
                v.wait_ge(*sg.last("step_dve"))
                for j in range(2):
                    v.scalar_tensor_tensor(m["qraw"][:, j, :], m["qraw"][:, j, :], vec[:, V_QG + j:V_QG + j + 1],
                                           m["rq"][:, 0, :], ALU.mult, ALU.mult)
                v.scalar_tensor_tensor(m["kvraw"][:], m["kvraw"][:], vec[:, V_KVG:V_KVG + 1], m["rq"][:, 1, :],
                                               ALU.mult, ALU.mult).then_inc(*sg.inc("dve_out", "cq", also=[("cq", None)]))
                v.wait_ge(*sg.event("cq"))
                v.wait_ge(*sg.event("act_hi", "cq"))
                v.tensor_tensor(m["cql"][:], m["qraw"][:], f(m["cqh"])[:], ALU.subtract)
                v.tensor_tensor(m["ckvl"][:], m["kvraw"][:], f(m["ckvh"])[:], ALU.subtract).then_inc(*sg.inc("dve_lo", "cq", also=[("cql", None)]))
            if i == 3:
                v.wait_ge(*sg.event("kp_acc"))
                v.tensor_copy(m["Kp"][:], b[6][:]).then_inc(*sg.inc("dve_out", "kp", also=[("kp", None)]))

    feed(W_INDEX["ukv", 0])
    v.wait_ge(*sg.event("ga_used", 2 * 3 + 1))
    for h in range(-2, HEADS):
        if 0 <= h + 1 < HEADS:
            for q in Q_ORDER:
                n = 4 * (h + 1) + q
                one = lambda t: m[t][:, n % 8:n % 8 + 1]
                v.wait_ge(*sg.event("s", n))
                if n >= 8:
                    v.wait_ge(*sg.event("act_exp", n - 8))
                v.tensor_reduce(one("mx"), score_bank(b, q), AX.X, ALU.max).then_inc(*sg.inc("step_dve"))
                v.wait_ge(*sg.last("step_dve"))
                v.tensor_scalar(one("nm"), one("mx"), -SCALE, None, ALU.mult).then_inc(*sg.inc("dve_max", n, also=[("max", n)] + [("max", n - 2)] * (q == 2)))
        if h + 2 < HEADS:
            a = h + 2
            v.wait_ge(*sg.event("qr_acc", a))
            if a >= 2:
                v.wait_ge(*sg.event("s", 4 * (a - 2) + 3))
            v.tensor_tensor(m["qa"][:, a % 2, :], b[4][:], m["T"][:], ALU.mult).then_inc(*sg.inc("dve_qa", a, also=[("qa", a)]))
        if 0 <= h + 1 < HEADS:
            for q in Q_ORDER:
                n, w = 4 * (h + 1) + q, (q + 1) * P
                one = lambda t: m[t][:, n % 8:n % 8 + 1]
                v.wait_ge(*sg.event("act_exp", n))
                v.reciprocal(one("rec"), one("sum")).then_inc(*sg.inc("step_dve"))
                v.wait_ge(*sg.last("step_dve"))
                pp = m["P2"][:, (h + 1) % 2, P_AT[q]:P_AT[q] + w]
                v.tensor_scalar(pp, pp, one("rec"), None, ALU.mult).then_inc(*sg.inc("dve_p", n, also=[("p", n)]))
        if h >= 0:
            for kb in (2, 3):
                w = (4 - kb) * P
                v.wait_ge(*sg.event("t", (h, kb)))
                if h:
                    v.wait_ge(*sg.event("o", h - 1))
                v.tensor_copy(m["PT"][:, T_AT[kb]:T_AT[kb] + w], b[5 + kb % 2][:, 0:w]).then_inc(*sg.inc("dve_pt", (h, kb), also=[("pt", (h, kb))]))
            v.wait_ge(*sg.event("o", h))
            v.scalar_tensor_tensor(m["to"][:], m["tgb"][:, h, :], 1.0, b[7][:], ALU.add, ALU.mult).then_inc(*sg.inc("step_dve"))
            v.wait_ge(*sg.last("step_dve"))
            v.tensor_tensor(m["ya"][:, h, :], m["ya"][:, h, :], m["to"][:], ALU.add).then_inc(*sg.inc("dve_y", h, also=[("y", h)]))
            for i in (8 + 2 * h, 9 + 2 * h):
                ada()
                ada_column(i)
    for k in range(KD):
        v.wait_ge(*sg.event("dve_y", k))
        v.wait_ge(*sg.event("act_hi", ("y", k)))
        v.tensor_tensor(HL[:, k, :], m["ya"][:, k, :], f(HH)[:, k, :], ALU.subtract).then_inc(*sg.inc("dve_lo", ("y", k), also=[("yl", k)]))
    v.wait_ge(*sg.event("ada_out", 23))
    v.tensor_scalar(mod[:, 16:24], mod[:, 16:24], 0.5, None, ALU.mult).then_inc(*sg.inc("step_dve"))
    v.wait_ge(*sg.last("step_dve"))
    v.tensor_scalar(mod[:, 32:40], mod[:, 32:40], 1.0, None, ALU.add).then_inc(*sg.inc("step_dve"))
    v.wait_ge(*sg.last("step_dve"))

    def residual(kind, i, count, gain, also=()):
        g = FIRST_GROUP[kind, i]
        for j in range(count):
            k = (i * count + j) % KD
            v.wait_ge(*sg.event("acc", g + j))
            v.scalar_tensor_tensor(X[:, k, :], b[(g + j) % 4][:], mod[:, gain + k:gain + k + 1], X[:, k, :],
                                           ALU.mult, ALU.add).then_inc(*sg.inc("dve_free", g + j, also=[("free", g + j), *also]))

    for i in range(4):
        feed(W_INDEX["out", i] + 2)
        residual("out", i, 2, 16, [("x", None)])
    norm(1, lambda k: mod[:, 32 + k:33 + k], lambda k: mod[:, 24 + k:25 + k])
    for q in range(2 * NF):
        half, j = divmod(q, NF)
        feed(W_INDEX["fi", q] + 2)
        g, fh = FIRST_GROUP["fi", q], m["fh"][:, q % 2, :]
        v.wait_ge(*sg.event("act_out", ("ff_tanh", q)))
        v.wait_ge(*sg.event("acc", g + 1))
        if q >= 2:
            v.wait_ge(*sg.event("act_hi", ("ff", q - 2)))
            v.wait_ge(*sg.event("ffl", q - 2))
        v.scalar_tensor_tensor(fh, m["fth"][:, q % 2, :], 1.0, b[g % 4][:], ALU.add, ALU.mult).then_inc(*sg.inc("dve_free", g, also=[("free", g)]))
        v.wait_ge(*sg.event("dve_free", g))
        v.scalar_tensor_tensor(fh, fh, 0.5, b[(g + 1) % 4][:], ALU.mult, ALU.mult).then_inc(*sg.inc("dve_free", g + 1, also=[("free", g + 1), ("ff_hid", q)]))
        v.wait_ge(*sg.event("dve_free", g + 1))
        v.wait_ge(*sg.event("act_hi", ("ff", q)))
        v.tensor_tensor(m["hidl"][:, j, :], fh, f(m["hidh"])[:, j, :], ALU.subtract).then_inc(*sg.inc("dve_lo", ("ff", q), also=[("ffl", q)]))
        if j == NF - 1:
            for jj in range(KD):
                feed(W_INDEX["fo", half * KD + jj] + 2)
                if half:
                    v.wait_ge(*sg.event("dve_free", FIRST_GROUP["fo", jj]))
                residual("fo", half * KD + jj, 1, 40)


def layer_pe(pe, sg, m, b):
    K, HH, HL = m["K"], m["HH"], m["HL"]
    one = K[:, K_ONE:K_ONE + P]

    def bank(g):
        if g >= 4:
            pe.wait_ge(*sg.event("free", g - 4))
        return b[g % 4]

    def weights(n):
        pe.wait_ge(*sg.event("w", n))
        return m["WHI"][:, n % W_SLOTS, :], m["WLO"][:, n % W_SLOTS, :]

    def stat(t):
        for k in range(KD):
            pe.wait_ge(*sg.event("act_sq", (t, k)))
            ins = pe.matmul(b[4][:], one, m["sq"][:, k % 2, :], start=(k == 0), stop=(k == KD - 1))
            ins.then_inc(*sg.inc("pe_step", also=[("sq_used", (t, k)), *([("stat", t)] if k == KD - 1 else [])]))

    def ada_columns(i):
        pe.wait_ge(*sg.event("ada_acc", i))
        if i:
            pe.wait_ge(*sg.event("ada_out", i - 1))
        for j in range(2):
            c = 400 + j if i >= 8 else 2 * i + j
            ins = pe.matmul(b[6][:, c:c + 1], m["acc"][:, i % 2, j * P:(j + 1) * P], one[:, 0:1], start=True, stop=True)
        ins.then_inc(*sg.inc("pe_step", also=[("ada_col", i)]))

    def dense(kind, i):
        n, g = W_INDEX[kind, i], FIRST_GROUP[kind, i]
        hi, lo = weights(n)
        for j in range(2):
            out = bank(g + j)
            for k in range(KD):
                c = k * 256 + j * P
                ins = split3(pe, out[:], hi[:, c:c + P], lo[:, c:c + P], HH[:, k, :], HL[:, k, :], k == 0, k == KD - 1)
            ins.then_inc(*sg.inc("pe_step", also=[("acc", g + j), *([("w_used", n)] if j else [])]))

    def gates(i):
        pe.wait_ge(*sg.event("lruw_in", 1))
        if i:
            pe.wait_ge(*sg.event("act_out", ("lru_tanh", i - 1)))
        for n in range(2):
            blk = 2 * i + n
            pe.wait_ge(*sg.event("xc", blk))
            for g in range(2):
                ins = pe.matmul(b[4 + 2 * n + g][:], m["lruw"][:, 8 * g + blk, :], m["xc"][:, blk % 4, :], start=True, stop=True)
        ins.then_inc(*sg.inc("pe_step", also=[("gate_pre", i)]))

    for i in range(8):
        ada_columns(i)
    stat(0)
    pe.wait_ge(*sg.event("hl", (0, KD - 1)))
    for i in range(4):
        dense("lru", i)
        if i:
            gates(i - 1)
    dense("q", 0)
    gates(3)
    dense("kv", 0)
    dense("ga", 0)
    pe.wait_ge(*sg.event("act_sq", "qkv"))
    pe.matmul(b[4][:], one, m["sq2"][:, 0, :], start=True, stop=False)
    pe.matmul(b[4][:], one, m["sq2"][:, 1, :], start=False, stop=True)
    pe.matmul(b[5][:], one, m["ti"][:, 0, :], start=True, stop=True).then_inc(*sg.inc("pe_step", also=[("stat", "qkv")]))
    dense("ga", 1)
    pe.wait_ge(*sg.event("ak"))
    pe.matmul(b[6][:], K[:, K_J2:K_J2 + P], m["Ak"][:], start=True, stop=True).then_inc(*sg.inc("pe_step", also=[("kp_acc", None)]))
    for kind, i in (("ga", 2), ("ga", 3), ("gb", 0), ("gb", 1), ("gb", 2), ("gb", 3)):
        dense(kind, i)

    pe.wait_ge(*sg.event("cql"))
    n, g = W_INDEX["ukv", 0], FIRST_GROUP["ukv", 0]
    ukv_hi, ukv_lo = weights(n)
    for j in range(8):
        out = bank(g + j)
        tok, c = slice((j // 2) * P, (j // 2 + 1) * P), 1024 + (j % 2) * 512
        ins = split3(pe, out[:], m["ckvh"][:, tok], m["ckvl"][:, tok], ukv_hi[:, c:c + 512], ukv_lo[:, c:c + 512], True, True)
        ins.then_inc(*sg.inc("pe_step", also=[("acc", g + j)]))
    for j in range(4, 8):
        pe.wait_ge(*sg.event("free", g + j))

    pe.wait_ge(*sg.event("kp"))
    for h in range(-2, HEADS):
        if 0 <= h + 1 < HEADS:
            a = h + 1
            pe.wait_ge(*sg.event("act_qk", ("kn", a)))
            pe.wait_ge(*sg.event("qa", a))
            for q in Q_ORDER:
                s, w = score_bank(b, q), (q + 1) * P
                if a:
                    pe.wait_ge(*sg.event("act_exp", 4 * (a - 1) + (2 if q == 0 else q)))
                tok = slice(q * P, (q + 1) * P)
                pe.matmul(s, m["qn"][:, a % 2, tok], m["kn"][:, a % 2, 0:w], start=True, stop=False)
                pe.matmul(s, m["qa"][:, a % 2, tok], m["Kp"][:, 0:w], start=False, stop=False)
                ins = pe.matmul(s[:, q * P:w], m["idb"][:], m["maskb"][:], start=False, stop=True)
                ins.then_inc(*sg.inc("pe_step", also=[("s", 4 * a + q), *([("s", 4 * a)] if q == 2 else [])]))
        if h + 2 < HEADS:
            a = h + 2
            hi, lo = weights(W_INDEX["uq", a // 4])
            if a:
                pe.wait_ge(*sg.event("act_qk", ("kn", a - 1)))
            for k in range(2):
                c = k * 1024 + (a % 4) * 256
                ins = split3(pe, b[3][:], hi[:, c:c + P], lo[:, c:c + P], m["cqh"][:, k, :], m["cql"][:, k, :], k == 0, k == 1)
            ins.then_inc(*sg.inc("pe_step", also=[("qn_acc", a)]))
            if a:
                pe.wait_ge(*sg.event("qa", a - 1))
            for k in range(2):
                c = k * 1024 + (a % 4) * 256 + P
                ins = split3(pe, b[4][:], hi[:, c:c + P], lo[:, c:c + P], m["cqh"][:, k, :], m["cql"][:, k, :], k == 0, k == 1)
            ins.then_inc(*sg.inc("pe_step", also=[("qr_acc", a)]))
            pe.wait_ge(*sg.event("act_qk", ("qn", a)))
            c = a * P
            ins = split3(pe, b[3][:], ukv_hi[:, c:c + P], ukv_lo[:, c:c + P], m["ckvh"][:], m["ckvl"][:], True, True)
            ins.then_inc(*sg.inc("pe_step", also=[("kn_acc", a), *([("w_used", W_INDEX["uq", 0])] if a == 3 else []), *([("w_used", W_INDEX["uq", 1]), ("w_used", W_INDEX["ukv", 0])] if a == 7 else [])]))
        if h >= 0:
            for kb in range(4):
                if kb < 2:
                    if h:
                        pe.wait_ge(*sg.event("pt", (h - 1, kb + 2)))
                        if kb == 0:
                            pe.wait_ge(*sg.event("ada_out", 9 + 2 * (h - 1)))
                else:
                    pe.wait_ge(*sg.event("pt", (h, kb - 2)))
                for q in range(kb, 4):
                    pe.wait_ge(*sg.event("p", 4 * h + q))
                    c = P_AT[q] + kb * P
                    ins = pe.transpose(b[5 + kb % 2][:, (q - kb) * P:(q - kb + 1) * P], m["P2"][:, h % 2, c:c + P], K[:, K_ID:K_ID + P])
                ins.then_inc(*sg.inc("pe_step", also=[("t", (h, kb))]))
            if h:
                pe.wait_ge(*sg.event("y", h - 1))
            for kb in range(4):
                w = (4 - kb) * P
                pe.wait_ge(*sg.event("pt", (h, kb)))
                ins = pe.matmul(b[7][:, kb * P:S], m["V"][:, kb, h * P:(h + 1) * P], m["PT"][:, T_AT[kb]:T_AT[kb] + w],
                                start=(kb == 0), stop=(kb == 3))
            ins.then_inc(*sg.inc("pe_step", also=[("o", h)]))
            ada_columns(8 + 2 * h)
            ada_columns(9 + 2 * h)
    pe.wait_ge(*sg.event("yl", KD - 1))
    for i in range(4):
        dense("out", i)
    stat(1)
    pe.wait_ge(*sg.event("hl", (1, KD - 1)))
    for half in range(2):
        for j in range(NF):
            dense("fi", half * NF + j)
        for j in range(KD):
            i = half * KD + j
            n, g = W_INDEX["fo", i], FIRST_GROUP["fo", i]
            hi, lo = weights(n)
            out = bank(g)
            pe.wait_ge(*sg.event("ffl", half * NF + NF - 1))
            for k in range(NF):
                c = k * P
                ins = split3(pe, out[:], hi[:, c:c + P], lo[:, c:c + P], m["hidh"][:, k, :], m["hidl"][:, k, :], k == 0, k == NF - 1)
            ins.then_inc(*sg.inc("pe_step", also=[("acc", g), ("w_used", n)]))

START_SIGNALS = """st_x st_k st_c st_pos st_dve st_xt st_ev st_sin"""


def start_program(engine, who, sg, m, b, W):
    K = m["K"]
    if who == "sp":
        engine.dma_start(K[:], W["consts"][:, 0:K_KEPT]).then_inc(*sg.inc("st_k", n=16))
        engine.dma_start(m["mask0"][:], W["consts"][:, K_MASK:K_MASK + P]).then_inc(*sg.inc("st_k", n=16))
        engine.dma_start(m["x0"][:], W["x"][0].rearrange("(t p) d -> p t d", p=P)).then_inc(*sg.inc("st_x", n=16))
        engine.dma_start(m["c"][:], W["c_cols"]).then_inc(*sg.inc("st_c", n=16))
        engine.dma_start(m["posi"][:], W["positions"].broadcast_to([P, S])).then_inc(*sg.inc("st_pos", n=16))
    if who == "dve":
        v = engine

        pf, a, k, T = m["posf"][:], m["ang"][:], m["rot"][:], m["T"][:]
        v.memset(m["xpad"][:, :, 0:3], 0.0)
        engine.wait_ge(*sg.event("st_k"))
        v.tensor_copy(m["idb"][:], K[:, K_ID:K_ID + P])
        v.tensor_copy(m["maskb"][:], m["mask0"][:])
        engine.wait_ge(*sg.event("st_pos"))
        v.tensor_copy(pf, m["posi"][:]).then_inc(*sg.inc("st_dve"))
        engine.wait_ge(*sg.last("st_dve"))
        v.tensor_scalar(m["rs"][:], pf, 0.0, None, ALU.is_equal)
        v.tensor_scalar(a, pf, K[:, K_INVF:K_INVF + 1], None, ALU.mult).then_inc(*sg.inc("st_dve"))
        engine.wait_ge(*sg.last("st_dve"))
        v.tensor_scalar(k, a, 1.0 / (2 * np.pi), None, ALU.mult).then_inc(*sg.inc("st_dve"))
        engine.wait_ge(*sg.last("st_dve"))
        v.tensor_scalar(k, k, 12582912.0, -12582912.0, ALU.add, ALU.add).then_inc(*sg.inc("st_dve"))
        engine.wait_ge(*sg.last("st_dve"))
        for part in TWO_PI:
            v.scalar_tensor_tensor(a, k, -part, a, ALU.mult, ALU.add).then_inc(*sg.inc("st_dve"))
            engine.wait_ge(*sg.last("st_dve"))
        v.tensor_scalar(a, a, K[:, K_SG:K_SG + 1], K[:, K_PH:K_PH + 1], ALU.mult, ALU.add).then_inc(*sg.inc("st_dve"))
        engine.wait_ge(*sg.last("st_dve"))
        v.tensor_scalar(k, a, float(np.pi), -2 * float(np.pi), ALU.is_gt, ALU.mult).then_inc(*sg.inc("st_dve"))
        engine.wait_ge(*sg.last("st_dve"))
        v.tensor_tensor(a, a, k, ALU.add).then_inc(*sg.inc("st_dve"))
        engine.wait_ge(*sg.last("st_dve"))
        v.tensor_scalar(a, a, 3.1415925, -3.1415925, ALU.min, ALU.max).then_inc(*sg.inc("st_dve", "ang"))
        for t in range(0, 8):
            engine.wait_ge(*sg.event("st_xt", t))
            dst = m["X"][:, t, :]
            if t % 2:
                v.tensor_copy(dst, b[t][:]).then_inc(*sg.inc("st_ev", t))
    if who == "act":
        engine.wait_ge(*sg.event("st_dve", "ang"))
        engine.activation(m["T"][:], m["ang"][:], ACT.Sin).then_inc(*sg.inc("st_sin"))
        for t in range(0, 8, 2):
            engine.wait_ge(*sg.event("st_xt", t))
            engine.activation(m["X"][:, t, :], b[t][:], ACT.Copy)
    if who == "pe":
        engine.wait_ge(*sg.event("st_k"))
        engine.wait_ge(*sg.event("st_x"))
        for k in range(KD):
            for t in range(NT):
                ins = engine.transpose(b[k][:, t * P:(t + 1) * P], m["x0"][:, t, k * P:(k + 1) * P], K[:, K_ID:K_ID + P])
            ins.then_inc(*sg.inc("st_xt", k))


TWO_PI = (6.28125, 0.0019350051879882812, 3.019915981956753e-07)


def tensors(nc, ctx):
    m = {}

    def at(name, kib, shape, dtype=F32):
        m[name] = nc.alloc_sbuf_tensor_at(name, [shape[0], *shape[1:]], dtype, offset=BASE + int(kib * KB))

    at("X", 0, [P, KD, S])
    at("RAW", 16, [P, RAW_SLOTS, SLOT])
    at("WHI", 48, [P, W_SLOTS, SLOT], F32R)
    at("WLO", 72, [P, W_SLOTS, SLOT], F32R)
    at("HH", 96, [P, KD, S], F32R)
    at("HL", 112, [P, KD, S], F32R)
    at("V", 96, [P, NT, D])
    at("P2", 112, [P, 2, 1280])
    at("PT", 122, [P, 1280])
    at("x0", 128, [P, NT, D])
    at("ya", 128, [P, KD, S])
    at("lruw", 144, [P, 2 * KD, P])
    at("tgb", 144, [P, KD, S])
    at("xc", 160, [P, 4, S])
    at("tr", 168, [P, 2, S])
    at("ti", 172, [P, 2, S])
    at("la", 176, [P, 2, S])
    at("sq2", 180, [P, 2, S])
    at("qraw", 184, [P, 2, S])
    at("kvraw", 188, [P, S])
    at("rq", 190, [P, 2, S])
    at("tg", 176, [P, 2, S])
    at("cqh", 160, [P, 2, S], F32R)
    at("cql", 164, [P, 2, S], F32R)
    at("ckvh", 168, [P, S], F32R)
    at("ckvl", 170, [P, S], F32R)
    at("Ak", 174, [P, S])
    at("Kp", 180, [P, S])
    at("qn", 184, [P, 2, S])
    at("qa", 188, [P, 2, S])
    at("kn", 172, [P, 2, S])
    at("to", 192, [P, S])
    at("hidh", 128, [P, NF, S], F32R)
    at("hidl", 150, [P, NF, S], F32R)
    at("fth", 172, [P, 2, S])
    at("fh", 176, [P, 2, S])
    at("nt", 180, [P, 2, S])
    at("nh", 184, [P, 2, S])
    at("rstd", 188, [P, S])
    at("sq", 190, [P, 2, S])
    at("posi", 160, [P, S], I32)
    at("posf", 162, [P, S])
    at("ang", 164, [P, S])
    at("rot", 166, [P, S])
    at("mask0", 168, [P, P])
    at("xpad", 194, [P, 2, 516])
    at("T", 198.125, [P, S])
    at("rs", 200.125, [P, S])
    at("K", 202.125, [P, K_KEPT])
    up = lambda size: (size + 31) // 32 * 32
    o = up(int(202.125 * KB) + K_KEPT * 4)
    mix_tensors(at, o)
    moe_tensors(at)
    for name, n, dt in (("vec", NVEC, F32), ("mod", 48, F32), ("acc", 512, F32), ("idb", P, BF16), ("maskb", P, BF16),
                        ("c", 8, F32), ("sm", 48, F32), ("hb", 32, F32), ("mx", 8, F32), ("nm", 8, F32),
                        ("sum", 8, F32), ("rec", 8, F32), ("zero", P, F32)):
        shape = [P, 2, 256] if name == "acc" else [P, n]
        at(name, o / KB, shape, dt)
        o += up(n * (2 if dt == BF16 else 4))
    assert BASE + o <= 229368, o
    return m


BASE = 16512


def program(nc, W, at, phases=("layers", "mix", "moe")):
    with ExitStack() as ctx:
        m = tensors(nc, ctx)
        b = [ctx.enter_context(nc.psum_tensor(f"bank{i}", [P, 512], F32)) for i in range(8)]
        start = Signals(nc, ctx, START_SIGNALS, at.setdefault("start", {}))
        layer = Signals(nc, ctx, LAYER_SIGNALS, at.setdefault("layer", {}))
        mix = Signals(nc, ctx, MIX_SIGNALS, at.setdefault("mix", {}))
        route = Signals(nc, ctx, ROUTE_SIGNALS, at.setdefault("route", {}))
        moe = LoopSignals(nc, ctx, MOE_SIGNALS, at.setdefault("moe", {}))
        final = Signals(nc, ctx, FINAL_SIGNALS, at.setdefault("final", {}))
        W = dict(W, h2tok=nc.dram_tensor("h2_by_token", (S, D), F32).ap(),
                 ybuf=nc.dram_tensor("expert_results", (MAXB * P, D), F32).ap())
        arrived, go = [ctx.enter_context(nc.semaphore(n)) for n in ("arrived", "go")]
        zeroed = ctx.enter_context(nc.semaphore("zeroed"))
        layers, mixes, experts = ["layers" in phases, "mix" in phases, "moe" in phases]
        done = ctx.enter_context(nc.semaphore("written"))
        after_mix = (DEPTH if layers else 0) + 2
        block = ctx.enter_context(nc.Block())

        def phase_end(eng, n):
            eng.drain().then_inc(arrived, 1)
            eng.wait_ge(go, n)

        def gather(sp):
            sp.wait_ge(arrived, 4)
            sp.sem_clear(arrived)
            sp.nop().then_inc(go, 1)

        def blocks(eng, who):
            eng.wait_ge(*route.event("bei"))
            return eng.value_load(m["bei"][0:1, NB:NB + 1], min_val=1, max_val=MAXB)

        def zero_results(pool, first, count):
            with pool.Fori(0, count) as i:
                rows = W["ybuf"][bass.ds((first + i) * P, P), :].rearrange("p (n d) -> p n d", d=P)
                zero = m["zero"][:].rearrange("p (o d) -> p o d", o=1).broadcast_to([P, KD, P])
                pool.dma_start(rows, zero).then_inc(zeroed, 16)

        def phases_of(eng, who, layer_part, moe_part):
            if who != "pool":
                start_program(eng, who, start, m, b, W)
            else:
                eng.memset(m["zero"][:], 0.0)
            phase_end(eng, 1)
            if layers:
                with eng.Fori(0, DEPTH) as l:
                    layer_part(eng)
                    phase_end(eng, l + 2)
            if who == "pool":
                zero_results(eng, MIN_BLOCKS, MAXB - MIN_BLOCKS)
                eng.wait_ge(zeroed, (MAXB - MIN_BLOCKS) * 16)
            elif mixes:
                mix_program(eng, who, mix, m, b, W)
            phase_end(eng, after_mix)
            if experts:
                route_program(eng, who, route, m, b, W, moe)
                moe_part(eng, blocks(eng, who))
                phase_end(eng, after_mix + 1)
                final_program(eng, who, final, m, W, moe)

        @block.sync
        def _(sp):
            start_program(sp, "sp", start, m, b, W)
            gather(sp)
            if layers:
                with sp.Fori(0, DEPTH) as l:
                    layer_loads(sp, l, layer, m, W)
                    sp.wait_ge(arrived, 4)
                    for s in layer.sem.values():
                        sp.sem_clear(s)
                    sp.sem_clear(arrived)
                    sp.nop().then_inc(go, 1)
            if mixes:
                mix_program(sp, "sp", mix, m, b, W)
            gather(sp)
            if experts:
                route_program(sp, "sp", route, m, b, W, moe)
                moe_sp(sp, moe, m, W, blocks(sp, "sp"))
                gather(sp)
                final_program(sp, "sp", final, m, W, moe)
            else:
                sp.dma_start(W["out"].rearrange("(k p) s -> p k s", p=P), m["X"][:]).then_inc(done, 16)
                sp.wait_ge(done, 16)

        @block.scalar
        def _(act):
            phases_of(act, "act", lambda e: layer_act(e, layer, m, b), lambda e, n: moe_act(e, moe, m, b, W, n))

        @block.vector
        def _(v):
            phases_of(v, "dve", lambda e: layer_dve(e, layer, m, b), lambda e, n: moe_dve(e, moe, m, b, n))

        @block.tensor
        def _(pe):
            phases_of(pe, "pe", lambda e: layer_pe(e, layer, m, b), lambda e, n: moe_pe(e, moe, m, b, n))

        @block.gpsimd
        def _(pool):
            phases_of(pool, "pool", lambda e: None, lambda e, n: moe_pool(e, moe, m, W, n))

        moe.close()


def constants():
    K = np.zeros((P, NK), np.float32)
    i = np.arange(P)
    K[:, K_ID:K_ID + P] = np.eye(P)
    K[:, K_J2:K_J2 + P] = (i[:, None] % ROPE) == (i[None, :] % ROPE)
    K[:, K_ONE:K_ONE + P] = 1.0
    K[:, K_MASK:K_MASK + P] = np.where(i[None, :] > i[:, None], -1e30, 0.0)
    half = ROPE // 2
    K[:, K_INVF] = (np.float64(10000.0) ** (-(np.arange(half) * 2) / ROPE)).astype(np.float32)[i % half]
    K[:, K_SG] = np.where((i >= 64) & (i < 96), -1.0, 1.0)
    K[:, K_PH] = np.where(i < 64, np.pi / 2, 0.0)
    K[:, K_TRI:K_TRI + P] = i[None, :] >= i[:, None]
    K[:, K_LT:K_LT + P] = i[:, None] < i[None, :]
    K[:, K_INV:K_INV + 16] = 1.0 / (np.arange(16) + 1)
    K[:, K_I32:K_I32 + 32] = np.arange(32)
    K[:, K_I48:K_I48 + 50] = np.arange(50)
    K[:, K_I128:K_I128 + P] = np.arange(P)
    K[:, K_E6], K[:, K_E5] = 1e-6, 1e-5
    return K


def columns(v):
    return np.ascontiguousarray(np.asarray(v).reshape(-1, P).T)


def layer_vectors(i, l):
    parts = [i["b_ada"][l], i["conv_w"][l], i["conv_b"][l], i["lru_ba"][l], i["lru_bx"][l], i["lru_a_param"][l],
             i["q_norm_g"][l], i["kv_norm_g"][l]]
    return np.concatenate([columns(p) for p in parts], axis=1)


def block_vectors(i):
    v = np.zeros((P, NV2), np.float32)
    for at, name in ((V2_FIN, "final_norm_g"), (V2_N1, "norm1_g_2"), (V2_CW, "conv_w_2"), (V2_HN, "head_norm_g_2"),
                     (V2_PS, "pool_scale_2"), (V2_N2, "norm2_g_2")):
        c = columns(i[name])
        v[:, at:at + c.shape[1]] = c
    v[0:MH, V2_IG] = np.asarray(i["ig_b_2"])[0]
    v[0:MH, V2_FG] = np.asarray(i["fg_b_2"])[0]
    p = np.arange(P)
    v[:, V2_TOK:V2_TOK + 4] = p[:, None] + P * np.arange(4)[None, :]
    v[:, V2_PM] = p % EXPERTS
    return v


def head_selectors():
    return np.repeat(np.eye(MH, dtype=np.float32), P, axis=1)

MH, MD = 4, 128
EXPERTS, TOP = 32, 4
EPS_COL = K_E5
MAXB = S * TOP // P + EXPERTS
MIN_BLOCKS = S * TOP // P
V2_FIN, V2_N1, V2_CW, V2_HN, V2_PS, V2_N2, V2_IG, V2_FG, V2_TOK, V2_PM = 0, 8, 16, 48, 52, 56, 64, 65, 66, 70
NV2 = 71
MIX_CHUNKS = ([("gate", 0)] + [("qk", i) for i in range(4)] + [("v", i) for i in range(2)]
              + [("o", i) for i in range(2)] + [("u", i) for i in range(2)] + [("out", i) for i in range(4)])
MIX_GROUPS = {"gate": 2, "qk": 2, "v": 4, "o": 2, "u": 2, "out": 2}
MIX_COLUMN = {"gate": 2048, "qk": 0, "v": 1024, "o": 1536, "u": 2056}
MIX_AT = {c: n for n, c in enumerate(MIX_CHUNKS)}


def mix_groups():
    first, g = {}, 0
    for c in MIX_CHUNKS:
        first[c] = g
        g += MIX_GROUPS[c[0]]
    return first


MIX_FIRST = mix_groups()
MIX_SIGNALS = """mix_act mix_dve mix_pe mix_raw0 mix_raw1 mix_raw2 mix_raw3 mix_used mix_hi mix_small mix_free_act
    mix_free_dve mix_out_act mix_out_dve"""


def mix_program(engine, who, sg, m, b, W):
    f = lambda t: t.bitcast(F32)
    K, X, HH, HL, vec = m["K"], m["X"], m["HH"], m["HL"], m["vec2"]
    one = K[:, K_ONE:K_ONE + P]
    CC = len(MIX_CHUNKS)

    if who == "sp":
        sp = engine
        for dst, src in ((vec[:], W["vecs2"]), (m["tri"][:], W["consts"][:, K_TRI:K_TRI + P]),
                         (m["inv"][:], W["consts"][:, K_INV:K_INV + 16]),
                         (m["sel4"][:], W["sel4"])):
            sp.dma_start(dst, src).then_inc(*sg.inc("mix_small", also=[("small", None)], n=16))
        w_in, w_out = [W[n][0].rearrange("(k p) n -> p k n", p=P) for n in ("w_in_2", "w_out_2")]
        for n, (kind, i) in enumerate(MIX_CHUNKS):
            if n >= RAW_SLOTS:
                sp.wait_ge(*sg.event("mix_used", n - RAW_SLOTS))
            if (kind, i) == ("o", 0):
                sp.wait_ge(*sg.event("pre", 7))
                sp.dma_start(m["pw"][:], W["pool_w_2"][0].rearrange("g c d -> c g d")).then_inc(*sg.inc("mix_small", "pw", n=16))
            src = w_out[:, :, i * 256:(i + 1) * 256] if kind == "out" else \
                w_in[:, :, MIX_COLUMN[kind] + i * 256:MIX_COLUMN[kind] + i * 256 + 256]
            sp.dma_start(m["RAW"][:, n % RAW_SLOTS, :].rearrange("p (k n) -> p k n", k=KD), src).then_inc(*sg.inc(f"mix_raw{n % RAW_SLOTS}", also=[("raw", n)], n=16))
        return

    if who == "act":
        act = engine
        fed = [0]

        def feed(upto):
            while fed[0] <= min(upto, CC - 1):
                n = fed[0]
                act.wait_ge(*sg.event("raw", n))
                if n >= W_SLOTS:
                    act.wait_ge(*sg.event("w_used", n - W_SLOTS))
                act.activation(m["WHI"][:, n % W_SLOTS, :], m["RAW"][:, n % RAW_SLOTS, :], ACT.Copy).then_inc(*sg.inc("mix_hi", n))
                fed[0] += 1

        for t in range(2):
            for k in range(KD):
                if t:
                    act.wait_ge(*sg.event("x1", k))
                if (t, k) >= (0, 2):
                    act.wait_ge(*sg.event("sq_used", (t, k - 2) if k >= 2 else (t - 1, KD - 2 + k)))
                act.activation(m["sq"][:, k % 2, :], X[:, k, :], ACT.Square).then_inc(*sg.inc("mix_out_act", also=[("sq", (t, k))]))
            act.wait_ge(*sg.event("stat", t))
            e = K_E5 if t else K_E6
            act.activation(m["rstd"][:], b[4][:], ACT.Sqrt, bias=K[:, e:e + 1], scale=1.0 / D).then_inc(*sg.inc("mix_out_act", also=[("root", t)]))
        for k in range(KD):
            act.wait_ge(*sg.event("h", k))
            act.activation(HH[:, k, :], m["nh"][:, k % 2, :], ACT.Copy).then_inc(*sg.inc("mix_out_act", also=[("hh", k)]))
        feed(1)
        tanh_n = 0
        for n, (kind, i) in enumerate(MIX_CHUNKS):
            feed(n + 2)
            g = MIX_FIRST[kind, i]
            if kind == "qk":
                for j in range(2):
                    act.wait_ge(*sg.event("acc", g + j))
                    if i:
                        act.wait_ge(*sg.event("pre", 2 * i + j - 2))
                    act.activation(m["xpad"][:, j, 3:3 + S], b[(g + j) % 4][:], ACT.Copy).then_inc(*sg.inc("mix_free_act", also=[("free", g + j)]))
                for j in range(2):
                    act.wait_ge(*sg.event("pre", 2 * i + j))
                    if i:
                        act.wait_ge(*sg.event("qk_done", 2 * i + j - 2))
                    act.activation(m["stm"][:, j, :], m["qk"][:, 2 * i + j, :], ACT.Tanh, scale=0.5).then_inc(*sg.inc("mix_out_act", also=[("qkt", 2 * i + j)]))
            elif kind == "v":
                for j in range(4):
                    act.wait_ge(*sg.event("acc", g + j))
                    act.activation(m["v2"][:, j, i * 256:(i + 1) * 256], b[(g + j) % 4][:, 0:256], ACT.Copy).then_inc(*sg.inc("mix_free_act", also=[("free", g + j)]))
                if i == 0:
                    act.wait_ge(*sg.event("row_abs"))
                    act.activation(m["row"][0:4, 2, :], m["row"][0:4, 1, :], ACT.Exp, scale=-1.0).then_inc(*sg.inc("mix_out_act", also=[("row_exp", None)]))
                else:
                    act.wait_ge(*sg.event("row_m"))
                    act.activation(m["row"][0:4, 2, :], m["row"][0:4, 1, :], ACT.Exp, scale=-1.0).then_inc(*sg.inc("mix_out_act", also=[("row_em", None)]))
            elif kind == "o":
                for j in range(2):
                    act.wait_ge(*sg.event("acc", g + j))
                    act.activation(m["tho"][:, 2 * i + j, :], b[(g + j) % 4][:], ACT.Tanh, scale=0.5).then_inc(*sg.inc("mix_free_act", also=[("free", g + j)]))
            elif kind == "u":
                for j in range(2):
                    act.wait_ge(*sg.event("acc", g + j))
                    if i:
                        act.wait_ge(*sg.event("pooled", j))
                    act.activation(m["upad"][:, j, 16:16 + S], b[(g + j) % 4][:], ACT.Copy).then_inc(*sg.inc("mix_free_act", also=[("free", g + j), ("u", 2 * i + j)]))
                if i:
                    break
        for j in range(4):
            act.wait_ge(*sg.event("yp", j))
            act.activation(HH[:, 4 + j, :], m["yp"][:, j, :], ACT.Copy).then_inc(*sg.inc("mix_out_act", also=[("yph", j)]))
        feed(MIX_AT["out", 0])
        feed(MIX_AT["out", 2])
        for h in range(MH):
            for s in range(4):
                w, n = (4 - s) * P, 4 * h + s
                act.wait_ge(*sg.event("e1", n))
                act.activation(m["dec"][:, s % 2, 0:w], m["dec"][:, s % 2, 0:w], ACT.Exp).then_inc(*sg.inc("mix_out_act", also=[("dec", n)]))
        for h in range(MH):
            act.wait_ge(*sg.event("hc", h))
            if h >= 2:
                act.wait_ge(*sg.event("var", h - 2))
            act.activation(m["sq"][:, h % 2, :], m["hm"][:, h, :], ACT.Square).then_inc(*sg.inc("mix_out_act", also=[("hsq", h)]))
        for h in range(MH):
            act.wait_ge(*sg.event("var", h))
            act.activation(m["hr"][:, h, :], b[h][:], ACT.Sqrt, bias=K[:, K_E5:K_E5 + 1], scale=1.0 / MD).then_inc(*sg.inc("mix_out_act", also=[("hroot", h)]))
        for h in range(MH):
            act.wait_ge(*sg.event("ym", h))
            act.activation(HH[:, h, :], m["hm"][:, h, :], ACT.Copy).then_inc(*sg.inc("mix_out_act", also=[("ymh", h)]))
        for i in range(4):
            feed(MIX_AT["out", i] + 2)

    if who == "dve":
        v = engine

        fed = [0]

        def feed(upto):
            while fed[0] <= min(upto, CC - 1):
                n = fed[0]
                v.wait_ge(*sg.event("mix_hi", n))
                v.tensor_tensor(m["WLO"][:, n % W_SLOTS, :], m["RAW"][:, n % RAW_SLOTS, :], f(m["WHI"])[:, n % W_SLOTS, :],
                                        ALU.subtract).then_inc(*sg.inc("mix_used", n, also=[("w", n)]))
                fed[0] += 1

        v.wait_ge(*sg.event("small"))
        v.tensor_scalar(vec[:, V2_HN:V2_HN + 4], vec[:, V2_HN:V2_HN + 4], 0.5, None, ALU.mult).then_inc(*sg.inc("mix_dve"))
        v.wait_ge(*sg.last("mix_dve"))
        for t in range(2):
            v.wait_ge(*sg.event("root", t))
            v.reciprocal(m["rstd"][:], m["rstd"][:]).then_inc(*sg.inc("mix_dve"))
            v.wait_ge(*sg.last("mix_dve"))
            for k in range(KD):
                if t == 0:
                    v.scalar_tensor_tensor(X[:, k, :], X[:, k, :], vec[:, V2_FIN + k:V2_FIN + k + 1], m["rstd"][:],
                                               ALU.mult, ALU.mult).then_inc(*sg.inc("mix_out_dve", also=[("x1", k)]))
                else:
                    if k >= 2:
                        v.wait_ge(*sg.event("hh", k - 2))
                        v.wait_ge(*sg.event("hl", k - 2))
                    v.scalar_tensor_tensor(m["nh"][:, k % 2, :], X[:, k, :], vec[:, V2_N1 + k:V2_N1 + k + 1], m["rstd"][:],
                                               ALU.mult, ALU.mult).then_inc(*sg.inc("mix_out_dve", also=[("h", k)]))
                    v.wait_ge(*sg.event("h", k))
                    v.wait_ge(*sg.event("hh", k))
                    v.tensor_tensor(HL[:, k, :], m["nh"][:, k % 2, :], f(HH)[:, k, :], ALU.subtract).then_inc(*sg.inc("mix_out_dve", also=[("hl", k)]))
        feed(1)
        row = lambda r: m["row"][0:4, r, :]
        for n, (kind, i) in enumerate(MIX_CHUNKS):
            feed(n + 2)
            g = MIX_FIRST[kind, i]
            if kind == "gate":
                v.wait_ge(*sg.event("acc", g))
                v.tensor_scalar(row(0), b[g % 4][0:4, :], vec[0:4, V2_IG:V2_IG + 1], None, ALU.add).then_inc(*sg.inc("mix_free_dve", also=[("free", g)]))
                v.wait_ge(*sg.event("acc", g + 1))
                v.tensor_scalar(row(5), b[(g + 1) % 4][0:4, :], vec[0:4, V2_FG:V2_FG + 1], None, ALU.add).then_inc(*sg.inc("mix_free_dve", also=[("free", g + 1)]))
                v.wait_ge(*sg.event("free", g + 1))
                v.tensor_scalar(row(3), row(5), -1.0, None, ALU.mult).then_inc(*sg.inc("mix_dve"))
                v.wait_ge(*sg.last("mix_dve"))
                v.tensor_tensor(row(1), row(5), row(3), ALU.max).then_inc(*sg.inc("mix_out_dve", also=[("row_abs", None)]))
            elif kind == "qk":
                for j in range(2):
                    blk = 2 * i + j
                    pre, pad = m["qk"][:, blk, :], m["xpad"][:, j, :]
                    cw = lambda t: vec[:, V2_CW + 8 * t + blk:V2_CW + 8 * t + blk + 1]
                    v.wait_ge(*sg.event("free", g + j))
                    v.tensor_scalar(pre, pad[:, 0:S], cw(0), None, ALU.mult).then_inc(*sg.inc("mix_dve"))
                    v.wait_ge(*sg.last("mix_dve"))
                    v.scalar_tensor_tensor(pre, pad[:, 1:1 + S], cw(1), pre, ALU.mult, ALU.add).then_inc(*sg.inc("mix_dve"))
                    v.wait_ge(*sg.last("mix_dve"))
                    v.scalar_tensor_tensor(pre, pad[:, 2:2 + S], cw(2), pre, ALU.mult, ALU.add).then_inc(*sg.inc("mix_dve"))
                    v.wait_ge(*sg.last("mix_dve"))
                    v.scalar_tensor_tensor(pre, pad[:, 3:3 + S], cw(3), pre, ALU.mult, ALU.add).then_inc(*sg.inc("mix_out_dve", also=[("pre", blk)]))
                for j in range(2):
                    blk = 2 * i + j
                    v.wait_ge(*sg.event("qkt", blk))
                    v.scalar_tensor_tensor(m["qk"][:, blk, :], m["stm"][:, j, :], 1.0, m["qk"][:, blk, :], ALU.add, ALU.mult).then_inc(*sg.inc("mix_out_dve", also=[("qk_done", blk)]))
            elif kind == "v" and i == 0:
                v.wait_ge(*sg.event("row_exp"))
                log1p(v, sg, "mix_dve", row(1), row(2), row(4), row(6))
                v.tensor_scalar(row(3), row(3), 0.0, None, ALU.max).then_inc(*sg.inc("mix_dve"))
                v.wait_ge(*sg.last("mix_dve"))
                v.tensor_tensor(row(3), row(3), row(1), ALU.add).then_inc(*sg.inc("mix_dve"))
                v.wait_ge(*sg.last("mix_dve"))
                v.tensor_scalar(row(3), row(3), -1.0, None, ALU.mult).then_inc(*sg.inc("mix_dve"))
                v.wait_ge(*sg.last("mix_dve"))
                v.memset(row(6), 1.0).then_inc(*sg.inc("mix_dve"))
                v.wait_ge(*sg.last("mix_dve"))
                v.tensor_tensor_scan(row(4), row(6), row(3), 0.0, ALU.mult, ALU.add).then_inc(*sg.inc("mix_dve"))
                v.wait_ge(*sg.last("mix_dve"))
                v.tensor_tensor(row(0), row(0), row(4), ALU.subtract).then_inc(*sg.inc("mix_dve"))
                v.wait_ge(*sg.last("mix_dve"))
                v.tensor_tensor_scan(row(5), row(0), row(0), 0.0, ALU.max, ALU.max).then_inc(*sg.inc("mix_dve"))
                v.wait_ge(*sg.last("mix_dve"))
                v.tensor_tensor(row(1), row(4), row(5), ALU.add).then_inc(*sg.inc("mix_out_dve", also=[("row_m", None)]))
                v.tensor_scalar(row(5), row(5), -1.0, None, ALU.mult).then_inc(*sg.inc("mix_out_dve", also=[("row_nm", None)]))
            elif kind == "v":
                v.wait_ge(*sg.event("gcol_t"))
                v.tensor_copy(m["gcol"][:], b[5][:, 0:16]).then_inc(*sg.inc("mix_out_dve", also=[("gcol", None)]))
            elif kind == "u":
                if i == 0:
                    v.memset(m["upad"][:, :, 0:16], 0.0)
                    v.memset(m["spad"][:, :, 0:16], 0.0).then_inc(*sg.inc("mix_dve"))
                    v.wait_ge(*sg.last("mix_dve"))
                for j in range(2):
                    gi = 2 * i + j
                    v.wait_ge(*sg.event("u", gi))
                    if gi >= 1:
                        v.wait_ge(*sg.event("pooled", gi - 1))
                    u = m["upad"][:, j, :]
                    src = u
                    for d in range(gi + 1):
                        dst = m["spad"][:, d % 2, :]
                        v.tensor_tensor(dst[:, 16:16 + S], src[:, 16:16 + S], src[:, 16 - (1 << d):16 - (1 << d) + S], ALU.add).then_inc(*sg.inc("mix_dve"))
                        v.wait_ge(*sg.last("mix_dve"))
                        src = dst
                    w = 1 << (gi + 1)
                    if gi >= 2:
                        v.wait_ge(*sg.event("ps_used", gi - 2))
                    pl = m["pl"][:, gi % 2, :]
                    v.scalar_tensor_tensor(pl[:, w:S], src[:, 16 + w:16 + S], 1.0 / w, u[:, 16 + w:16 + S], ALU.mult, ALU.subtract)
                    v.tensor_tensor(pl[:, 0:w], src[:, 16:16 + w], m["inv"][:, 0:w], ALU.mult).then_inc(*sg.inc("mix_dve"))
                    v.wait_ge(*sg.last("mix_dve"))
                    v.tensor_tensor(pl[:, 0:w], pl[:, 0:w], u[:, 16:16 + w], ALU.subtract).then_inc(*sg.inc("mix_out_dve", also=[("pooled", gi)]))
                    v.wait_ge(*sg.event("mixed", gi))
                    v.tensor_scalar(m["yp"][:, gi, :], b[4 + gi][:], vec[:, V2_PS + gi:V2_PS + gi + 1], None, ALU.mult).then_inc(*sg.inc("mix_out_dve", also=[("yp", gi)]))
                if i:
                    break
        for j in range(4):
            v.wait_ge(*sg.event("yp", j))
            v.wait_ge(*sg.event("yph", j))
            v.tensor_tensor(HL[:, 4 + j, :], m["yp"][:, j, :], f(HH)[:, 4 + j, :], ALU.subtract).then_inc(*sg.inc("mix_out_dve", also=[("ypl", j)]))
        feed(MIX_AT["out", 2])
        v.wait_ge(*sg.event("gcol"))
        for h in range(MH):
            for s in range(4):
                w, n = (4 - s) * P, 4 * h + s
                v.wait_ge(*sg.event("nmb", h))
                if n >= 2:
                    v.wait_ge(*sg.event("pm", n - 2))
                v.tensor_scalar(m["dec"][:, s % 2, 0:w], b[0][:, s * P:S], m["gcol"][:, 4 * s + h:4 * s + h + 1], 0.0,
                                    ALU.add, ALU.min).then_inc(*sg.inc("mix_out_dve", also=[("e1", n)]))
                if s >= 1:
                    scores(v, m, b, sg, h, s - 1)
            scores(v, m, b, sg, h, 3)
            t = m["dn"][:]
            v.wait_ge(*sg.event("numden", h))
            v.tensor_scalar(t, b[5][:], -1.0, None, ALU.mult).then_inc(*sg.inc("mix_dve"))
            v.wait_ge(*sg.last("mix_dve"))
            v.tensor_tensor(t, t, b[5][:], ALU.max).then_inc(*sg.inc("mix_dve"))
            v.wait_ge(*sg.last("mix_dve"))
            v.tensor_tensor(t, t, b[1][:], ALU.max).then_inc(*sg.inc("mix_dve"))
            v.wait_ge(*sg.last("mix_dve"))
            v.reciprocal(t, t).then_inc(*sg.inc("mix_dve"))
            v.wait_ge(*sg.last("mix_dve"))
            v.tensor_tensor(m["hm"][:, h, :], t, b[4][:], ALU.mult).then_inc(*sg.inc("mix_out_dve", also=[("hm", h)]))
        for h in range(MH):
            v.wait_ge(*sg.event("mean", h))
            v.scalar_tensor_tensor(m["hm"][:, h, :], b[4 + h][:], -1.0 / MD, m["hm"][:, h, :], ALU.mult, ALU.add).then_inc(*sg.inc("mix_out_dve", also=[("hc", h)]))
        for h in range(MH):
            v.wait_ge(*sg.event("hroot", h))
            v.wait_ge(*sg.event("hc", h))
            v.reciprocal(m["hr"][:, h, :], m["hr"][:, h, :]).then_inc(*sg.inc("mix_dve"))
            v.wait_ge(*sg.last("mix_dve"))
            v.scalar_tensor_tensor(m["hm"][:, h, :], m["hm"][:, h, :], vec[:, V2_HN + h:V2_HN + h + 1], m["hr"][:, h, :], ALU.mult, ALU.mult).then_inc(*sg.inc("mix_dve"))
            v.wait_ge(*sg.last("mix_dve"))
            v.scalar_tensor_tensor(m["hm"][:, h, :], m["tho"][:, h, :], 1.0, m["hm"][:, h, :], ALU.add, ALU.mult).then_inc(*sg.inc("mix_out_dve", also=[("ym", h)]))
        for h in range(MH):
            v.wait_ge(*sg.event("ym", h))
            v.wait_ge(*sg.event("ymh", h))
            v.tensor_tensor(HL[:, h, :], m["hm"][:, h, :], f(HH)[:, h, :], ALU.subtract).then_inc(*sg.inc("mix_out_dve", also=[("yml", h)]))
        for i in range(4):
            feed(MIX_AT["out", i] + 2)
            g = MIX_FIRST["out", i]
            for j in range(2):
                v.wait_ge(*sg.event("acc", g + j))
                v.wait_ge(*sg.event("x1", 2 * i + j))
                v.tensor_tensor(X[:, 2 * i + j, :], X[:, 2 * i + j, :], b[(g + j) % 4][:], ALU.add).then_inc(*sg.inc("mix_free_dve", also=[("free", g + j), ("x2", 2 * i + j)]))

    if who == "pe":
        pe = engine

        for t in range(2):
            for k in range(KD):
                pe.wait_ge(*sg.event("sq", (t, k)))
                if t and k == 0:
                    pe.wait_ge(*sg.event("root", 0))
                ins = pe.matmul(b[4][:], one, m["sq"][:, k % 2, :], start=(k == 0), stop=(k == KD - 1))
                ins.then_inc(*sg.inc("mix_pe", also=[("sq_used", (t, k)), *([("stat", t)] if k == KD - 1 else [])]))
        pe.wait_ge(*sg.event("hl", KD - 1))

        def bank(g):
            if g >= 4:
                pe.wait_ge(*sg.event("free", g - 4))
            return b[g % 4]

        for n, (kind, i) in enumerate(MIX_CHUNKS):
            if kind == "out" and i == 0:
                mlstm_pe(pe, m, b, sg, one)
            pe.wait_ge(*sg.event("w", n))
            hi, lo = m["WHI"][:, n % W_SLOTS, :], m["WLO"][:, n % W_SLOTS, :]
            g = MIX_FIRST[kind, i]
            for j in range(MIX_GROUPS[kind]):
                o = bank(g + j)
                for k in range(KD):
                    if kind == "v":
                        tok = slice(j * P, (j + 1) * P)
                        ins = split3(pe, o[:, 0:256], HH[:, k, tok], HL[:, k, tok], hi[:, k * 256:(k + 1) * 256],
                                     lo[:, k * 256:(k + 1) * 256], k == 0, k == KD - 1)
                    else:
                        c = k * 256 + j * (4 if kind == "gate" else P)
                        ins = split3(pe, o[:], hi[:, c:c + P], lo[:, c:c + P], HH[:, k, :], HL[:, k, :], k == 0, k == KD - 1)
                ins.then_inc(*sg.inc("mix_pe", also=[("acc", g + j), *([("w_used", n)] if j == MIX_GROUPS[kind] - 1 else [])]))
            if (kind, i) == ("o", 0):
                pe.wait_ge(*sg.event("row_m"))
                for s in range(4):
                    ins = pe.transpose(b[5][:, 4 * s:4 * s + 4], m["row"][0:4, 0, s * P:(s + 1) * P], K[0:4, K_ID:K_ID + 4])
                ins.then_inc(*sg.inc("mix_pe", also=[("gcol_t", None)]))


def scores(v, m, b, sg, h, s):
    w, n = (4 - s) * P, 4 * h + s
    v.wait_ge(*sg.event("dec", n))
    v.wait_ge(*sg.event("sc", n))
    if n >= 4:
        v.wait_ge(*sg.event("numden", h - 1))
    pm = m["pm"][:, T_AT[s]:T_AT[s] + w]
    v.scalar_tensor_tensor(pm, b[2 + s % 2][:, 0:w], 0.25 * MD ** -0.5, m["dec"][:, s % 2, 0:w], ALU.mult, ALU.mult).then_inc(*sg.inc("mix_dve"))
    v.wait_ge(*sg.last("mix_dve"))
    v.tensor_tensor(pm[:, 0:P], pm[:, 0:P], m["tri"][:], ALU.mult).then_inc(*sg.inc("mix_out_dve", also=[("pm", n)]))


def mlstm_pe(pe, m, b, sg, one):
    pe.wait_ge(*sg.event("mix_small", "pw"))
    for gi in range(4):
        pe.wait_ge(*sg.event("pooled", gi))
        pe.matmul(b[4 + gi][:], m["pw"][:, gi, :], m["pl"][:, gi % 2, :], start=True, stop=True).then_inc(*sg.inc("mix_pe", also=[("mixed", gi), ("ps_used", gi)]))
    pe.wait_ge(*sg.event("free", MIX_FIRST["u", 1] + 1))
    pe.wait_ge(*sg.event("row_nm"))
    pe.wait_ge(*sg.event("row_em"))
    pe.wait_ge(*sg.event("yp", 3))
    pe.wait_ge(*sg.event("qk_done", 7))
    for h in range(MH):
        sel = m["sel4"][0:4, h * P:(h + 1) * P]
        if h:
            pe.wait_ge(*sg.event("e1", 4 * h - 1))
            pe.wait_ge(*sg.event("hm", h - 1))
        pe.matmul(b[0][:], sel, m["row"][0:4, 5, :], start=True, stop=True).then_inc(*sg.inc("mix_pe", also=[("nmb", h)]))
        pe.matmul(b[1][:], sel, m["row"][0:4, 2, :], start=True, stop=True)
        for s in range(4):
            n = 4 * h + s
            if n >= 2:
                pe.wait_ge(*sg.event("pm", n - 2))
            w = (4 - s) * P
            pe.matmul(b[2 + s % 2][:, 0:w], m["qk"][:, 4 + h, s * P:(s + 1) * P], m["qk"][:, h, s * P:S], start=True, stop=True).then_inc(*sg.inc("mix_pe", also=[("sc", n)]))
            if s:
                numden(pe, m, b, sg, one, h, s - 1)
        numden(pe, m, b, sg, one, h, 3)
    for h in range(MH):
        pe.wait_ge(*sg.event("hm", h))
        if h == 0:
            pe.wait_ge(*sg.event("hm", 3))
        pe.matmul(b[4 + h][:], one, m["hm"][:, h, :], start=True, stop=True).then_inc(*sg.inc("mix_pe", also=[("mean", h)]))
    for h in range(MH):
        pe.wait_ge(*sg.event("hsq", h))
        pe.wait_ge(*sg.event("pm", 15))
        pe.matmul(b[h][:], one, m["sq"][:, h % 2, :], start=True, stop=True).then_inc(*sg.inc("mix_pe", also=[("var", h)]))
    pe.wait_ge(*sg.event("yml", 3))
    pe.wait_ge(*sg.event("ypl", 3))
    pe.wait_ge(*sg.event("hroot", 3))


def numden(pe, m, b, sg, one, h, s):
    w = (4 - s) * P
    pe.wait_ge(*sg.event("pm", 4 * h + s))
    pm = m["pm"][:, T_AT[s]:T_AT[s] + w]
    pe.matmul(b[4][:, s * P:S], m["v2"][:, s, h * P:(h + 1) * P], pm, start=(s == 0), stop=(s == 3))
    ins = pe.matmul(b[5][:, s * P:S], one, pm, start=(s == 0), stop=(s == 3))
    if s == 3:
        ins.then_inc(*sg.inc("mix_pe", also=[("numden", h)]))


def mix_tensors(at, tail):
    at("qk", 128, [P, KD, S])
    at("hr", 128, [P, MH, S])
    at("v2", 144, [P, NT, MH * MD])
    at("tho", 152, [P, MH, S])
    at("row", 160, [P, 7, S])
    at("yp", 174, [P, 4, S])
    at("hm", 174, [P, MH, S])
    at("stm", 182, [P, 2, S])
    at("upad", 182, [P, 2, S + 16])
    at("spad", 186.25, [P, 2, S + 16])
    at("dec", 182, [P, 2, S])
    at("pm", 186, [P, 1280])
    at("dn", 192, [P, S])
    at("pw", 194, [P, 4, P])
    at("pl", 198.125, [P, 2, S])
    o = tail
    for name, shape in (("vec2", [P, NV2]), ("tri", [P, P]), ("inv", [P, 16]), ("gcol", [P, 16]), ("sel4", [4, MH * P])):
        at(name, o / KB, shape)
        size = 4
        for n in shape[1:]:
            size *= n
        o += (size + 31) // 32 * 32
    return o

ROUTE_SIGNALS = """ro_small ro_bias ro_act ro_dve ro_pe ro_pool ro_store ro_step"""
NB = MAXB + 1
MOE_SLOTS = 12
MOE_CHUNKS = [(w, f, a) for f in range(2) for w in ("gate", "up") for a in range(2)] + \
             [("down", 0, 0), ("down", 1, 0), ("down", 0, 1), ("down", 1, 1)]
MOE_SIGNALS = "mo_gain mo_act mo_dve mo_pe mo_idx mo_x mo_y " + " ".join(f"mo_raw{c}" for c in range(MOE_SLOTS))
MOE_SEEDED = ("mo_act", "mo_dve", "mo_pe", "mo_x", "mo_y")


class LoopSignals(Signals):

    def total(self, sem):
        return self.known.get(("total", sem), ("", 1))[1]

    def close(self):
        for sem, count in self.count.items():
            self.at["total", sem] = (sem, count)

    def event(self, name, number=None, loop=None, back=0):
        if not self.known:
            return self.sem["mo_pe"], loop + 1
        sem, value = self.known[name, number]
        total = self.total(sem)
        return self.sem[sem], loop * total + (value + total * ((sem in MOE_SEEDED) - back))


def route_program(engine, who, sg, m, b, W, mo):
    K, X, vec = m["K"], m["X"], m["vec2"]
    one = K[:, K_ONE:K_ONE + P]
    ident = K[:, K_ID:K_ID + P]

    if who == "sp":
        sp = engine
        for dst, src in ((m["wr"][:], W["w_router_2"][0].rearrange("(k p) e -> p k e", p=P)),
                         (m["brow"][:], W["b_router_2"]),
                         (m["lt"][:], W["consts"][:, K_LT:K_LT + P]), (m["i32"][:], W["consts"][:, K_I32:K_I32 + EXPERTS]),
                         (m["i48"][:], W["consts"][:, K_I48:K_I48 + NB + 1]), (m["i128"][:], W["consts"][:, K_I128:K_I128 + P])):
            sp.dma_start(dst, src).then_inc(*sg.inc("ro_small", also=[("rsmall", None)], n=16))
        for j in range(3):
            for i, name in enumerate(("b_gate_2", "b_up_2", "b_down_2")):
                sp.dma_start(m["bf"][32 * j:32 * j + 32, i * D:(i + 1) * D], W[name][0]).then_inc(*sg.inc("ro_bias", also=[("bias", None)], n=16))
        for t in range(NT):
            sp.wait_ge(*sg.event("evac", 2 * t + 1))
            sp.dma_start(W["h2tok"][t * P:(t + 1) * P, :], m["h2t"][:, t, :]).then_inc(*sg.inc("ro_store", also=[("stored", None)], n=16))
        sp.wait_ge(*sg.event("bei"))
        return

    if who == "act":
        act = engine
        for k in range(KD):
            if k >= 2:
                act.wait_ge(*sg.event("sq_used", k - 2))
            act.activation(m["sqm"][:, k % 2, :], X[:, k, :], ACT.Square).then_inc(*sg.inc("ro_act", k, also=[("sq", k)]))
        act.wait_ge(*sg.event("stat"))
        act.activation(m["rstdm"][:], b[4][:], ACT.Sqrt, bias=K[:, K_E5:K_E5 + 1], scale=1.0 / D).then_inc(*sg.inc("ro_act", "root", also=[("root", None)]))
        for g in range(16):
            act.wait_ge(*sg.event("tg", g))
            dst = m["h2t" if g < 8 else "x2t"][:, g % 8 // 2, (g % 2) * 512:(g % 2 + 1) * 512]
            act.activation(dst, b[g % 4][:], ACT.Copy).then_inc(*sg.inc("ro_act", ("evac", g), also=[("evac", g)]))
            if g == 7:
                act.wait_ge(*sg.event("nmx"))
                for t in range(NT):
                    ins = act.activation(m["gates"][:, 4 * t:4 * t + 4], m["mxm"][:, 8 * t:8 * t + 4], ACT.Exp,
                                         bias=m["nmx"][:, t:t + 1], accum_out=m["gs"][:, t:t + 1])
                ins.then_inc(*sg.inc("ro_act", "gexp", also=[("gexp", None)]))

    if who == "dve":
        v = engine

        v.wait_ge(*sg.event("root"))
        v.reciprocal(m["rstdm"][:], m["rstdm"][:]).then_inc(*sg.inc("ro_step"))
        v.wait_ge(*sg.last("ro_step"))
        for k in range(KD):
            v.scalar_tensor_tensor(m["h2T"][:, k, :], X[:, k, :], vec[:, V2_N2 + k:V2_N2 + k + 1], m["rstdm"][:],
                                        ALU.mult, ALU.mult).then_inc(*sg.inc("ro_dve", also=[("h2", k)]))
        v.wait_ge(*sg.event("logits"))
        L, mx, mi = m["L"], m["mxm"], m["mi"]
        v.tensor_copy(L[:], b[5][:, 0:P]).then_inc(*sg.inc("ro_step"))
        v.wait_ge(*sg.last("ro_step"))
        for t in range(NT):
            ins = v.max(mx[:, 8 * t:8 * t + 8], L[:, 32 * t:32 * t + 32])
        ins.then_inc(*sg.inc("ro_step"))
        v.wait_ge(*sg.last("ro_step"))
        for t in range(NT):
            v.max_index(mi[:, 8 * t:8 * t + 8], mx[:, 8 * t:8 * t + 8], L[:, 32 * t:32 * t + 32])
        v.tensor_scalar(m["nmx"][:], mx[:].rearrange("p (t k) -> p t k", k=8)[:, :, 0], -1.0, None, ALU.mult).then_inc(*sg.inc("ro_step"))
        v.wait_ge(*sg.last("ro_step"))
        v.tensor_copy(m["mif"][:], mi[:]).then_inc(*sg.inc("ro_dve", also=[("nmx", None)]))
        v.wait_ge(*sg.event("rsmall"))
        v.wait_ge(*sg.event("nmx"))
        oh = m["oh"]
        for k in range(TOP):
            for t in range(NT):
                ins = v.tensor_scalar(oh[:, k, t * 32:t * 32 + 32], m["i32"][:], m["mif"][:, 8 * t + k:8 * t + k + 1], None, ALU.is_equal)
        ins.then_inc(*sg.inc("ro_step"))
        v.wait_ge(*sg.last("ro_step"))
        v.tensor_tensor(m["M"][:], oh[:, 0, :], oh[:, 1, :], ALU.add).then_inc(*sg.inc("ro_step"))
        v.wait_ge(*sg.last("ro_step"))
        v.tensor_tensor(m["M"][:], m["M"][:], oh[:, 2, :], ALU.add).then_inc(*sg.inc("ro_step"))
        v.wait_ge(*sg.last("ro_step"))
        v.tensor_tensor(m["M"][:], m["M"][:], oh[:, 3, :], ALU.add).then_inc(*sg.inc("ro_dve", also=[("M", None)]))
        v.wait_ge(*sg.event("ranks"))
        cnt, nb, incl, excl, be = m["cnt"][:], m["nb"][:], m["incl"][:], m["excl"][:], m["bef"][:]
        rk, rb, sr, pr = m["rk"][:], m["rb"][:], m["sr"][:], m["pr"][:]
        v.tensor_copy(rk, b[6][:, 0:P])
        v.tensor_copy(cnt, b[6][:, P:P + 32]).then_inc(*sg.inc("ro_step"))
        v.wait_ge(*sg.last("ro_step"))
        v.tensor_scalar(nb, cnt, 0.0, None, ALU.is_gt).then_inc(*sg.inc("ro_step"))
        v.wait_ge(*sg.last("ro_step"))
        for j in range(1, NT):
            v.scalar_tensor_tensor(nb, cnt, float(P * j), nb, ALU.is_gt, ALU.add).then_inc(*sg.inc("ro_step"))
            v.wait_ge(*sg.last("ro_step"))
        v.tensor_tensor_scan(incl, one[:, 0:32], nb, 0.0, ALU.mult, ALU.add).then_inc(*sg.inc("ro_step"))
        v.wait_ge(*sg.last("ro_step"))
        v.tensor_scalar(be, m["i48"][:], incl[:, 0:1], None, ALU.is_ge).then_inc(*sg.inc("ro_step"))
        v.wait_ge(*sg.last("ro_step"))
        for e in range(1, EXPERTS):
            v.scalar_tensor_tensor(be, m["i48"][:], incl[:, e:e + 1], be, ALU.is_ge, ALU.add).then_inc(*sg.inc("ro_step"))
            v.wait_ge(*sg.last("ro_step"))
        v.tensor_scalar(be, be, float(EXPERTS - 1), None, ALU.min).then_inc(*sg.inc("ro_step"))
        v.wait_ge(*sg.last("ro_step"))
        v.tensor_copy(m["bei"][:, 0:NB], be[0:1, 0:NB])
        v.tensor_copy(m["bei"][:, NB:NB + 1], incl[0:1, 31:32]).then_inc(*sg.inc("ro_dve", also=[("bei", None)]))
        v.tensor_tensor(excl, incl, nb, ALU.subtract).then_inc(*sg.inc("ro_step"))
        v.wait_ge(*sg.last("ro_step"))
        v.tensor_scalar(rb, rk, float(P), None, ALU.is_ge).then_inc(*sg.inc("ro_step"))
        v.wait_ge(*sg.last("ro_step"))
        for j in range(2, NT):
            v.scalar_tensor_tensor(rb, rk, float(P * j), rb, ALU.is_ge, ALU.add).then_inc(*sg.inc("ro_step"))
            v.wait_ge(*sg.last("ro_step"))
        v.scalar_tensor_tensor(rk, rb, -float(P), rk, ALU.mult, ALU.add).then_inc(*sg.inc("ro_step"))
        v.wait_ge(*sg.last("ro_step"))
        for t in range(NT):
            ins = v.tensor_tensor(sr[:, t * 32:t * 32 + 32], rb[:, t * 32:t * 32 + 32], excl, ALU.add)
        ins.then_inc(*sg.inc("ro_step"))
        v.wait_ge(*sg.last("ro_step"))
        for k in range(TOP):
            for src, dst in ((sr, "bk"), (rk, "pk")):
                v.tensor_tensor(pr, oh[:, k, :], src, ALU.mult).then_inc(*sg.inc("ro_step"))
                v.wait_ge(*sg.last("ro_step"))
                v.tensor_reduce(m[dst][:, 4 * k:4 * k + 4], pr.rearrange("p (t e) -> p t e", e=32), AX.X, ALU.add).then_inc(*sg.inc("ro_step"))
                v.wait_ge(*sg.last("ro_step"))
        v.scalar_tensor_tensor(m["df"][:], m["bk"][:], float(P), m["pk"][:], ALU.mult, ALU.add).then_inc(*sg.inc("ro_step"))
        v.wait_ge(*sg.last("ro_step"))
        v.tensor_copy(m["dest"][:], m["df"][:])
        for n in range(16):
            t = n % 4
            if n >= 2:
                v.wait_ge(*sg.event("ohp_used", n - 2))
            v.tensor_scalar(m["ohp"][:, n % 2, :], m["i128"][:], m["pk"][:, n:n + 1], None, ALU.is_equal)
            v.tensor_scalar(m["ohb"][:, n % 2, :], m["i48"][:], m["bk"][:, n:n + 1], vec[:, V2_TOK + t:V2_TOK + t + 1],
                                 ALU.is_equal, ALU.mult).then_inc(*sg.inc("ro_dve", also=[("ohp", n)]))
        v.wait_ge(*sg.event("tokens"))
        v.tensor_copy(m["tokcol"][:], b[7][:, 0:NB + 1]).then_inc(*sg.inc("ro_dve", also=[("tokcol", None)]))
        v.wait_ge(*sg.event("gexp"))
        v.reciprocal(m["gs"][:], m["gs"][:]).then_inc(*sg.inc("ro_step"))
        v.wait_ge(*sg.last("ro_step"))
        for t in range(NT):
            v.tensor_scalar(m["gates"][:, 4 * t:4 * t + 4], m["gates"][:, 4 * t:4 * t + 4], m["gs"][:, t:t + 1], None, ALU.mult)
        v.wait_ge(*sg.event("bp"))
        v.tensor_scalar(m["pmb"][:], one[0:96, :], vec[0:96, V2_PM:V2_PM + 1], None, ALU.mult).then_inc(*sg.inc("ro_step"))
        v.wait_ge(*sg.last("ro_step"))
        v.tensor_scalar(m["sel"][:], m["pmb"][:], m["bef"][0:96, 0:1], None, ALU.is_equal)
        for half in range(2):
            v.wait_ge(*sg.event("tx0", half))
            v.tensor_copy(m["xT"][:, 4 * half:4 * half + 4, :], b[7 - half][:])
        v.drain().then_inc(mo.sem["mo_dve"], mo.total("mo_dve"))

    if who == "pe":
        pe = engine
        pe.nop().then_inc(mo.sem["mo_pe"], mo.total("mo_pe"))

        for k in range(KD):
            pe.wait_ge(*sg.event("sq", k))
            ins = pe.matmul(b[4][:], one, m["sqm"][:, k % 2, :], start=(k == 0), stop=(k == KD - 1))
            ins.then_inc(*sg.inc("ro_pe", also=[("sq_used", k), *([("stat", None)] if k == KD - 1 else [])]))
        pe.wait_ge(*sg.event("rsmall"))
        for t in range(NT):
            o = b[5][:, t * 32:t * 32 + 32]
            pe.matmul(o, one[0:1, :], m["brow"][:], start=True, stop=False)
            for k in range(KD):
                pe.wait_ge(*sg.event("h2", k))
                ins = pe.matmul(o, m["h2T"][:, k, t * P:(t + 1) * P], m["wr"][:, k, :], start=False, stop=(k == KD - 1))
        ins.then_inc(*sg.inc("ro_pe", also=[("logits", None)]))

        def turn(g):
            src = m["h2T"] if g < 8 else X
            if g >= 4:
                pe.wait_ge(*sg.event("evac", g - 4))
            t = g % 8 // 2
            for j in range(4):
                k = (g % 2) * 4 + j
                ins = pe.transpose(b[g % 4][:, j * P:(j + 1) * P], src[:, k, t * P:(t + 1) * P], ident)
            ins.then_inc(*sg.inc("ro_pe", also=[("tg", g)]))

        for g in range(8):
            turn(g)
        pe.wait_ge(*sg.event("M"))
        M = lambda t: m["M"][:, t * 32:t * 32 + 32]
        for t in range(NT):
            o = b[6][:, t * 32:t * 32 + 32]
            for u in range(t):
                pe.matmul(o, one, M(u), start=(u == 0), stop=False)
            pe.matmul(o, m["lt"][:], M(t), start=(t == 0), stop=True)
        for t in range(NT):
            ins = pe.matmul(b[6][:, P:P + 32], one, M(t), start=(t == 0), stop=(t == NT - 1))
        ins.then_inc(*sg.inc("ro_pe", also=[("ranks", None)]))
        for g in range(8, 16):
            turn(g)
        for n in range(16):
            pe.wait_ge(*sg.event("ohp", n))
            ins = pe.matmul(b[7][:, 0:NB + 1], m["ohp"][:, n % 2, :], m["ohb"][:, n % 2, :], start=(n == 0), stop=(n == 15))
            ins.then_inc(*sg.inc("ro_pe", also=[("ohp_used", n), *([("tokens", None)] if n == 15 else [])]))
        pe.wait_ge(*sg.event("evac", 15))
        pe.wait_ge(*sg.event("tokcol"))
        pe.wait_ge(*sg.event("x0"))
        for half in range(2):
            for j in range(4):
                ins = pe.transpose(b[7 - half][:, j * P:(j + 1) * P], m["xg"][:, (4 * half + j) * P:(4 * half + j + 1) * P], ident)
            ins.then_inc(*sg.inc("ro_pe", also=[("tx0", half)]))
        pe.wait_ge(*sg.event("bp"))

    if who == "pool":
        pool = engine
        bf, br, bp = m["bf"], m["br"], m["bp"]

        pool.wait_ge(*sg.event("bias"))
        pool.tensor_copy(bp[:], bf[:]).then_inc(*sg.inc("ro_pool", also=[("bp", None)]))
        pool.wait_ge(*sg.last("ro_pool"))
        pool.tensor_tensor(br[:], bf[:], bp[:], ALU.subtract).then_inc(*sg.inc("ro_pool", also=[("bp", None)]))
        pool.wait_ge(*sg.last("ro_pool"))
        pool.tensor_copy(bp[32:64, :], br[32:64, :])
        pool.tensor_copy(bp[64:96, :], br[64:96, :]).then_inc(*sg.inc("ro_pool", also=[("bp", None)]))
        pool.wait_ge(*sg.last("ro_pool"))
        pool.tensor_tensor(br[64:96, :], br[64:96, :], bp[64:96, :], ALU.subtract).then_inc(*sg.inc("ro_pool", also=[("bp", None)]))
        pool.wait_ge(*sg.last("ro_pool"))
        pool.tensor_copy(bp[64:96, :], br[64:96, :]).then_inc(*sg.inc("ro_pool", also=[("bp", None)]))
        pool.wait_ge(*sg.last("ro_pool"))
        pool.wait_ge(*sg.event("tokcol"))
        pool.wait_ge(*sg.event("stored"))
        pool.wait_ge(*sg.event("tg", 15))
        pool.indirect_dma_start(m["xg"][:], None, W["h2tok"][:, :],
                                bass.IndirectOffsetOnAxis(m["tokcol"][:, 0:1], 0)).then_inc(mo.sem["mo_x"], 16)
        pool.wait_ge(mo.sem["mo_x"], 16)
        pool.nop().then_inc(*sg.inc("ro_pool", "x0", also=[("x0", None)]))
        pool.wait_ge(*sg.event("tx0", 1))


def moe_sp(sp, sg, m, W, count):
    with sp.Fori(0, count) as b:
        e = sp.value_load(m["bei"][0:1, bass.ds(b, 1)], min_val=0, max_val=EXPERTS - 1)
        for c, (kind, f, a) in enumerate(MOE_CHUNKS):
            w = W[f"w_{kind}_2"][0][e].rearrange("(k p) n -> p k n", p=P)
            sp.wait_ge(*sg.event("used", c, loop=b, back=1))
            sp.dma_start(m["ring"][:, c, :].rearrange("p (k n) -> p k n", k=4),
                                 w[:, 4 * a:4 * a + 4, f * 512:(f + 1) * 512]).then_inc(*sg.inc(f"mo_raw{c}", also=[("raw", c)], n=16))
    sp.wait_ge(sg.sem["mo_y"], count * 16 + 16)
    sp.dma_start(m["gf"][:], W["normf_g_2"].rearrange("(o d) -> o d", o=1).broadcast_to([P, D])).then_inc(sg.sem["mo_gain"], 16)


def moe_act(act, sg, m, b, W, count):
    act.nop().then_inc(sg.sem["mo_act"], sg.total("mo_act"))
    act.nop().then_inc(sg.sem["mo_y"], 16)
    with act.Fori(0, count) as i:
        for f in range(2):
            act.wait_ge(*sg.event("gc", f, loop=i))
            act.activation(m["th"][:, f, :], m["gc"][:, f, :], ACT.Tanh, scale=SWIGLU_ALPHA / 2).then_inc(*sg.inc("mo_act", also=[("th", f)]))
        for f in range(2):
            act.wait_ge(*sg.event("th_t", f, loop=i))
            act.activation(m["hT"][:, 4 * f:4 * f + 4, :], b[6][:], ACT.Copy, scale=0.5).then_inc(*sg.inc("mo_act", also=[("hT", f)]))
        act.wait_ge(*sg.event("stored", loop=i, back=1))
        for o in range(2):
            act.wait_ge(*sg.event("y", o, loop=i))
            act.activation(m["ysb"][:, o * 512:(o + 1) * 512], b[4 + o][:], ACT.Copy).then_inc(*sg.inc("mo_act", also=[("ycopy", o)]))
        act.wait_ge(*sg.event("ycopy", 1, loop=i))
        act.dma_start(W["ybuf"][bass.ds(i * P, P), :], m["ysb"][:]).then_inc(*sg.inc("mo_y", also=[("stored", None)], n=16))


def moe_dve(v, sg, m, b, count):
    with v.Fori(0, count) as i:
        for f in range(2):
            gc, uc, th, hh = [m[n][:, f, :] for n in ("gc", "uc", "th", "hh")]
            v.wait_ge(*sg.event("g", f, loop=i))
            v.tensor_scalar(gc, b[2 * f][:], SWIGLU_LIMIT, None, ALU.min).then_inc(*sg.inc("mo_dve", also=[("gc", f)]))
            v.wait_ge(*sg.event("u", f, loop=i))
            v.tensor_scalar(uc, b[2 * f + 1][:], SWIGLU_LIMIT, -SWIGLU_LIMIT, ALU.min, ALU.max).then_inc(*sg.inc("mo_dve", also=[("uc", f)]))
            v.wait_ge(*sg.event("uc", f, loop=i))
            v.scalar_tensor_tensor(uc, uc, 1.0, gc, ALU.add, ALU.mult).then_inc(*sg.inc("mo_dve", also=[("up", f)]))
            v.wait_ge(*sg.event("up", f, loop=i))
            v.wait_ge(*sg.event("th", f, loop=i))
            v.scalar_tensor_tensor(hh, th, 1.0, uc, ALU.add, ALU.mult).then_inc(*sg.inc("mo_dve", also=[("hh", f)]))
        for half in range(2):
            v.wait_ge(*sg.event("tx", half, loop=i))
            v.tensor_copy(m["xT"][:, 4 * half:4 * half + 4, :], b[7][:]).then_inc(*sg.inc("mo_dve", also=[("xT", half)]))
        v.wait_ge(*sg.event("used", 9, loop=i))
        v.tensor_scalar(m["sel"][:], m["pmb"][:], m["bef"][0:96, bass.ds(i + 1, 1)], None, ALU.is_equal).then_inc(*sg.inc("mo_dve", also=[("sel", None)]))


def moe_pe(pe, sg, m, b, count):
    ident = m["K"][:, K_ID:K_ID + P]
    with pe.Fori(0, count) as i:

        def chunk(c, out, x, *keys):
            kind, f, a = MOE_CHUNKS[c]
            if a == 0:
                pe.matmul(out, m["sel"][:], m["bp"][:, {"gate": 0, "up": D, "down": 2 * D}[kind] + f * 512:][:, 0:512],
                          start=True, stop=False)
            pe.wait_ge(*sg.event("raw", c, loop=i))
            for k in range(4):
                ins = pe.matmul(out, x[:, 4 * a + k, :], m["ring"][:, c, k * 512:(k + 1) * 512], start=False, stop=(a == 1 and k == 3))
            ins.then_inc(*sg.inc("mo_pe", also=[("used", c), *keys]))

        def turn(out, src, *keys):
            for k in range(4):
                ins = pe.transpose(out[:, k * P:(k + 1) * P], src[:, k * P:(k + 1) * P], ident)
            ins.then_inc(*sg.inc("mo_pe", also=[*keys]))

        pe.wait_ge(*sg.event("sel", loop=i, back=1))
        pe.wait_ge(*sg.event("xT", 1, loop=i, back=1))
        for f in range(2):
            pe.wait_ge(*sg.event("gc", f, loop=i, back=1))
            chunk(4 * f, b[2 * f][:], m["xT"])
            chunk(4 * f + 1, b[2 * f][:], m["xT"], ("g", f))
            pe.wait_ge(*sg.event("uc", f, loop=i, back=1))
            chunk(4 * f + 2, b[2 * f + 1][:], m["xT"])
            chunk(4 * f + 3, b[2 * f + 1][:], m["xT"], ("u", f))
        pe.wait_ge(*sg.event("hh", 0, loop=i))
        pe.wait_ge(*sg.event("hT", 1, loop=i, back=1))
        turn(b[6], m["hh"][:, 0, :], ("th_t", 0))
        pe.wait_ge(*sg.event("gathered", loop=i))
        turn(b[7], m["xg"][:, 0:512], ("tx", 0))
        pe.wait_ge(*sg.event("ycopy", 0, loop=i, back=1))
        pe.wait_ge(*sg.event("hT", 0, loop=i))
        chunk(8, b[4][:], m["hT"])
        pe.wait_ge(*sg.event("ycopy", 1, loop=i, back=1))
        chunk(9, b[5][:], m["hT"])
        pe.wait_ge(*sg.event("hh", 1, loop=i))
        turn(b[6], m["hh"][:, 1, :], ("th_t", 1))
        pe.wait_ge(*sg.event("xT", 0, loop=i))
        turn(b[7], m["xg"][:, 512:1024], ("tx", 1))
        pe.wait_ge(*sg.event("hT", 1, loop=i))
        chunk(10, b[4][:], m["hT"], ("y", 0))
        chunk(11, b[5][:], m["hT"], ("y", 1))


def moe_pool(pool, sg, m, W, count):
    with pool.Fori(0, count) as i:
        pool.wait_ge(*sg.event("tx", 1, loop=i, back=1))
        pool.tensor_copy(m["idx"][:], m["tokcol"][:, bass.ds(i + 1, 1)]).then_inc(sg.sem["mo_idx"], 1)
        pool.wait_ge(sg.sem["mo_idx"], 1)
        pool.indirect_dma_start(m["xg"][:], None, W["h2tok"][:, :], bass.IndirectOffsetOnAxis(m["idx"][:, 0:1], 0)).then_inc(*sg.inc("mo_x", also=[("gathered", None)], n=16))
        pool.sem_clear(sg.sem["mo_idx"])


FINAL_SIGNALS = "fi_g0 fi_g1 fi_g2 fi_g3  fi_dve fi_act fi_out fi_step"


def final_program(engine, who, sg, m, W, mo):
    if who == "sp":
        for t in range(NT):
            engine.wait_ge(*sg.event("done", t))
            engine.dma_start(W["out"][0, t * P:(t + 1) * P, :], m["ot"][:, t, :]).then_inc(sg.sem["fi_out"], 16)
        engine.wait_ge(sg.sem["fi_out"], 16 * NT)
    if who == "pool":
        for t in range(NT):
            for k in range(TOP):
                engine.indirect_dma_start(m["fy"][:, 4 * t + k, :], None, W["ybuf"][:, :],
                                                  bass.IndirectOffsetOnAxis(m["dest"][:, 4 * k + t:4 * k + t + 1], 0)).then_inc(*sg.inc(f"fi_g{t}", also=[("fy", t)], n=16))
    if who == "dve":
        v = engine

        def norm(t):
            v.wait_ge(*sg.event("root", t))
            v.reciprocal(m["fs"][:, t:t + 1], m["fs"][:, t:t + 1]).then_inc(*sg.inc("fi_step"))
            v.wait_ge(*sg.last("fi_step"))
            v.scalar_tensor_tensor(m["ot"][:, t, :], m["x2t"][:, t, :], m["fs"][:, t:t + 1], m["gf"][:], ALU.mult, ALU.mult).then_inc(*sg.inc("fi_dve", ("done", t), also=[("done", t)]))

        v.wait_ge(mo.sem["mo_gain"], 16)
        for t in range(NT):
            x = m["x2t"][:, t, :]
            v.wait_ge(*sg.event("fy", t))
            for k in range(TOP):
                ins = v.scalar_tensor_tensor(x, m["fy"][:, 4 * t + k, :], m["gates"][:, 4 * t + k:4 * t + k + 1], x, ALU.mult, ALU.add)
                if k < TOP - 1:
                    ins.then_inc(*sg.inc("fi_step"))
                    v.wait_ge(*sg.last("fi_step"))
            ins.then_inc(*sg.inc("fi_dve", ("sum", t), also=[("sum", t)]))
            if t:
                norm(t - 1)
        norm(NT - 1)
    if who == "act":
        for t in range(NT):
            engine.wait_ge(*sg.event("sum", t))
            engine.activation(m["fq"][:, t % 2, :], m["x2t"][:, t, :], ACT.Square, accum_out=m["fs"][:, t:t + 1]).then_inc(*sg.inc("fi_act", ("fsq", t), also=[("fsq", t)]))
            engine.wait_ge(*sg.event("fsq", t))
            engine.activation(m["fs"][:, t:t + 1], m["fs"][:, t:t + 1], ACT.Sqrt, bias=m["K"][:, K_E5:K_E5 + 1], scale=1.0 / D).then_inc(*sg.inc("fi_act", ("root", t), also=[("root", t)]))


SWIGLU_LIMIT, SWIGLU_ALPHA = 7.0, 1.702


def moe_tensors(at):
    at("x2t", 16, [P, NT, D])
    at("h2T", 32, [P, KD, S])
    at("sqm", 48, [P, 2, S])
    at("h2t", 48, [P, NT, D])
    at("wr", 60, [P, KD, EXPERTS])
    at("bf", 64, [96, 3 * D])
    at("br", 76, [96, 3 * D])
    at("bp", 88, [96, 3 * D], BF16)
    for base, names in ((94, (("oh", [P, TOP, P]), ("L", [P, P]), ("M", [P, P]), ("sr", [P, P]), ("pr", [P, P]), ("rk", [P, P]),
                              ("rb", [P, P]), ("i128", [P, P]), ("lt", [P, P]))),
                        (196, (("rstdm", [P, S]),)),
                        (198, (("mxm", [P, 32]), ("mi", [P, 32], U32), ("mif", [P, 32]), ("nmx", [P, 4]), ("gs", [P, 4]),
                               ("pk", [P, 16]), ("bk", [P, 16]), ("df", [P, 16]), ("dest", [P, 16], U32), ("gates", [P, 16]),
                               ("cnt", [P, 32]), ("nb", [P, 32]), ("incl", [P, 32]), ("excl", [P, 32]), ("i32", [P, 32]),
                               ("bef", [P, NB + 1]), ("bei", [1, NB + 1], I32), ("i48", [P, NB + 1]), ("brow", [1, 32]),
                               ("ohp", [P, 2, P]), ("ohb", [P, 2, NB + 1]), ("tokcol", [P, NB + 1], U32), ("idx", [P, 1], U32),
                               ("fs", [P, 4])))):
        o = base * KB
        for name, shape, *dt in names:
            at(name, o / KB, shape, *dt)
            size = 4
            for n in shape[1:]:
                size *= n
            o += (size + 31) // 32 * 32
        assert o <= {94: 100, 196: 198, 198: 202.125}[base] * KB, (base, o / KB)
    at("ring", 100, [P, MOE_SLOTS, SLOT])
    at("xg", 0, [P, D])
    at("xT", 4, [P, KD, P])
    at("hT", 8, [P, KD, P])
    at("ysb", 12, [P, D])
    for n, name in enumerate(("gc", "th", "uc", "hh")):
        at(name, 32 + 4 * n, [P, 2, S])
    at("sel", 64, [96, P], BF16)
    at("pmb", 65, [96, P], BF16)
    at("fy", 100, [P, 16, D])
    at("gf", 48, [P, D])
    at("ot", 168, [P, NT, D])
    at("fq", 184, [P, 2, D])


AS_THEY_ARE = ["x", "positions", "w_ada", "w_in", "lru_wa", "lru_wx", "w_uq", "w_ukv", "w_out", "w_ffn_in", "w_ffn_out",
               "w_in_2", "w_out_2", "pool_w_2", "w_router_2", "b_router_2", "w_gate_2", "b_gate_2", "w_up_2", "b_up_2",
               "w_down_2", "b_down_2", "normf_g_2"]


def kernel(**inputs):
    import concourse.bacc as _bacc
    from concourse.bass_utils import run_bass_kernel_spmd as _run

    arrays = {n: np.ascontiguousarray(inputs[n]) for n in AS_THEY_ARE}
    arrays["c_cols"] = columns(inputs["c"])
    arrays["vecs"] = np.stack([layer_vectors(inputs, l) for l in range(DEPTH)])
    arrays["vecs2"] = block_vectors(inputs)
    arrays["consts"], arrays["sel4"] = constants(), head_selectors()

    at = {}
    for _ in range(2):
        nc = _bacc.Bacc("TRN2", target_bir_lowering=False, num_devices=1)
        W = {n: nc.dram_tensor(n, a.shape, mybir.dt.from_np(a.dtype), kind="ExternalInput").ap() for n, a in arrays.items()}
        W["out"] = nc.dram_tensor("out", (1, S, D), F32, kind="ExternalOutput").ap()
        program(nc, W, at)
    r = _run(nc, [arrays], core_ids=[0])
    return r.results[0]["out"]
```

```python
from contextlib import ExitStack

import numpy as np
import concourse.bass as bass
from concourse import mybir

F32 = mybir.dt.float32
F32R = mybir.dt.float32r
BF16 = mybir.dt.bfloat16
I32 = mybir.dt.int32
U32 = mybir.dt.uint32
ACT = mybir.ActivationFunctionType
ALU = mybir.AluOpType
AX = mybir.AxisListType

P = 128
D = 1024
S = 512
KD = D // P
NT = S // P
DEPTH = 2
HEADS = 8
NOPE, ROPE = 128, 64
QR, KVR = 256, 128
DFF = 2816
NF = DFF // P // 2
C_Q = D
C_KV = D + QR
C_KR = C_KV + KVR
C_GA = C_KR + ROPE
C_GB = C_GA + D
KB = 1024
LRU_C = 8.0

V_BADA, V_CW, V_CB, V_BA, V_BX, V_AP, V_QG, V_KVG = 0, 48, 80, 88, 96, 104, 112, 114
NVEC = 115
K_ID, K_J2, K_ONE = 0, 128, 256
K_INVF, K_SG, K_PH, K_E6, K_E5, K_MOD = 384, 385, 386, 387, 388, 389
K_KEPT = 390
K_MASK, K_TRI, K_LT = 390, 518, 646
K_INV, K_I32, K_I48 = 774, 790, 822
K_I128 = 872
NK = 1000

RAW_SLOTS, W_SLOTS = 4, 3
ADA_CHUNKS = 6 * D // 256
ADA_SLOTS = 8
SLOT = 2048


class Signals:

    def __init__(self, nc, ctx, names, at):
        self.sem = {n: ctx.enter_context(nc.semaphore(n)) for n in names.split()}
        self.count = {n: 0 for n in self.sem}
        self.at, self.known = at, dict(at)

    def inc(self, name, number=None, also=(), n=1):
        self.count[name] += n
        for key in [(name, number), *also]:
            self.at[key] = (name, self.count[name])
        return self.sem[name], n

    def event(self, name, number=None):
        sem, value = self.known[name, number] if self.known else (next(iter(self.sem)), 1)
        return self.sem[sem], value

    def last(self, name):
        return self.sem[name], self.count[name]


def layer_chunks():
    out = [("lru", i, True) for i in range(4)]
    out += [("q", 0, True), ("kv", 0, True)]
    out += [("ga", i, True) for i in range(4)] + [("gb", i, True) for i in range(4)]
    out += [("uq", 0, True), ("uq", 1, True), ("ukv", 0, True)]
    out += [("out", i, True) for i in range(4)]
    ada = iter(range(ADA_CHUNKS))
    for half in range(2):
        for j in range(NF):
            out += [("fi", half * NF + j, True)] + ([("ada", next(ada), False)] if j else [])
        for j in range(KD):
            out += [("fo", half * KD + j, True)] + ([("ada", next(ada), False)] if j % 2 and half == 0 else [])
    assert next(ada, None) is None
    return out


CHUNKS = layer_chunks()
W_CHUNKS = [c for c in CHUNKS if c[2]]
ADA_AFTER = {c[:2]: CHUNKS[n + 1][1] for n, c in enumerate(CHUNKS[:-1]) if not CHUNKS[n + 1][2]}
W_INDEX = {(k, i): n for n, (k, i, _) in enumerate(W_CHUNKS)}
POSITION = {(k, i): n for n, (k, i, _) in enumerate(CHUNKS)}
GROUPS_OF = {"lru": 2, "q": 2, "kv": 2, "ga": 2, "gb": 2, "uq": 0, "ukv": 8, "out": 2, "fi": 2, "fo": 1}


def first_groups():
    first, g = {}, 0
    for kind, i, _ in W_CHUNKS:
        first[kind, i] = g
        g += GROUPS_OF[kind]
    return first


FIRST_GROUP = first_groups()
P_AT = [0, 128, 384, 768]
T_AT = [0, 512, 896, 1152]


def split3(pe, out, lhi, llo, rhi, rlo, start, stop):
    pe.matmul(out, lhi, rhi, start=start, stop=False)
    pe.matmul(out, lhi, rlo, start=False, stop=False)
    return pe.matmul(out, llo, rhi, start=False, stop=stop)

def log1p(v, sg, sem, out, u, s, p):
    v.tensor_scalar(s, u, 2.0, None, ALU.add).then_inc(*sg.inc(sem))
    v.wait_ge(*sg.last(sem))
    v.reciprocal(s, s).then_inc(*sg.inc(sem))
    v.wait_ge(*sg.last(sem))
    v.tensor_tensor(s, s, u, ALU.mult).then_inc(*sg.inc(sem))
    v.wait_ge(*sg.last(sem))
    v.tensor_tensor(p, s, s, ALU.mult).then_inc(*sg.inc(sem))
    v.wait_ge(*sg.last(sem))
    v.tensor_scalar(out, p, 1.0 / 17, 1.0 / 15, ALU.mult, ALU.add).then_inc(*sg.inc(sem))
    v.wait_ge(*sg.last(sem))
    for n in (13, 11, 9, 7, 5, 3, 1):
        v.tensor_tensor(out, out, p, ALU.mult).then_inc(*sg.inc(sem))
        v.wait_ge(*sg.last(sem))
        v.tensor_scalar(out, out, 1.0 / n, None, ALU.add).then_inc(*sg.inc(sem))
        v.wait_ge(*sg.last(sem))
    v.scalar_tensor_tensor(out, out, 2.0, s, ALU.mult, ALU.mult).then_inc(*sg.inc(sem))
    v.wait_ge(*sg.last(sem))


LAYER_SIGNALS = """step_act step_dve raw_in0 raw_in1 raw_in2 raw_in3 vec_in lruw_in raw_used w_hi pe_step
    act_free dve_free act_out dve_out act_sq act_root act_hi dve_h dve_lo act_exp act_pt act_qk
    dve_max dve_p dve_qa dve_pt dve_y ada_out"""


def layer_loads(sp, l, sg, m, W):
    sp.dma_start(m["vec"][:], W["vecs"][l]).then_inc(*sg.inc("vec_in", n=16))
    by_k = lambda name: W[name][l].rearrange("(k p) n -> p k n", p=P)
    w_in, w_out = by_k("w_in"), by_k("w_out")
    w_fi, w_fo = by_k("w_ffn_in"), by_k("w_ffn_out")
    w_uq = W["w_uq"][l].rearrange("(k p) h d -> p k h d", p=P)
    w_ukv = W["w_ukv"][l]
    h = ROPE // 2
    for n, (kind, i, _) in enumerate(CHUNKS):
        slot = n % RAW_SLOTS
        if n == 2:
            for j, name in enumerate(("lru_wa", "lru_wx")):
                sp.dma_start(m["lruw"][:, 8 * j:8 * j + 8, :],
                             W[name][l].rearrange("g i j -> i g j")).then_inc(*sg.inc("lruw_in", j, n=16))
        if n >= RAW_SLOTS:
            sp.wait_ge(*sg.event("raw_used", n - RAW_SLOTS))
        raw = m["RAW"][:, slot, :]
        by256 = raw.rearrange("p (k n) -> p k n", k=KD)
        if kind == "ada":
            with sp.If(l < DEPTH - 1):
                w_ada = W["w_ada"][(l + 1) % DEPTH].rearrange("(k p) n -> p k n", p=P)
                sp.dma_start(by256, w_ada[:, :, i * 256:(i + 1) * 256]).then_inc(*sg.inc(f"raw_in{slot}", also=[("raw", n)], n=16))
            with sp.If(l >= DEPTH - 1):
                sp.wait_ge(*sg.event("raw_used", n - RAW_SLOTS)).then_inc(sg.sem[f"raw_in{slot}"], 16)
            continue
        if kind in ("lru", "q", "ga", "gb"):
            c = {"lru": 0, "q": C_Q, "ga": C_GA, "gb": C_GB}[kind] + i * 256
            parts = [(by256, w_in[:, :, c:c + 256])]
        elif kind == "kv":
            parts = [(by256[:, :, 0:192], w_in[:, :, C_KV:C_KV + 192]),
                     (by256[:, :, 192:192 + h], w_in[:, :, C_KR + h:C_KR + ROPE]),
                     (by256[:, :, 192 + h:256], w_in[:, :, C_KR:C_KR + h])]
        elif kind == "uq":
            parts = []
            for k in range(2):
                dst = raw[:, k * 1024:(k + 1) * 1024].rearrange("p (h n) -> p h n", h=4)
                src = w_uq[:, k, 4 * i:4 * i + 4, :]
                parts += [(dst[:, :, 0:192], src), (dst[:, :, 192:192 + h], src[:, :, 160:192]),
                          (dst[:, :, 192 + h:256], src[:, :, 128:160])]
        elif kind == "ukv":
            parts = [(raw[:, 0:1024].rearrange("p (h n) -> p h n", h=HEADS), w_ukv[:, :, 0:128]),
                     (raw[:, 1024:2048].rearrange("p (h n) -> p h n", h=HEADS), w_ukv[:, :, 128:256])]
        elif kind == "out":
            parts = [(by256, w_out[:, :, i * 256:(i + 1) * 256])]
        elif kind == "fi":
            parts = [(by256[:, :, 0:128], w_fi[:, :, i * P:(i + 1) * P]),
                     (by256[:, :, 128:256], w_fi[:, :, DFF + i * P:DFF + (i + 1) * P])]
        else:
            half, j = divmod(i, KD)
            parts = [(raw[:, 0:NF * P].rearrange("p (k n) -> p k n", k=NF),
                      w_fo[:, half * NF:(half + 1) * NF, j * P:(j + 1) * P])]
        for dst, src in parts:
            sp.dma_start(dst, src).then_inc(*sg.inc(f"raw_in{slot}", also=[("raw", n)], n=16))


def score_bank(b, q):
    w = (q + 1) * P
    return {3: b[0][:, 0:w], 2: b[1][:, 0:w], 0: b[1][:, 384:512], 1: b[2][:, 0:w]}[q]


Q_ORDER = (1, 0, 2, 3)
FLOATS = {"fo": NF * P}
SCALE = (NOPE + ROPE) ** -0.5


def layer_act(act, sg, m, b):
    K, X, HH = m["K"], m["X"], m["HH"]

    fed = [0]

    def feed(upto):
        while fed[0] <= min(upto, len(W_CHUNKS) - 1):
            n = fed[0]
            kind, i, _ = W_CHUNKS[n]
            c, size = POSITION[kind, i], FLOATS.get(kind, SLOT)
            act.wait_ge(*sg.event("raw", c))
            if n >= W_SLOTS:
                act.wait_ge(*sg.event("w_used", n - W_SLOTS))
            act.activation(m["WHI"][:, n % W_SLOTS, 0:size], m["RAW"][:, c % RAW_SLOTS, 0:size], ACT.Copy).then_inc(*sg.inc("w_hi", n))
            fed[0] += 1

    def square(t, k):
        if (t, k) >= (0, 2):
            act.wait_ge(*sg.event("sq_used", (t, k - 2) if k >= 2 else (t - 1, KD - 2 + k)))
        act.activation(m["sq"][:, k % 2, :], X[:, k, :], ACT.Square).then_inc(*sg.inc("act_sq", (t, k)))

    def norm(t, eps):
        act.wait_ge(*sg.event("stat", t))
        act.activation(m["rstd"][:], b[4][:], ACT.Sqrt, bias=K[:, eps:eps + 1], scale=1.0 / D).then_inc(*sg.inc("act_root", t))
        scale, shift = (8, 0) if t == 0 else (32, 24)
        act.wait_ge(*sg.event("ada_out"))
        for k in range(KD):
            act.wait_ge(*sg.event("dve_h", ("n", t, k)))
            if k >= 2:
                act.wait_ge(*sg.event("hl", (t, k - 2)))
            h = dict(scale=m["mod"][:, scale + k:scale + k + 1], bias=m["mod"][:, shift + k:shift + k + 1])
            act.activation(m["nh"][:, k % 2, :], m["nt"][:, k % 2, :], ACT.Identity, **h)
            act.activation(HH[:, k, :], m["nt"][:, k % 2, :], ACT.Identity, **h).then_inc(*sg.inc("act_hi", ("h", t, k)))

    for k in range(KD):
        square(0, k)
    feed(1)
    norm(0, K_E6)
    act.wait_ge(*sg.event("absa"))
    act.activation(m["sm"][:, 8:16], m["sm"][:, 0:8], ACT.Exp, scale=-1.0).then_inc(*sg.inc("act_out", "expa"))

    def lru_tail(i):
        act.wait_ge(*sg.event("gate_pre", i))
        if i:
            act.wait_ge(*sg.event("lru_done", i - 1))
        act.wait_ge(*sg.event("hb"))
        hb = m["hb"]
        for n in range(2):
            blk = 2 * i + n
            act.activation(m["tr"][:, n, :], b[4 + 2 * n][:], ACT.Tanh, scale=0.5, bias=hb[:, blk:blk + 1])
            ins = act.activation(m["ti"][:, n, :], b[5 + 2 * n][:], ACT.Tanh, scale=0.5, bias=hb[:, 8 + blk:9 + blk])
        ins.then_inc(*sg.inc("act_out", ("lru_tanh", i)))
        act.wait_ge(*sg.event("act_out", ("lru_tanh", i)))
        for n in range(2):
            r = hb[:, 16 + 2 * i + n:17 + 2 * i + n]
            ins = act.activation(m["la"][:, n, :], m["tr"][:, n, :], ACT.Exp, scale=r, bias=r)
        ins.then_inc(*sg.inc("step_act"))
        act.wait_ge(*sg.last("step_act"))
        for n in range(2):
            r = hb[:, 24 + 2 * i + n:25 + 2 * i + n]
            act.activation(m["tr"][:, n, :], m["tr"][:, n, :], ACT.Tanh, scale=r, bias=r)
            ins = act.activation(m["sq2"][:, n, :], m["la"][:, n, :], ACT.Square)
        ins.then_inc(*sg.inc("act_out", ("lru_square", i)))
        act.wait_ge(*sg.event("lru_var", i))
        for n in range(2):
            ins = act.activation(m["tr"][:, n, :], m["tr"][:, n, :], ACT.Sqrt)
        ins.then_inc(*sg.inc("act_out", ("lru_root", i)))

    for n, (kind, i, _) in enumerate(W_CHUNKS):
        if kind == "uq":
            break
        feed(n + 2)
        g = FIRST_GROUP[kind, i]
        if kind == "lru":
            for j in range(2):
                act.wait_ge(*sg.event("acc", g + j))
                if i:
                    act.wait_ge(*sg.event("xc", 2 * i + j - 2))
                act.activation(m["xpad"][:, j, 3:3 + S], b[(g + j) % 4][:], ACT.Copy).then_inc(*sg.inc("act_free", g + j, also=[("free", g + j)]))
            if i:
                lru_tail(i - 1)
        elif kind == "q":
            for j in range(2):
                act.wait_ge(*sg.event("acc", g + j))
                act.activation(m["qraw"][:, j, :], b[(g + j) % 4][:], ACT.Copy).then_inc(*sg.inc("act_free", g + j, also=[("free", g + j)]))
            lru_tail(3)
        elif kind == "kv":
            act.wait_ge(*sg.event("acc", g))
            act.activation(m["kvraw"][:], b[g % 4][:], ACT.Copy).then_inc(*sg.inc("act_free", g, also=[("free", g)]))
            act.wait_ge(*sg.event("act_free", g))
            act.wait_ge(*sg.event("lru_done", 3))
            for j in range(2):
                act.activation(m["sq2"][:, j, :], m["qraw"][:, j, :], ACT.Square)
            act.activation(m["ti"][:, 0, :], m["kvraw"][:], ACT.Square).then_inc(*sg.inc("act_sq", "qkv"))
        elif kind == "ga":
            for j in range(2):
                act.wait_ge(*sg.event("acc", g + j))
                if i:
                    act.wait_ge(*sg.event("ga_used", 2 * i + j - 2))
                act.activation(m["tg"][:, j, :], b[(g + j) % 4][:], ACT.Tanh, scale=0.5).then_inc(*sg.inc("act_free", g + j, also=[("free", g + j)]))
            if i == 1:
                act.wait_ge(*sg.event("stat", "qkv"))
                act.activation(m["rq"][:, 0, :], b[4][:], ACT.Sqrt, bias=K[:, K_E6:K_E6 + 1], scale=1.0 / QR)
                act.activation(m["rq"][:, 1, :], b[5][:], ACT.Sqrt, bias=K[:, K_E6:K_E6 + 1], scale=1.0 / KVR).then_inc(*sg.inc("act_root", "qkv"))
                act.wait_ge(*sg.event("cq"))
                act.activation(m["cqh"][:], m["qraw"][:], ACT.Copy)
                act.activation(m["ckvh"][:], m["kvraw"][:], ACT.Copy).then_inc(*sg.inc("act_hi", "cq"))
        elif kind == "gb":
            act.wait_ge(*sg.event("gate_pre", 3))
            for j in range(2):
                act.wait_ge(*sg.event("acc", g + j))
                act.activation(m["tgb"][:, 2 * i + j, :], b[(g + j) % 4][:], ACT.Tanh, scale=0.5).then_inc(*sg.inc("act_free", g + j, also=[("free", g + j)]))

    feed(W_INDEX["ukv", 0])
    g = FIRST_GROUP["ukv", 0]
    for j in range(8):
        act.wait_ge(*sg.event("acc", g + j))
        act.activation(m["V"][:, j // 2, (j % 2) * 512:(j % 2 + 1) * 512], b[(g + j) % 4][:], ACT.Copy).then_inc(*sg.inc("act_free", g + j, also=[("free", g + j)]))

    def rounded(h):
        act.wait_ge(*sg.event("y", h))
        act.activation(m["yh"][:, h, :], m["ya"][:, h, :], ACT.Copy).then_inc(*sg.inc("act_hi", ("y", h)))

    for h in range(-2, HEADS):
        if 0 <= h + 1 < HEADS:
            for q in Q_ORDER:
                n, w = 4 * (h + 1) + q, (q + 1) * P
                act.wait_ge(*sg.event("max", n))
                if h >= 1:
                    act.wait_ge(*sg.event("t", (h - 1, 3)))
                act.activation(m["P2"][:, (h + 1) % 2, P_AT[q]:P_AT[q] + w], score_bank(b, q), ACT.Exp,
                                       bias=m["nm"][:, n % 8:n % 8 + 1], scale=SCALE,
                                       accum_out=m["sum"][:, n % 8:n % 8 + 1]).then_inc(*sg.inc("act_exp", n))
        if h + 2 < HEADS:
            a = h + 2
            act.wait_ge(*sg.event("qn_acc", a))
            if a >= 2:
                act.wait_ge(*sg.event("s", 4 * (a - 2) + 3))
            act.activation(m["qn"][:, a % 2, :], b[3][:], ACT.Copy).then_inc(*sg.inc("act_qk", ("qn", a)))
            act.wait_ge(*sg.event("kn_acc", a))
            act.activation(m["kn"][:, a % 2, :], b[3][:], ACT.Copy).then_inc(*sg.inc("act_qk", ("kn", a)))
        if h >= 0:
            for kb in (0, 1):
                w = (4 - kb) * P
                act.wait_ge(*sg.event("t", (h, kb)))
                if h:
                    act.wait_ge(*sg.event("o", h - 1))
                act.activation(m["PT"][:, T_AT[kb]:T_AT[kb] + w], b[5 + kb % 2][:, 0:w], ACT.Copy).then_inc(*sg.inc("act_pt", (h, kb), also=[("pt", (h, kb))]))
            if h:
                rounded(h - 1)
            if h >= 6:
                feed(W_INDEX["out", h - 6])
    rounded(HEADS - 1)
    for i in range(4):
        feed(W_INDEX["out", i] + 2)
        for j in range(2):
            act.wait_ge(*sg.event("dve_free", FIRST_GROUP["out", i] + j))
            square(1, 2 * i + j)
    norm(1, K_E6)
    for q in range(2 * NF):
        half, j = divmod(q, NF)
        feed(W_INDEX["fi", q] + 2)
        g = FIRST_GROUP["fi", q]
        act.wait_ge(*sg.event("acc", g))
        if q >= 2:
            act.wait_ge(*sg.event("ff_hid", q - 2))
        act.activation(m["fth"][:, q % 2, :], b[g % 4][:], ACT.Tanh, scale=0.5).then_inc(*sg.inc("act_out", ("ff_tanh", q)))
        act.wait_ge(*sg.event("ff_hid", q))
        act.activation(m["hidh"][:, j, :], m["fh"][:, q % 2, :], ACT.Copy).then_inc(*sg.inc("act_hi", ("ff", q)))
        if j == NF - 1:
            for jj in range(KD):
                feed(W_INDEX["fo", half * KD + jj] + 2)


def layer_dve(v, sg, m, b):
    f = lambda t: t.bitcast(F32)
    K, X, HH, HL, vec, mod = m["K"], m["X"], m["HH"], m["HL"], m["vec"], m["mod"]

    fed, nw = [0], [0]

    def ada():
        c, i = fed[0], CHUNKS[fed[0]][1]
        v.wait_ge(*sg.event("raw", c))
        if i >= 2:
            v.wait_ge(*sg.event("ada_col", i - 2))
        acc, raw = m["acc"][:, i % 2, :], m["RAW"][:, c % RAW_SLOTS, :]
        v.tensor_scalar(acc, raw[:, 0:256], m["c"][:, 0:1], None, ALU.mult).then_inc(*sg.inc("step_dve"))
        v.wait_ge(*sg.last("step_dve"))
        for k in range(1, KD):
            ins = v.scalar_tensor_tensor(acc, raw[:, k * 256:(k + 1) * 256], m["c"][:, k:k + 1], acc, ALU.mult, ALU.add)
            if k < KD - 1:
                ins.then_inc(*sg.inc("step_dve"))
                v.wait_ge(*sg.last("step_dve"))
        ins.then_inc(*sg.inc("raw_used", c, also=[("ada_acc", i)]))
        fed[0] += 1

    def feed(upto):
        while nw[0] <= min(upto, len(W_CHUNKS) - 1):
            if not CHUNKS[fed[0]][2]:
                ada()
                continue
            n, c = nw[0], fed[0]
            size = FLOATS.get(W_CHUNKS[n][0], SLOT)
            v.wait_ge(*sg.event("w_hi", n))
            v.tensor_tensor(m["WLO"][:, n % W_SLOTS, 0:size], m["RAW"][:, c % RAW_SLOTS, 0:size],
                                    f(m["WHI"])[:, n % W_SLOTS, 0:size], ALU.subtract).then_inc(*sg.inc("raw_used", c, also=[("w", n)]))
            nw[0] += 1
            fed[0] += 1

    def norm(t):
        v.wait_ge(*sg.event("act_root", t))
        v.reciprocal(m["rstd"][:], m["rstd"][:]).then_inc(*sg.inc("step_dve"))
        v.wait_ge(*sg.last("step_dve"))
        for k in range(KD + 1):
            if k < KD:
                if k >= 2:
                    v.wait_ge(*sg.event("act_hi", ("h", t, k - 2)))
                v.tensor_tensor(m["nt"][:, k % 2, :], X[:, k, :], m["rstd"][:], ALU.mult).then_inc(*sg.inc("dve_h", ("n", t, k)))
            if k:
                v.wait_ge(*sg.event("act_hi", ("h", t, k - 1)))
                v.tensor_tensor(HL[:, k - 1, :], m["nh"][:, (k - 1) % 2, :], f(HH)[:, k - 1, :],
                                ALU.subtract).then_inc(*sg.inc("dve_lo", ("h", t, k - 1), also=[("hl", (t, k - 1))]))

    v.wait_ge(*sg.event("vec_in"))
    v.tensor_tensor(mod[:], mod[:], vec[:, V_BADA:V_BADA + 48], ALU.add).then_inc(*sg.inc("step_dve"))
    v.wait_ge(*sg.last("step_dve"))
    v.tensor_scalar(mod[:, 8:16], mod[:, 8:16], 1.0, None, ALU.add)
    v.tensor_scalar(mod[:, 16:24], mod[:, 16:24], 0.5, None, ALU.mult)
    v.tensor_scalar(mod[:, 32:40], mod[:, 32:40], 1.0, None, ALU.add).then_inc(*sg.inc("ada_out"))
    v.wait_ge(*sg.event("ada_out"))
    feed(1)
    norm(0)
    sm, hb = m["sm"], m["hb"]
    v.tensor_scalar(hb[:, 0:16], vec[:, V_BA:V_BA + 16], 0.5, None, ALU.mult).then_inc(*sg.inc("step_dve"))
    v.wait_ge(*sg.last("step_dve"))
    ap = vec[:, V_AP:V_AP + 8]
    v.tensor_scalar(sm[:, 16:24], ap, -1.0, None, ALU.mult).then_inc(*sg.inc("step_dve"))
    v.wait_ge(*sg.last("step_dve"))
    v.tensor_tensor(sm[:, 0:8], ap, sm[:, 16:24], ALU.max).then_inc(*sg.inc("dve_out", "absa", also=[("absa", None)]))
    v.wait_ge(*sg.event("act_out", "expa"))
    log1p(v, sg, "step_dve", sm[:, 24:32], sm[:, 8:16], sm[:, 32:40], sm[:, 40:48])
    v.tensor_scalar(sm[:, 16:24], sm[:, 16:24], 0.0, None, ALU.max).then_inc(*sg.inc("step_dve"))
    v.wait_ge(*sg.last("step_dve"))
    v.tensor_tensor(sm[:, 24:32], sm[:, 24:32], sm[:, 16:24], ALU.add).then_inc(*sg.inc("step_dve"))
    v.wait_ge(*sg.last("step_dve"))
    v.tensor_scalar(hb[:, 16:24], sm[:, 24:32], -LRU_C / 2, None, ALU.mult)
    v.tensor_scalar(hb[:, 24:32], sm[:, 24:32], LRU_C / 2, None, ALU.mult).then_inc(*sg.inc("dve_out", "hb", also=[("hb", None)]))

    def lru_head(i):
        g = FIRST_GROUP["lru", i]
        for j in range(2):
            blk = 2 * i + j
            xc, pad = m["xc"][:, blk % 4, :], m["xpad"][:, j, :]
            cw = lambda t: vec[:, V_CW + 8 * t + blk:V_CW + 8 * t + blk + 1]
            v.wait_ge(*sg.event("act_free", g + j))
            if blk >= 4:
                v.wait_ge(*sg.event("gate_pre", i - 2))
            v.tensor_scalar(xc, pad[:, 0:S], cw(0), vec[:, V_CB + blk:V_CB + blk + 1], ALU.mult, ALU.add).then_inc(*sg.inc("step_dve"))
            v.wait_ge(*sg.last("step_dve"))
            v.scalar_tensor_tensor(xc, pad[:, 1:1 + S], cw(1), xc, ALU.mult, ALU.add).then_inc(*sg.inc("step_dve"))
            v.wait_ge(*sg.last("step_dve"))
            v.scalar_tensor_tensor(xc, pad[:, 2:2 + S], cw(2), xc, ALU.mult, ALU.add).then_inc(*sg.inc("step_dve"))
            v.wait_ge(*sg.last("step_dve"))
            v.scalar_tensor_tensor(xc, pad[:, 3:3 + S], cw(3), xc, ALU.mult, ALU.add).then_inc(*sg.inc("dve_out", ("xc", blk), also=[("xc", blk)]))

    def lru_tail(i):
        tr, ti, la, sq2, rs = m["tr"], m["ti"], m["la"], m["sq2"], m["rs"]
        v.wait_ge(*sg.event("act_out", ("lru_square", i)))
        for n in range(2):
            v.scalar_tensor_tensor(tr[:, n, :], sq2[:, n, :], 1.0, tr[:, n, :], ALU.add, ALU.mult).then_inc(*sg.inc("step_dve"))
            v.wait_ge(*sg.last("step_dve"))
            ins = v.tensor_tensor(tr[:, n, :], tr[:, n, :], rs[:], ALU.max)
        ins.then_inc(*sg.inc("dve_out", ("lru_var", i), also=[("lru_var", i)]))
        v.wait_ge(*sg.event("dve_out", ("xc", 2 * i + 1)))
        for n in range(2):
            v.scalar_tensor_tensor(ti[:, n, :], ti[:, n, :], 1.0, m["xc"][:, (2 * i + n) % 4, :], ALU.add, ALU.mult)
            ins = v.scalar_tensor_tensor(la[:, n, :], rs[:], 0.0, la[:, n, :], ALU.is_equal, ALU.mult)
        ins.then_inc(*sg.inc("step_dve"))
        v.wait_ge(*sg.last("step_dve"))
        v.wait_ge(*sg.event("act_out", ("lru_root", i)))
        for n in range(2):
            v.scalar_tensor_tensor(ti[:, n, :], ti[:, n, :], 0.5, tr[:, n, :], ALU.mult, ALU.mult).then_inc(*sg.inc("step_dve"))
            v.wait_ge(*sg.last("step_dve"))
            ins = v.tensor_tensor_scan(m["ya"][:, 2 * i + n, :], la[:, n, :], ti[:, n, :], 0.0, ALU.mult, ALU.add)
        ins.then_inc(*sg.inc("dve_out", ("lru_done", i), also=[("lru_done", i)]))

    for n, (kind, i, _) in enumerate(W_CHUNKS):
        if kind == "uq":
            break
        feed(n + 2)
        g = FIRST_GROUP[kind, i]
        if kind == "lru":
            lru_head(i)
            if i:
                lru_tail(i - 1)
        elif kind == "q":
            lru_tail(3)
            v.wait_ge(*sg.event("lru_done", 3))
        elif kind == "kv":
            v.wait_ge(*sg.event("acc", g + 1))
            v.tensor_tensor(m["Ak"][:], b[(g + 1) % 4][:], m["T"][:], ALU.mult).then_inc(*sg.inc("dve_free", g + 1, also=[("free", g + 1), ("ak", None)]))
        elif kind == "ga":
            for j in range(2):
                blk = 2 * i + j
                v.wait_ge(*sg.event("act_free", g + j))
                v.scalar_tensor_tensor(m["ya"][:, blk, :], m["tg"][:, j, :], 1.0, m["ya"][:, blk, :], ALU.add, ALU.mult).then_inc(*sg.inc("dve_out", ("ga", blk), also=[("ga_used", blk)]))
            if i == 1:
                v.wait_ge(*sg.event("act_root", "qkv"))
                v.reciprocal(m["rq"][:], m["rq"][:]).then_inc(*sg.inc("step_dve"))
                v.wait_ge(*sg.last("step_dve"))
                for j in range(2):
                    v.scalar_tensor_tensor(m["qraw"][:, j, :], m["qraw"][:, j, :], vec[:, V_QG + j:V_QG + j + 1],
                                           m["rq"][:, 0, :], ALU.mult, ALU.mult)
                v.scalar_tensor_tensor(m["kvraw"][:], m["kvraw"][:], vec[:, V_KVG:V_KVG + 1], m["rq"][:, 1, :],
                                               ALU.mult, ALU.mult).then_inc(*sg.inc("dve_out", "cq", also=[("cq", None)]))
                v.wait_ge(*sg.event("cq"))
                v.wait_ge(*sg.event("act_hi", "cq"))
                v.tensor_tensor(m["cql"][:], m["qraw"][:], f(m["cqh"])[:], ALU.subtract)
                v.tensor_tensor(m["ckvl"][:], m["kvraw"][:], f(m["ckvh"])[:], ALU.subtract).then_inc(*sg.inc("dve_lo", "cq", also=[("cql", None)]))
            if i == 3:
                v.wait_ge(*sg.event("kp_acc"))
                v.tensor_copy(m["Kp"][:], b[6][:]).then_inc(*sg.inc("dve_out", "kp", also=[("kp", None)]))

    feed(W_INDEX["ukv", 0])
    v.wait_ge(*sg.event("ga_used", 2 * 3 + 1))
    def low_y(h):
        v.wait_ge(*sg.event("act_hi", ("y", h)))
        v.tensor_tensor(m["yl"][:, h, :], m["ya"][:, h, :], f(m["yh"])[:, h, :], ALU.subtract).then_inc(*sg.inc("dve_lo", ("y", h), also=[("yl", h)]))

    for h in range(-2, HEADS):
        if 0 <= h + 1 < HEADS:
            for q in Q_ORDER:
                n = 4 * (h + 1) + q
                one = lambda t: m[t][:, n % 8:n % 8 + 1]
                v.wait_ge(*sg.event("s", n))
                if n >= 8:
                    v.wait_ge(*sg.event("act_exp", n - 8))
                v.tensor_reduce(one("mx"), score_bank(b, q), AX.X, ALU.max).then_inc(*sg.inc("step_dve"))
                v.wait_ge(*sg.last("step_dve"))
                v.tensor_scalar(one("nm"), one("mx"), -SCALE, None, ALU.mult).then_inc(*sg.inc("dve_max", n, also=[("max", n)] + [("max", n - 2)] * (q == 2)))
        if h + 2 < HEADS:
            a = h + 2
            v.wait_ge(*sg.event("qr_acc", a))
            if a >= 2:
                v.wait_ge(*sg.event("s", 4 * (a - 2) + 3))
            v.tensor_tensor(m["qa"][:, a % 2, :], b[4][:], m["T"][:], ALU.mult).then_inc(*sg.inc("dve_qa", a, also=[("qa", a)]))
        if 0 <= h + 1 < HEADS:
            for q in Q_ORDER:
                n, w = 4 * (h + 1) + q, (q + 1) * P
                one = lambda t: m[t][:, n % 8:n % 8 + 1]
                v.wait_ge(*sg.event("act_exp", n))
                v.reciprocal(one("rec"), one("sum")).then_inc(*sg.inc("step_dve"))
                v.wait_ge(*sg.last("step_dve"))
                pp = m["P2"][:, (h + 1) % 2, P_AT[q]:P_AT[q] + w]
                v.tensor_scalar(pp, pp, one("rec"), None, ALU.mult).then_inc(*sg.inc("dve_p", n, also=[("p", n)]))
        if h >= 0:
            for kb in (2, 3):
                w = (4 - kb) * P
                v.wait_ge(*sg.event("t", (h, kb)))
                if h:
                    v.wait_ge(*sg.event("o", h - 1))
                v.tensor_copy(m["PT"][:, T_AT[kb]:T_AT[kb] + w], b[5 + kb % 2][:, 0:w]).then_inc(*sg.inc("dve_pt", (h, kb), also=[("pt", (h, kb))]))
            if h:
                low_y(h - 1)
            if h >= 6:
                feed(W_INDEX["out", h - 6])
            v.wait_ge(*sg.event("o", h))
            v.scalar_tensor_tensor(m["to"][:], m["tgb"][:, h, :], 1.0, b[7][:], ALU.add, ALU.mult).then_inc(*sg.inc("step_dve"))
            v.wait_ge(*sg.last("step_dve"))
            v.tensor_tensor(m["ya"][:, h, :], m["ya"][:, h, :], m["to"][:], ALU.add).then_inc(*sg.inc("dve_y", h, also=[("y", h)]))
    low_y(HEADS - 1)

    def residual(kind, i, count, gain, also=()):
        g = FIRST_GROUP[kind, i]
        for j in range(count):
            k = (i * count + j) % KD
            v.wait_ge(*sg.event("acc", g + j))
            v.scalar_tensor_tensor(X[:, k, :], b[(g + j) % 4][:], mod[:, gain + k:gain + k + 1], X[:, k, :],
                                           ALU.mult, ALU.add).then_inc(*sg.inc("dve_free", g + j, also=[("free", g + j), *also]))

    for i in range(4):
        feed(W_INDEX["out", i] + 2)
        residual("out", i, 2, 16, [("x", None)])
    norm(1)
    for q in range(2 * NF):
        half, j = divmod(q, NF)
        feed(W_INDEX["fi", q] + 2)
        g, fh = FIRST_GROUP["fi", q], m["fh"][:, q % 2, :]
        v.wait_ge(*sg.event("act_out", ("ff_tanh", q)))
        v.wait_ge(*sg.event("acc", g + 1))
        if q >= 2:
            v.wait_ge(*sg.event("act_hi", ("ff", q - 2)))
            v.wait_ge(*sg.event("ffl", q - 2))
        v.scalar_tensor_tensor(fh, m["fth"][:, q % 2, :], 1.0, b[g % 4][:], ALU.add, ALU.mult).then_inc(*sg.inc("dve_free", g, also=[("free", g)]))
        v.wait_ge(*sg.event("dve_free", g))
        v.scalar_tensor_tensor(fh, fh, 0.5, b[(g + 1) % 4][:], ALU.mult, ALU.mult).then_inc(*sg.inc("dve_free", g + 1, also=[("free", g + 1), ("ff_hid", q)]))
        v.wait_ge(*sg.event("dve_free", g + 1))
        v.wait_ge(*sg.event("act_hi", ("ff", q)))
        v.tensor_tensor(m["hidl"][:, j, :], fh, f(m["hidh"])[:, j, :], ALU.subtract).then_inc(*sg.inc("dve_lo", ("ff", q), also=[("ffl", q)]))
        if j == NF - 1:
            for jj in range(KD):
                feed(W_INDEX["fo", half * KD + jj] + 2)
                if half:
                    v.wait_ge(*sg.event("dve_free", FIRST_GROUP["fo", jj]))
                residual("fo", half * KD + jj, 1, 40)
    v.wait_ge(*sg.event("dve_free", FIRST_GROUP["fo", 2 * KD - 1]))
    v.wait_ge(*sg.event("ada_col", ADA_CHUNKS - 1))
    v.tensor_copy(mod[:], b[6][:, 0:48]).then_inc(*sg.inc("step_dve"))


def layer_pe(pe, sg, m, b):
    K, HH, HL = m["K"], m["HH"], m["HL"]
    one = K[:, K_ONE:K_ONE + P]

    def bank(g):
        if g >= 4:
            pe.wait_ge(*sg.event("free", g - 4))
        return b[g % 4]

    def weights(n):
        pe.wait_ge(*sg.event("w", n))
        return m["WHI"][:, n % W_SLOTS, :], m["WLO"][:, n % W_SLOTS, :]

    def stat(t, blocks):
        for k in blocks:
            pe.wait_ge(*sg.event("act_sq", (t, k)))
            ins = pe.matmul(b[4][:], one, m["sq"][:, k % 2, :], start=(k == 0), stop=(k == KD - 1))
            ins.then_inc(*sg.inc("pe_step", also=[("sq_used", (t, k)), *([("stat", t)] if k == KD - 1 else [])]))

    def ada_columns(i):
        pe.wait_ge(*sg.event("ada_acc", i))
        for j in range(2):
            c = 2 * i + j
            ins = pe.matmul(b[6][:, c:c + 1], m["acc"][:, i % 2, j * P:(j + 1) * P], one[:, 0:1], start=True, stop=True)
        ins.then_inc(*sg.inc("pe_step", also=[("ada_col", i)]))

    def dense(kind, i, xh=HH, xl=HL, norm=None):
        n, g = W_INDEX[kind, i], FIRST_GROUP[kind, i]
        hi, lo = weights(n)
        for j in range(2):
            out = bank(g + j)
            for k in range(KD):
                c = k * 256 + j * P
                if norm is not None and j == 0:
                    pe.wait_ge(*sg.event("hl", (norm, k)))
                ins = split3(pe, out[:], hi[:, c:c + P], lo[:, c:c + P], xh[:, k, :], xl[:, k, :], k == 0, k == KD - 1)
            ins.then_inc(*sg.inc("pe_step", also=[("acc", g + j), *([("w_used", n)] if j else [])]))

    def gates(i):
        pe.wait_ge(*sg.event("lruw_in", 1))
        if i:
            pe.wait_ge(*sg.event("act_out", ("lru_tanh", i - 1)))
        for n in range(2):
            blk = 2 * i + n
            pe.wait_ge(*sg.event("xc", blk))
            for g in range(2):
                ins = pe.matmul(b[4 + 2 * n + g][:], m["lruw"][:, 8 * g + blk, :], m["xc"][:, blk % 4, :], start=True, stop=True)
        ins.then_inc(*sg.inc("pe_step", also=[("gate_pre", i)]))

    stat(0, range(KD))
    for i in range(4):
        dense("lru", i, norm=None if i else 0)
        if i:
            gates(i - 1)
    dense("q", 0)
    gates(3)
    dense("kv", 0)
    dense("ga", 0)
    pe.wait_ge(*sg.event("act_sq", "qkv"))
    pe.matmul(b[4][:], one, m["sq2"][:, 0, :], start=True, stop=False)
    pe.matmul(b[4][:], one, m["sq2"][:, 1, :], start=False, stop=True)
    pe.matmul(b[5][:], one, m["ti"][:, 0, :], start=True, stop=True).then_inc(*sg.inc("pe_step", also=[("stat", "qkv")]))
    dense("ga", 1)
    pe.wait_ge(*sg.event("ak"))
    pe.matmul(b[6][:], K[:, K_J2:K_J2 + P], m["Ak"][:], start=True, stop=True).then_inc(*sg.inc("pe_step", also=[("kp_acc", None)]))
    for kind, i in (("ga", 2), ("ga", 3), ("gb", 0), ("gb", 1), ("gb", 2), ("gb", 3)):
        dense(kind, i)

    pe.wait_ge(*sg.event("cql"))
    n, g = W_INDEX["ukv", 0], FIRST_GROUP["ukv", 0]
    ukv_hi, ukv_lo = weights(n)
    for j in range(8):
        out = bank(g + j)
        tok, c = slice((j // 2) * P, (j // 2 + 1) * P), 1024 + (j % 2) * 512
        ins = split3(pe, out[:], m["ckvh"][:, tok], m["ckvl"][:, tok], ukv_hi[:, c:c + 512], ukv_lo[:, c:c + 512], True, True)
        ins.then_inc(*sg.inc("pe_step", also=[("acc", g + j)]))
    for j in range(4, 8):
        pe.wait_ge(*sg.event("free", g + j))

    pe.wait_ge(*sg.event("kp"))
    for h in range(-2, HEADS):
        if 0 <= h + 1 < HEADS:
            a = h + 1
            pe.wait_ge(*sg.event("act_qk", ("kn", a)))
            pe.wait_ge(*sg.event("qa", a))
            for q in Q_ORDER:
                s, w = score_bank(b, q), (q + 1) * P
                if a:
                    pe.wait_ge(*sg.event("act_exp", 4 * (a - 1) + (2 if q == 0 else q)))
                tok = slice(q * P, (q + 1) * P)
                pe.matmul(s, m["qn"][:, a % 2, tok], m["kn"][:, a % 2, 0:w], start=True, stop=False)
                pe.matmul(s, m["qa"][:, a % 2, tok], m["Kp"][:, 0:w], start=False, stop=False)
                ins = pe.matmul(s[:, q * P:w], m["idb"][:], m["maskb"][:], start=False, stop=True)
                ins.then_inc(*sg.inc("pe_step", also=[("s", 4 * a + q), *([("s", 4 * a)] if q == 2 else [])]))
        if h + 2 < HEADS:
            a = h + 2
            hi, lo = weights(W_INDEX["uq", a // 4])
            if a:
                pe.wait_ge(*sg.event("act_qk", ("kn", a - 1)))
            for k in range(2):
                c = k * 1024 + (a % 4) * 256
                ins = split3(pe, b[3][:], hi[:, c:c + P], lo[:, c:c + P], m["cqh"][:, k, :], m["cql"][:, k, :], k == 0, k == 1)
            ins.then_inc(*sg.inc("pe_step", also=[("qn_acc", a)]))
            if a:
                pe.wait_ge(*sg.event("qa", a - 1))
            for k in range(2):
                c = k * 1024 + (a % 4) * 256 + P
                ins = split3(pe, b[4][:], hi[:, c:c + P], lo[:, c:c + P], m["cqh"][:, k, :], m["cql"][:, k, :], k == 0, k == 1)
            ins.then_inc(*sg.inc("pe_step", also=[("qr_acc", a)]))
            pe.wait_ge(*sg.event("act_qk", ("qn", a)))
            c = a * P
            ins = split3(pe, b[3][:], ukv_hi[:, c:c + P], ukv_lo[:, c:c + P], m["ckvh"][:], m["ckvl"][:], True, True)
            ins.then_inc(*sg.inc("pe_step", also=[("kn_acc", a), *([("w_used", W_INDEX["uq", 0])] if a == 3 else []), *([("w_used", W_INDEX["uq", 1]), ("w_used", W_INDEX["ukv", 0])] if a == 7 else [])]))
        if h >= 0:
            for kb in range(4):
                if kb < 2:
                    if h:
                        pe.wait_ge(*sg.event("pt", (h - 1, kb + 2)))
                else:
                    pe.wait_ge(*sg.event("pt", (h, kb - 2)))
                for q in range(kb, 4):
                    pe.wait_ge(*sg.event("p", 4 * h + q))
                    c = P_AT[q] + kb * P
                    ins = pe.transpose(b[5 + kb % 2][:, (q - kb) * P:(q - kb + 1) * P], m["P2"][:, h % 2, c:c + P], K[:, K_ID:K_ID + P])
                ins.then_inc(*sg.inc("pe_step", also=[("t", (h, kb))]))
            if h:
                pe.wait_ge(*sg.event("y", h - 1))
            for kb in range(4):
                w = (4 - kb) * P
                pe.wait_ge(*sg.event("pt", (h, kb)))
                ins = pe.matmul(b[7][:, kb * P:S], m["V"][:, kb, h * P:(h + 1) * P], m["PT"][:, T_AT[kb]:T_AT[kb] + w],
                                start=(kb == 0), stop=(kb == 3))
            ins.then_inc(*sg.inc("pe_step", also=[("o", h)]))
    pe.wait_ge(*sg.event("yl", KD - 1))
    for i in range(4):
        dense("out", i, m["yh"], m["yl"])
        if i:
            stat(1, (2 * i - 2, 2 * i - 1))
    stat(1, (KD - 2, KD - 1))
    for half in range(2):
        for j in range(NF):
            dense("fi", half * NF + j, norm=None if half or j else 1)
            if ("fi", half * NF + j) in ADA_AFTER:
                ada_columns(ADA_AFTER["fi", half * NF + j])
        for j in range(KD):
            i = half * KD + j
            n, g = W_INDEX["fo", i], FIRST_GROUP["fo", i]
            hi, lo = weights(n)
            out = bank(g)
            pe.wait_ge(*sg.event("ffl", half * NF + NF - 1))
            for k in range(NF):
                c = k * P
                ins = split3(pe, out[:], hi[:, c:c + P], lo[:, c:c + P], m["hidh"][:, k, :], m["hidl"][:, k, :], k == 0, k == NF - 1)
            ins.then_inc(*sg.inc("pe_step", also=[("acc", g), ("w_used", n)]))
            if ("fo", i) in ADA_AFTER:
                ada_columns(ADA_AFTER["fo", i])

ADA_DVE = [i for i in range(ADA_CHUNKS) if i % 3]
START_SIGNALS = "st_x st_k st_c st_pos st_dve st_xt st_ev st_sin st_eva st_ada st_mod " + " ".join(f"st_w{i}" for i in range(ADA_SLOTS))


def start_program(engine, who, sg, m, b, W):
    K = m["K"]
    if who == "sp":
        engine.dma_start(K[:], W["consts"][:, 0:K_KEPT]).then_inc(*sg.inc("st_k", n=16))
        engine.dma_start(m["mask0"][:], W["consts"][:, K_MASK:K_MASK + P]).then_inc(*sg.inc("st_k", n=16))
        engine.dma_start(m["x0"][:], W["x"][0].rearrange("(t p) d -> p t d", p=P)).then_inc(*sg.inc("st_x", n=16))
        engine.dma_start(m["c"][:], W["c_cols"]).then_inc(*sg.inc("st_c", n=16))
        engine.dma_start(m["posi"][:], W["positions"].broadcast_to([P, S])).then_inc(*sg.inc("st_pos", n=16))
        w_ada = W["w_ada"][0].rearrange("(k p) n -> p k n", p=P)
        for i in range(ADA_CHUNKS):
            if i >= ADA_SLOTS:
                engine.wait_ge(*sg.event("ada_used", i - ADA_SLOTS))
            engine.dma_start(m["ada0"][:, i % ADA_SLOTS, :].rearrange("p (k n) -> p k n", k=KD),
                             w_ada[:, :, i * 256:(i + 1) * 256]).then_inc(*sg.inc(f"st_w{i % ADA_SLOTS}", also=[("ada_in", i)], n=16))
    if who == "dve":
        v = engine

        pf, a, k, T = m["posf"][:], m["ang"][:], m["rot"][:], m["T"][:]
        v.memset(m["xpad"][:, :, 0:3], 0.0)
        engine.wait_ge(*sg.event("st_k"))
        v.tensor_copy(m["idb"][:], K[:, K_ID:K_ID + P])
        v.tensor_copy(m["maskb"][:], m["mask0"][:])
        engine.wait_ge(*sg.event("st_pos"))
        v.tensor_copy(pf, m["posi"][:]).then_inc(*sg.inc("st_dve"))
        engine.wait_ge(*sg.last("st_dve"))
        v.tensor_scalar(m["rs"][:], pf, 0.0, None, ALU.is_equal)
        v.tensor_scalar(a, pf, K[:, K_INVF:K_INVF + 1], None, ALU.mult).then_inc(*sg.inc("st_dve"))
        engine.wait_ge(*sg.last("st_dve"))
        v.tensor_scalar(k, a, 1.0 / (2 * np.pi), None, ALU.mult).then_inc(*sg.inc("st_dve"))
        engine.wait_ge(*sg.last("st_dve"))
        v.tensor_scalar(k, k, 12582912.0, -12582912.0, ALU.add, ALU.add).then_inc(*sg.inc("st_dve"))
        engine.wait_ge(*sg.last("st_dve"))
        for part in TWO_PI:
            v.scalar_tensor_tensor(a, k, -part, a, ALU.mult, ALU.add).then_inc(*sg.inc("st_dve"))
            engine.wait_ge(*sg.last("st_dve"))
        v.tensor_scalar(a, a, K[:, K_SG:K_SG + 1], K[:, K_PH:K_PH + 1], ALU.mult, ALU.add).then_inc(*sg.inc("st_dve"))
        engine.wait_ge(*sg.last("st_dve"))
        v.tensor_scalar(k, a, float(np.pi), -2 * float(np.pi), ALU.is_gt, ALU.mult).then_inc(*sg.inc("st_dve"))
        engine.wait_ge(*sg.last("st_dve"))
        v.tensor_tensor(a, a, k, ALU.add).then_inc(*sg.inc("st_dve"))
        engine.wait_ge(*sg.last("st_dve"))
        v.tensor_scalar(a, a, 3.1415925, -3.1415925, ALU.min, ALU.max).then_inc(*sg.inc("st_dve", "ang"))
        for t in range(0, 8):
            engine.wait_ge(*sg.event("st_xt", t))
            dst = m["X"][:, t, :]
            if t % 2:
                v.tensor_copy(dst, b[t][:]).then_inc(*sg.inc("st_ev", t))
        for n, i in enumerate(ADA_DVE):
            acc, raw = m["acc"][:, n % 2, :], m["ada0"][:, i % ADA_SLOTS, :]
            engine.wait_ge(*sg.event("ada_in", i))
            if n >= 2:
                engine.wait_ge(*sg.event("ada_col", ADA_DVE[n - 2]))
            engine.tensor_scalar(acc, raw[:, 0:256], m["c"][:, 0:1], None, ALU.mult).then_inc(*sg.inc("st_dve"))
            for k in range(1, KD):
                engine.wait_ge(*sg.last("st_dve"))
                engine.scalar_tensor_tensor(acc, raw[:, k * 256:(k + 1) * 256], m["c"][:, k:k + 1], acc,
                                            ALU.mult, ALU.add).then_inc(*sg.inc("st_dve", also=[("ada_used", i)]))
        engine.wait_ge(*sg.event("ada_done"))
        engine.tensor_copy(m["mod"][:], b[6][:, 0:48]).then_inc(*sg.inc("st_mod"))
    if who == "act":
        engine.wait_ge(*sg.event("st_dve", "ang"))
        engine.activation(m["T"][:], m["ang"][:], ACT.Sin).then_inc(*sg.inc("st_sin"))
        for t in range(0, 8, 2):
            engine.wait_ge(*sg.event("st_xt", t))
            engine.activation(m["X"][:, t, :], b[t][:], ACT.Copy).then_inc(*sg.inc("st_eva", t))
    if who == "pe":
        engine.wait_ge(*sg.event("st_k"))
        engine.wait_ge(*sg.event("st_x"))
        for k in range(KD):
            for t in range(NT):
                ins = engine.transpose(b[k][:, t * P:(t + 1) * P], m["x0"][:, t, k * P:(k + 1) * P], K[:, K_ID:K_ID + P])
            ins.then_inc(*sg.inc("st_xt", k))
        engine.wait_ge(*sg.event("st_c"))
        engine.wait_ge(*sg.event("st_eva", 6))
        for i in range(ADA_CHUNKS + 2):
            if i - 2 in ADA_DVE:
                engine.wait_ge(*sg.event("ada_used", i - 2))
                for j in range(2):
                    c = 2 * (i - 2) + j
                    ins = engine.matmul(b[6][:, c:c + 1], m["acc"][:, ADA_DVE.index(i - 2) % 2, j * P:(j + 1) * P],
                                        K[:, K_ONE:K_ONE + 1], start=True, stop=True)
                ins.then_inc(*sg.inc("st_ada", also=[("ada_col", i - 2), ("ada_done", None)]))
            if i >= ADA_CHUNKS or i in ADA_DVE:
                continue
            engine.wait_ge(*sg.event("ada_in", i))
            for j in range(2):
                for k in range(KD):
                    c = k * 256 + j * P
                    ins = engine.matmul(b[6][:, 2 * i + j:2 * i + j + 1], m["ada0"][:, i % ADA_SLOTS, c:c + P], m["c"][:, k:k + 1],
                                        start=(k == 0), stop=(k == KD - 1))
            ins.then_inc(*sg.inc("st_ada", also=[("ada_used", i), ("ada_done", None)]))


TWO_PI = (6.28125, 0.0019350051879882812, 3.019915981956753e-07)


def tensors(nc, ctx):
    m = {}

    def at(name, kib, shape, dtype=F32):
        m[name] = nc.alloc_sbuf_tensor_at(name, [shape[0], *shape[1:]], dtype, offset=BASE + int(kib * KB))

    at("X", 0, [P, KD, S])
    at("RAW", 16, [P, RAW_SLOTS, SLOT])
    at("WHI", 48, [P, W_SLOTS, SLOT], F32R)
    at("WLO", 72, [P, W_SLOTS, SLOT], F32R)
    at("ada0", 16, [P, ADA_SLOTS, SLOT])
    at("HH", 96, [P, KD, S], F32R)
    at("HL", 112, [P, KD, S], F32R)
    at("V", 96, [P, NT, D])
    at("P2", 112, [P, 2, 1280])
    at("PT", 122, [P, 1280])
    at("x0", 128, [P, NT, D])
    at("ya", 128, [P, KD, S])
    at("lruw", 144, [P, 2 * KD, P])
    at("tgb", 144, [P, KD, S])
    at("yh", 144, [P, KD, S], F32R)
    at("yl", 128, [P, KD, S], F32R)
    at("xc", 160, [P, 4, S])
    at("tr", 168, [P, 2, S])
    at("ti", 172, [P, 2, S])
    at("la", 176, [P, 2, S])
    at("sq2", 180, [P, 2, S])
    at("qraw", 184, [P, 2, S])
    at("kvraw", 188, [P, S])
    at("rq", 190, [P, 2, S])
    at("tg", 176, [P, 2, S])
    at("cqh", 160, [P, 2, S], F32R)
    at("cql", 164, [P, 2, S], F32R)
    at("ckvh", 168, [P, S], F32R)
    at("ckvl", 170, [P, S], F32R)
    at("Ak", 174, [P, S])
    at("Kp", 180, [P, S])
    at("qn", 184, [P, 2, S])
    at("qa", 188, [P, 2, S])
    at("kn", 172, [P, 2, S])
    at("to", 192, [P, S])
    at("hidh", 128, [P, NF, S], F32R)
    at("hidl", 150, [P, NF, S], F32R)
    at("fth", 172, [P, 2, S])
    at("fh", 176, [P, 2, S])
    at("nt", 180, [P, 2, S])
    at("nh", 184, [P, 2, S])
    at("rstd", 188, [P, S])
    at("sq", 190, [P, 2, S])
    at("posi", 160, [P, S], I32)
    at("posf", 162, [P, S])
    at("ang", 164, [P, S])
    at("rot", 166, [P, S])
    at("mask0", 168, [P, P])
    at("xpad", 194, [P, 2, 516])
    at("T", 198.125, [P, S])
    at("rs", 200.125, [P, S])
    at("K", 202.125, [P, K_KEPT])
    up = lambda size: (size + 31) // 32 * 32
    o = up(int(202.125 * KB) + K_KEPT * 4)
    mix_tensors(at, o)
    moe_tensors(at)
    for name, n, dt in (("vec", NVEC, F32), ("mod", 48, F32), ("acc", 512, F32), ("idb", P, BF16), ("maskb", P, BF16),
                        ("c", 8, F32), ("sm", 48, F32), ("hb", 32, F32), ("mx", 8, F32), ("nm", 8, F32),
                        ("sum", 8, F32), ("rec", 8, F32), ("zero", P, F32)):
        shape = [P, 2, 256] if name == "acc" else [P, n]
        at(name, o / KB, shape, dt)
        o += up(n * (2 if dt == BF16 else 4))
    assert BASE + o <= 229368, o
    return m


BASE = 16512


def program(nc, W, at):
    with ExitStack() as ctx:
        m = tensors(nc, ctx)
        b = [ctx.enter_context(nc.psum_tensor(f"bank{i}", [P, 512], F32)) for i in range(8)]
        start = Signals(nc, ctx, START_SIGNALS, at.setdefault("start", {}))
        layer = Signals(nc, ctx, LAYER_SIGNALS, at.setdefault("layer", {}))
        mix = Signals(nc, ctx, MIX_SIGNALS, at.setdefault("mix", {}))
        route = Signals(nc, ctx, ROUTE_SIGNALS, at.setdefault("route", {}))
        moe = LoopSignals(nc, ctx, MOE_SIGNALS, at.setdefault("moe", {}))
        final = Signals(nc, ctx, FINAL_SIGNALS, at.setdefault("final", {}))
        W = dict(W, h2tok=nc.dram_tensor("h2_by_token", (S, D), F32).ap(),
                 ybuf=nc.dram_tensor("expert_results", ((MAXB + 1) * P, D), F32).ap())
        arrived, go = [ctx.enter_context(nc.semaphore(n)) for n in ("arrived", "go")]
        zeroed = ctx.enter_context(nc.semaphore("zeroed"))
        after_mix = DEPTH + 2
        block = ctx.enter_context(nc.Block())

        def phase_end(eng, n):
            eng.drain().then_inc(arrived, 1)
            eng.wait_ge(go, n)

        def gather(sp):
            sp.wait_ge(arrived, 4)
            sp.sem_clear(arrived)
            sp.nop().then_inc(go, 1)

        def blocks(eng, who):
            eng.wait_ge(*route.event("bei"))
            return eng.value_load(m["bei"][0:1, NB:NB + 1], min_val=1, max_val=MAXB)

        def zero_results(pool, first, count):
            with pool.Fori(0, count) as i:
                rows = W["ybuf"][bass.ds((first + i) * P, P), :].rearrange("p (n d) -> p n d", d=P)
                zero = m["zero"][:].rearrange("p (o d) -> p o d", o=1).broadcast_to([P, KD, P])
                pool.dma_start(rows, zero).then_inc(zeroed, 16)

        def phases_of(eng, who, layer_part, moe_part):
            if who != "pool":
                start_program(eng, who, start, m, b, W)
            else:
                eng.memset(m["zero"][:], 0.0)
            phase_end(eng, 1)
            with eng.Fori(0, DEPTH) as l:
                layer_part(eng)
                phase_end(eng, l + 2)
            if who == "pool":
                zero_results(eng, MIN_BLOCKS + 1, MAXB - MIN_BLOCKS)
                eng.wait_ge(zeroed, (MAXB - MIN_BLOCKS) * 16)
            else:
                mix_program(eng, who, mix, m, b, W)
            phase_end(eng, after_mix)
            route_program(eng, who, route, m, b, W, moe)
            moe_part(eng, blocks(eng, who))
            phase_end(eng, after_mix + 1)
            final_program(eng, who, final, m, W, moe)

        @block.sync
        def _(sp):
            start_program(sp, "sp", start, m, b, W)
            gather(sp)
            with sp.Fori(0, DEPTH) as l:
                layer_loads(sp, l, layer, m, W)
                sp.wait_ge(arrived, 4)
                for s in layer.sem.values():
                    sp.sem_clear(s)
                sp.sem_clear(arrived)
                sp.nop().then_inc(go, 1)
            mix_program(sp, "sp", mix, m, b, W)
            gather(sp)
            route_program(sp, "sp", route, m, b, W, moe)
            moe_sp(sp, moe, m, W, blocks(sp, "sp"))
            gather(sp)
            final_program(sp, "sp", final, m, W, moe)

        @block.scalar
        def _(act):
            phases_of(act, "act", lambda e: layer_act(e, layer, m, b), lambda e, n: moe_act(e, moe, m, b, W, n))

        @block.vector
        def _(v):
            phases_of(v, "dve", lambda e: layer_dve(e, layer, m, b), lambda e, n: moe_dve(e, moe, m, b, n))

        @block.tensor
        def _(pe):
            phases_of(pe, "pe", lambda e: layer_pe(e, layer, m, b), lambda e, n: moe_pe(e, moe, m, b, n))

        @block.gpsimd
        def _(pool):
            phases_of(pool, "pool", lambda e: None, lambda e, n: moe_pool(e, moe, m, W, n))

        moe.close()


def constants():
    K = np.zeros((P, NK), np.float32)
    i = np.arange(P)
    K[:, K_ID:K_ID + P] = np.eye(P)
    K[:, K_J2:K_J2 + P] = (i[:, None] % ROPE) == (i[None, :] % ROPE)
    K[:, K_ONE:K_ONE + P] = 1.0
    K[:, K_MASK:K_MASK + P] = np.where(i[None, :] > i[:, None], -1e30, 0.0)
    half = ROPE // 2
    K[:, K_INVF] = (np.float64(10000.0) ** (-(np.arange(half) * 2) / ROPE)).astype(np.float32)[i % half]
    K[:, K_SG] = np.where((i >= 64) & (i < 96), -1.0, 1.0)
    K[:, K_PH] = np.where(i < 64, np.pi / 2, 0.0)
    K[:, K_TRI:K_TRI + P] = i[None, :] >= i[:, None]
    K[:, K_LT:K_LT + P] = i[:, None] < i[None, :]
    K[:, K_INV:K_INV + 16] = 1.0 / (np.arange(16) + 1)
    K[:, K_I32:K_I32 + 32] = np.arange(32)
    K[:, K_I48:K_I48 + 50] = np.arange(50)
    K[:, K_I128:K_I128 + P] = np.arange(P)
    K[:, K_E6], K[:, K_E5] = 1e-6, 1e-5
    return K


def columns(v):
    return np.ascontiguousarray(np.asarray(v).reshape(-1, P).T)


def layer_vectors(i, l):
    parts = [i["b_ada"][l], i["conv_w"][l], i["conv_b"][l], i["lru_ba"][l], i["lru_bx"][l], i["lru_a_param"][l],
             i["q_norm_g"][l], i["kv_norm_g"][l]]
    return np.concatenate([columns(p) for p in parts], axis=1)


def block_vectors(i):
    v = np.zeros((P, NV2), np.float32)
    for at, name in ((V2_FIN, "final_norm_g"), (V2_N1, "norm1_g_2"), (V2_CW, "conv_w_2"), (V2_HN, "head_norm_g_2"),
                     (V2_PS, "pool_scale_2"), (V2_N2, "norm2_g_2")):
        c = columns(i[name])
        v[:, at:at + c.shape[1]] = c
    v[0:MH, V2_IG] = np.asarray(i["ig_b_2"])[0]
    v[0:MH, V2_FG] = np.asarray(i["fg_b_2"])[0]
    p = np.arange(P)
    v[:, V2_TOK:V2_TOK + 4] = p[:, None] + P * np.arange(4)[None, :]
    v[:, V2_PM] = p % EXPERTS
    return v


def head_selectors():
    return np.repeat(np.eye(MH, dtype=np.float32), P, axis=1)

MH, MD = 4, 128
EXPERTS, TOP = 32, 4
MAXB = S * TOP // P + EXPERTS
MIN_BLOCKS = S * TOP // P
V2_FIN, V2_N1, V2_CW, V2_HN, V2_PS, V2_N2, V2_IG, V2_FG, V2_TOK, V2_PM = 0, 8, 16, 48, 52, 56, 64, 65, 66, 70
NV2 = 71
MIX_CHUNKS = ([("gate", 0)] + [("qk", i) for i in range(4)] + [("v", i) for i in range(2)]
              + [("o", i) for i in range(2)] + [("u", i) for i in range(2)] + [("out", i) for i in range(4)])
MIX_GROUPS = {"gate": 2, "qk": 2, "v": 4, "o": 2, "u": 2, "out": 2}
MIX_COLUMN = {"gate": 2048, "qk": 0, "v": 1024, "o": 1536, "u": 2056}
MIX_AT = {c: n for n, c in enumerate(MIX_CHUNKS)}


def mix_groups():
    first, g = {}, 0
    for c in MIX_CHUNKS:
        first[c] = g
        g += MIX_GROUPS[c[0]]
    return first


MIX_FIRST = mix_groups()
MIX_SIGNALS = """mix_act mix_dve mix_pe mix_raw0 mix_raw1 mix_raw2 mix_raw3 mix_used mix_hi mix_small mix_free_act
    mix_free_dve mix_out_act mix_out_dve"""


def mix_program(engine, who, sg, m, b, W):
    f = lambda t: t.bitcast(F32)
    K, X, HH, HL, vec = m["K"], m["X"], m["HH"], m["HL"], m["vec2"]
    one = K[:, K_ONE:K_ONE + P]
    CC = len(MIX_CHUNKS)

    if who == "sp":
        sp = engine
        for dst, src in ((vec[:], W["vecs2"]), (m["tri"][:], W["consts"][:, K_TRI:K_TRI + P]),
                         (m["inv"][:], W["consts"][:, K_INV:K_INV + 16]),
                         (m["sel4"][:], W["sel4"])):
            sp.dma_start(dst, src).then_inc(*sg.inc("mix_small", also=[("small", None)], n=16))
        w_in, w_out = [W[n][0].rearrange("(k p) n -> p k n", p=P) for n in ("w_in_2", "w_out_2")]
        for n, (kind, i) in enumerate(MIX_CHUNKS):
            if n >= RAW_SLOTS:
                sp.wait_ge(*sg.event("mix_used", n - RAW_SLOTS))
            if (kind, i) == ("o", 0):
                sp.wait_ge(*sg.event("pre", 7))
                sp.dma_start(m["pw"][:], W["pool_w_2"][0].rearrange("g c d -> c g d")).then_inc(*sg.inc("mix_small", "pw", n=16))
            src = w_out[:, :, i * 256:(i + 1) * 256] if kind == "out" else \
                w_in[:, :, MIX_COLUMN[kind] + i * 256:MIX_COLUMN[kind] + i * 256 + 256]
            sp.dma_start(m["RAW"][:, n % RAW_SLOTS, :].rearrange("p (k n) -> p k n", k=KD), src).then_inc(*sg.inc(f"mix_raw{n % RAW_SLOTS}", also=[("raw", n)], n=16))
        return

    if who == "act":
        act = engine
        fed = [0]

        def feed(upto):
            while fed[0] <= min(upto, CC - 1):
                n = fed[0]
                act.wait_ge(*sg.event("raw", n))
                if n >= W_SLOTS:
                    act.wait_ge(*sg.event("w_used", n - W_SLOTS))
                act.activation(m["WHI"][:, n % W_SLOTS, :], m["RAW"][:, n % RAW_SLOTS, :], ACT.Copy).then_inc(*sg.inc("mix_hi", n))
                fed[0] += 1

        for t in range(2):
            for k in range(KD):
                if t:
                    act.wait_ge(*sg.event("x1", k))
                if (t, k) >= (0, 2):
                    act.wait_ge(*sg.event("sq_used", (t, k - 2) if k >= 2 else (t - 1, KD - 2 + k)))
                act.activation(m["sq"][:, k % 2, :], X[:, k, :], ACT.Square).then_inc(*sg.inc("mix_out_act", also=[("sq", (t, k))]))
            act.wait_ge(*sg.event("stat", t))
            e = K_E5 if t else K_E6
            act.activation(m["rstd"][:], b[4][:], ACT.Sqrt, bias=K[:, e:e + 1], scale=1.0 / D).then_inc(*sg.inc("mix_out_act", also=[("root", t)]))
            if t == 0:
                feed(1)
        for k in range(KD):
            act.wait_ge(*sg.event("h", k))
            act.activation(HH[:, k, :], m["nh"][:, k % 2, :], ACT.Copy).then_inc(*sg.inc("mix_out_act", also=[("hh", k)]))
        tanh_n = 0
        for n, (kind, i) in enumerate(MIX_CHUNKS):
            feed(n + 2)
            g = MIX_FIRST[kind, i]
            if kind == "qk":
                for j in range(2):
                    act.wait_ge(*sg.event("acc", g + j))
                    if i:
                        act.wait_ge(*sg.event("pre", 2 * i + j - 2))
                    act.activation(m["xpad"][:, j, 3:3 + S], b[(g + j) % 4][:], ACT.Copy).then_inc(*sg.inc("mix_free_act", also=[("free", g + j)]))
                for j in range(2):
                    act.wait_ge(*sg.event("pre", 2 * i + j))
                    if i:
                        act.wait_ge(*sg.event("qk_done", 2 * i + j - 2))
                    act.activation(m["stm"][:, j, :], m["qk"][:, 2 * i + j, :], ACT.Tanh, scale=0.5).then_inc(*sg.inc("mix_out_act", also=[("qkt", 2 * i + j)]))
            elif kind == "v":
                for j in range(4):
                    act.wait_ge(*sg.event("acc", g + j))
                    act.activation(m["v2"][:, j, i * 256:(i + 1) * 256], b[(g + j) % 4][:, 0:256], ACT.Copy).then_inc(*sg.inc("mix_free_act", also=[("free", g + j)]))
                if i == 0:
                    act.wait_ge(*sg.event("row_abs"))
                    act.activation(m["row"][0:4, 2, :], m["row"][0:4, 1, :], ACT.Exp, scale=-1.0).then_inc(*sg.inc("mix_out_act", also=[("row_exp", None)]))
                else:
                    act.wait_ge(*sg.event("row_m"))
                    act.activation(m["row"][0:4, 2, :], m["row"][0:4, 1, :], ACT.Exp, scale=-1.0).then_inc(*sg.inc("mix_out_act", also=[("row_em", None)]))
            elif kind == "o":
                for j in range(2):
                    act.wait_ge(*sg.event("acc", g + j))
                    act.activation(m["tho"][:, 2 * i + j, :], b[(g + j) % 4][:], ACT.Tanh, scale=0.5).then_inc(*sg.inc("mix_free_act", also=[("free", g + j)]))
            elif kind == "u":
                for j in range(2):
                    act.wait_ge(*sg.event("acc", g + j))
                    if i:
                        act.wait_ge(*sg.event("pooled", j))
                    act.activation(m["upad"][:, j, 16:16 + S], b[(g + j) % 4][:], ACT.Copy).then_inc(*sg.inc("mix_free_act", also=[("free", g + j), ("u", 2 * i + j)]))
                if i:
                    break
        for j in range(4):
            act.wait_ge(*sg.event("yp", j))
            act.activation(HH[:, 4 + j, :], m["yp"][:, j, :], ACT.Copy).then_inc(*sg.inc("mix_out_act", also=[("yph", j)]))
        feed(MIX_AT["out", 0])
        feed(MIX_AT["out", 2])
        for h in range(MH):
            for s in range(4):
                w, n = (4 - s) * P, 4 * h + s
                act.wait_ge(*sg.event("e1", n))
                act.activation(m["dec"][:, s % 2, 0:w], m["dec"][:, s % 2, 0:w], ACT.Exp).then_inc(*sg.inc("mix_out_act", also=[("dec", n)]))
        for h in range(MH):
            act.wait_ge(*sg.event("hc", h))
            if h >= 2:
                act.wait_ge(*sg.event("var", h - 2))
            act.activation(m["sq"][:, h % 2, :], m["hm"][:, h, :], ACT.Square).then_inc(*sg.inc("mix_out_act", also=[("hsq", h)]))
        for h in range(MH):
            act.wait_ge(*sg.event("var", h))
            act.activation(m["hr"][:, h, :], b[h][:], ACT.Sqrt, bias=K[:, K_E5:K_E5 + 1], scale=1.0 / MD).then_inc(*sg.inc("mix_out_act", also=[("hroot", h)]))
        for h in range(MH):
            act.wait_ge(*sg.event("ym", h))
            act.activation(HH[:, h, :], m["hm"][:, h, :], ACT.Copy).then_inc(*sg.inc("mix_out_act", also=[("ymh", h)]))
        for i in range(4):
            feed(MIX_AT["out", i] + 2)

    if who == "dve":
        v = engine

        fed = [0]

        def feed(upto):
            while fed[0] <= min(upto, CC - 1):
                n = fed[0]
                v.wait_ge(*sg.event("mix_hi", n))
                v.tensor_tensor(m["WLO"][:, n % W_SLOTS, :], m["RAW"][:, n % RAW_SLOTS, :], f(m["WHI"])[:, n % W_SLOTS, :],
                                        ALU.subtract).then_inc(*sg.inc("mix_used", n, also=[("w", n)]))
                fed[0] += 1

        v.wait_ge(*sg.event("small"))
        v.tensor_scalar(vec[:, V2_HN:V2_HN + 4], vec[:, V2_HN:V2_HN + 4], 0.5, None, ALU.mult).then_inc(*sg.inc("mix_dve"))
        v.wait_ge(*sg.last("mix_dve"))
        for t in range(2):
            v.wait_ge(*sg.event("root", t))
            v.reciprocal(m["rstd"][:], m["rstd"][:]).then_inc(*sg.inc("mix_dve"))
            v.wait_ge(*sg.last("mix_dve"))
            if t == 0:
                for k in range(KD):
                    v.scalar_tensor_tensor(X[:, k, :], X[:, k, :], vec[:, V2_FIN + k:V2_FIN + k + 1], m["rstd"][:],
                                           ALU.mult, ALU.mult).then_inc(*sg.inc("mix_out_dve", also=[("x1", k)]))
                feed(1)
                continue
            for k in range(KD + 1):
                if k < KD:
                    if k >= 2:
                        v.wait_ge(*sg.event("hh", k - 2))
                        v.wait_ge(*sg.event("hl", k - 2))
                    v.scalar_tensor_tensor(m["nh"][:, k % 2, :], X[:, k, :], vec[:, V2_N1 + k:V2_N1 + k + 1], m["rstd"][:],
                                           ALU.mult, ALU.mult).then_inc(*sg.inc("mix_out_dve", also=[("h", k)]))
                if k:
                    v.wait_ge(*sg.event("h", k - 1))
                    v.wait_ge(*sg.event("hh", k - 1))
                    v.tensor_tensor(HL[:, k - 1, :], m["nh"][:, (k - 1) % 2, :], f(HH)[:, k - 1, :],
                                    ALU.subtract).then_inc(*sg.inc("mix_out_dve", also=[("hl", k - 1)]))
        row = lambda r: m["row"][0:4, r, :]
        for n, (kind, i) in enumerate(MIX_CHUNKS):
            feed(n + 2)
            g = MIX_FIRST[kind, i]
            if kind == "gate":
                v.wait_ge(*sg.event("acc", g))
                v.tensor_scalar(row(0), b[g % 4][0:4, :], vec[0:4, V2_IG:V2_IG + 1], None, ALU.add).then_inc(*sg.inc("mix_free_dve", also=[("free", g)]))
                v.wait_ge(*sg.event("acc", g + 1))
                v.tensor_scalar(row(5), b[(g + 1) % 4][0:4, :], vec[0:4, V2_FG:V2_FG + 1], None, ALU.add).then_inc(*sg.inc("mix_free_dve", also=[("free", g + 1)]))
                v.wait_ge(*sg.event("free", g + 1))
                v.tensor_scalar(row(3), row(5), -1.0, None, ALU.mult).then_inc(*sg.inc("mix_dve"))
                v.wait_ge(*sg.last("mix_dve"))
                v.tensor_tensor(row(1), row(5), row(3), ALU.max).then_inc(*sg.inc("mix_out_dve", also=[("row_abs", None)]))
            elif kind == "qk":
                for j in range(2):
                    blk = 2 * i + j
                    pre, pad = m["qk"][:, blk, :], m["xpad"][:, j, :]
                    cw = lambda t: vec[:, V2_CW + 8 * t + blk:V2_CW + 8 * t + blk + 1]
                    v.wait_ge(*sg.event("free", g + j))
                    v.tensor_scalar(pre, pad[:, 0:S], cw(0), None, ALU.mult).then_inc(*sg.inc("mix_dve"))
                    v.wait_ge(*sg.last("mix_dve"))
                    v.scalar_tensor_tensor(pre, pad[:, 1:1 + S], cw(1), pre, ALU.mult, ALU.add).then_inc(*sg.inc("mix_dve"))
                    v.wait_ge(*sg.last("mix_dve"))
                    v.scalar_tensor_tensor(pre, pad[:, 2:2 + S], cw(2), pre, ALU.mult, ALU.add).then_inc(*sg.inc("mix_dve"))
                    v.wait_ge(*sg.last("mix_dve"))
                    v.scalar_tensor_tensor(pre, pad[:, 3:3 + S], cw(3), pre, ALU.mult, ALU.add).then_inc(*sg.inc("mix_out_dve", also=[("pre", blk)]))
                for j in range(2):
                    blk = 2 * i + j
                    v.wait_ge(*sg.event("qkt", blk))
                    v.scalar_tensor_tensor(m["qk"][:, blk, :], m["stm"][:, j, :], 1.0, m["qk"][:, blk, :], ALU.add, ALU.mult).then_inc(*sg.inc("mix_out_dve", also=[("qk_done", blk)]))
            elif kind == "v" and i == 0:
                v.wait_ge(*sg.event("row_exp"))
                log1p(v, sg, "mix_dve", row(1), row(2), row(4), row(6))
                v.tensor_scalar(row(3), row(3), 0.0, None, ALU.max).then_inc(*sg.inc("mix_dve"))
                v.wait_ge(*sg.last("mix_dve"))
                v.tensor_tensor(row(3), row(3), row(1), ALU.add).then_inc(*sg.inc("mix_dve"))
                v.wait_ge(*sg.last("mix_dve"))
                v.tensor_scalar(row(3), row(3), -1.0, None, ALU.mult).then_inc(*sg.inc("mix_dve"))
                v.wait_ge(*sg.last("mix_dve"))
                v.memset(row(6), 1.0).then_inc(*sg.inc("mix_dve"))
                v.wait_ge(*sg.last("mix_dve"))
                v.tensor_tensor_scan(row(4), row(6), row(3), 0.0, ALU.mult, ALU.add).then_inc(*sg.inc("mix_dve"))
                v.wait_ge(*sg.last("mix_dve"))
                v.tensor_tensor(row(0), row(0), row(4), ALU.subtract).then_inc(*sg.inc("mix_dve"))
                v.wait_ge(*sg.last("mix_dve"))
                v.tensor_tensor_scan(row(5), row(0), row(0), 0.0, ALU.max, ALU.max).then_inc(*sg.inc("mix_dve"))
                v.wait_ge(*sg.last("mix_dve"))
                v.tensor_tensor(row(1), row(4), row(5), ALU.add).then_inc(*sg.inc("mix_out_dve", also=[("row_m", None)]))
                v.tensor_scalar(row(5), row(5), -1.0, None, ALU.mult).then_inc(*sg.inc("mix_out_dve", also=[("row_nm", None)]))
            elif kind == "v":
                v.wait_ge(*sg.event("gcol_t"))
                v.tensor_copy(m["gcol"][:], b[5][:, 0:16]).then_inc(*sg.inc("mix_out_dve", also=[("gcol", None)]))
            elif kind == "u":
                if i == 0:
                    v.memset(m["upad"][:, :, 0:16], 0.0)
                    v.memset(m["spad"][:, :, 0:16], 0.0).then_inc(*sg.inc("mix_dve"))
                    v.wait_ge(*sg.last("mix_dve"))
                for j in range(2):
                    gi = 2 * i + j
                    v.wait_ge(*sg.event("u", gi))
                    if gi >= 1:
                        v.wait_ge(*sg.event("pooled", gi - 1))
                    u = m["upad"][:, j, :]
                    src = u
                    for d in range(gi + 1):
                        dst = m["spad"][:, d % 2, :]
                        v.tensor_tensor(dst[:, 16:16 + S], src[:, 16:16 + S], src[:, 16 - (1 << d):16 - (1 << d) + S], ALU.add).then_inc(*sg.inc("mix_dve"))
                        v.wait_ge(*sg.last("mix_dve"))
                        src = dst
                    w = 1 << (gi + 1)
                    if gi >= 2:
                        v.wait_ge(*sg.event("ps_used", gi - 2))
                    pl = m["pl"][:, gi % 2, :]
                    v.scalar_tensor_tensor(pl[:, w:S], src[:, 16 + w:16 + S], 1.0 / w, u[:, 16 + w:16 + S], ALU.mult, ALU.subtract)
                    v.tensor_tensor(pl[:, 0:w], src[:, 16:16 + w], m["inv"][:, 0:w], ALU.mult).then_inc(*sg.inc("mix_dve"))
                    v.wait_ge(*sg.last("mix_dve"))
                    v.tensor_tensor(pl[:, 0:w], pl[:, 0:w], u[:, 16:16 + w], ALU.subtract).then_inc(*sg.inc("mix_out_dve", also=[("pooled", gi)]))
                    v.wait_ge(*sg.event("mixed", gi))
                    v.tensor_scalar(m["yp"][:, gi, :], b[4 + gi][:], vec[:, V2_PS + gi:V2_PS + gi + 1], None, ALU.mult).then_inc(*sg.inc("mix_out_dve", also=[("yp", gi)]))
                if i:
                    break
        for j in range(4):
            v.wait_ge(*sg.event("yp", j))
            v.wait_ge(*sg.event("yph", j))
            v.tensor_tensor(HL[:, 4 + j, :], m["yp"][:, j, :], f(HH)[:, 4 + j, :], ALU.subtract).then_inc(*sg.inc("mix_out_dve", also=[("ypl", j)]))
        feed(MIX_AT["out", 2])
        def divide(h):
            t, num, den = m["dn"][:], b[4 + 2 * (h % 2)], b[5 + 2 * (h % 2)]
            v.wait_ge(*sg.event("numden", h))
            v.tensor_scalar(t, den[:], -1.0, None, ALU.mult).then_inc(*sg.inc("mix_dve"))
            v.wait_ge(*sg.last("mix_dve"))
            v.tensor_tensor(t, t, den[:], ALU.max).then_inc(*sg.inc("mix_dve"))
            v.wait_ge(*sg.last("mix_dve"))
            v.tensor_tensor(t, t, b[1][:], ALU.max).then_inc(*sg.inc("mix_dve"))
            v.wait_ge(*sg.last("mix_dve"))
            v.reciprocal(t, t).then_inc(*sg.inc("mix_dve"))
            v.wait_ge(*sg.last("mix_dve"))
            v.tensor_tensor(m["hm"][:, h, :], t, num[:], ALU.mult).then_inc(*sg.inc("mix_out_dve", also=[("hm", h)]))

        v.wait_ge(*sg.event("gcol"))
        for h in range(MH):
            for s in range(4):
                w, n = (4 - s) * P, 4 * h + s
                v.wait_ge(*sg.event("nmb", h))
                if n >= 2:
                    v.wait_ge(*sg.event("pm", n - 2))
                v.tensor_scalar(m["dec"][:, s % 2, 0:w], b[0][:, s * P:S], m["gcol"][:, 4 * s + h:4 * s + h + 1], 0.0,
                                    ALU.add, ALU.min).then_inc(*sg.inc("mix_out_dve", also=[("e1", n)]))
                if s >= 1:
                    scores(v, m, b, sg, h, s - 1)
                if s == 2 and h:
                    divide(h - 1)
            scores(v, m, b, sg, h, 3)
        divide(MH - 1)
        for h in range(MH):
            v.wait_ge(*sg.event("mean", h))
            v.scalar_tensor_tensor(m["hm"][:, h, :], b[4 + h][:], -1.0 / MD, m["hm"][:, h, :], ALU.mult, ALU.add).then_inc(*sg.inc("mix_out_dve", also=[("hc", h)]))
        for h in range(MH):
            v.wait_ge(*sg.event("hroot", h))
            v.wait_ge(*sg.event("hc", h))
            v.reciprocal(m["hr"][:, h, :], m["hr"][:, h, :]).then_inc(*sg.inc("mix_dve"))
            v.wait_ge(*sg.last("mix_dve"))
            v.scalar_tensor_tensor(m["hm"][:, h, :], m["hm"][:, h, :], vec[:, V2_HN + h:V2_HN + h + 1], m["hr"][:, h, :], ALU.mult, ALU.mult).then_inc(*sg.inc("mix_dve"))
            v.wait_ge(*sg.last("mix_dve"))
            v.scalar_tensor_tensor(m["hm"][:, h, :], m["tho"][:, h, :], 1.0, m["hm"][:, h, :], ALU.add, ALU.mult).then_inc(*sg.inc("mix_out_dve", also=[("ym", h)]))
        for h in range(MH):
            v.wait_ge(*sg.event("ym", h))
            v.wait_ge(*sg.event("ymh", h))
            v.tensor_tensor(HL[:, h, :], m["hm"][:, h, :], f(HH)[:, h, :], ALU.subtract).then_inc(*sg.inc("mix_out_dve", also=[("yml", h)]))
        for i in range(4):
            feed(MIX_AT["out", i] + 2)
            g = MIX_FIRST["out", i]
            for j in range(2):
                v.wait_ge(*sg.event("acc", g + j))
                v.wait_ge(*sg.event("x1", 2 * i + j))
                v.tensor_tensor(X[:, 2 * i + j, :], X[:, 2 * i + j, :], b[(g + j) % 4][:], ALU.add).then_inc(*sg.inc("mix_free_dve", also=[("free", g + j), ("x2", 2 * i + j)]))

    if who == "pe":
        pe = engine

        for t in range(2):
            for k in range(KD):
                pe.wait_ge(*sg.event("sq", (t, k)))
                if t and k == 0:
                    pe.wait_ge(*sg.event("root", 0))
                ins = pe.matmul(b[4][:], one, m["sq"][:, k % 2, :], start=(k == 0), stop=(k == KD - 1))
                ins.then_inc(*sg.inc("mix_pe", also=[("sq_used", (t, k)), *([("stat", t)] if k == KD - 1 else [])]))

        def bank(g):
            if g >= 4:
                pe.wait_ge(*sg.event("free", g - 4))
            return b[g % 4]

        for n, (kind, i) in enumerate(MIX_CHUNKS):
            if kind == "out" and i == 0:
                mlstm_pe(pe, m, b, sg, one)
            pe.wait_ge(*sg.event("w", n))
            hi, lo = m["WHI"][:, n % W_SLOTS, :], m["WLO"][:, n % W_SLOTS, :]
            g = MIX_FIRST[kind, i]
            for j in range(MIX_GROUPS[kind]):
                o = bank(g + j)
                for k in range(KD):
                    if kind == "v":
                        tok = slice(j * P, (j + 1) * P)
                        ins = split3(pe, o[:, 0:256], HH[:, k, tok], HL[:, k, tok], hi[:, k * 256:(k + 1) * 256],
                                     lo[:, k * 256:(k + 1) * 256], k == 0, k == KD - 1)
                    else:
                        c = k * 256 + j * (4 if kind == "gate" else P)
                        if n == 0 and j == 0:
                            pe.wait_ge(*sg.event("hl", k))
                        ins = split3(pe, o[:], hi[:, c:c + P], lo[:, c:c + P], HH[:, k, :], HL[:, k, :], k == 0, k == KD - 1)
                ins.then_inc(*sg.inc("mix_pe", also=[("acc", g + j), *([("w_used", n)] if j == MIX_GROUPS[kind] - 1 else [])]))
            if (kind, i) == ("o", 0):
                pe.wait_ge(*sg.event("row_m"))
                for s in range(4):
                    ins = pe.transpose(b[5][:, 4 * s:4 * s + 4], m["row"][0:4, 0, s * P:(s + 1) * P], K[0:4, K_ID:K_ID + 4])
                ins.then_inc(*sg.inc("mix_pe", also=[("gcol_t", None)]))


def scores(v, m, b, sg, h, s):
    w, n = (4 - s) * P, 4 * h + s
    v.wait_ge(*sg.event("dec", n))
    v.wait_ge(*sg.event("sc", n))
    if n >= 4:
        v.wait_ge(*sg.event("numden", h - 1))
    pm = m["pm"][:, T_AT[s]:T_AT[s] + w]
    v.scalar_tensor_tensor(pm, b[2 + s % 2][:, 0:w], 0.25 * MD ** -0.5, m["dec"][:, s % 2, 0:w], ALU.mult, ALU.mult).then_inc(*sg.inc("mix_dve"))
    v.wait_ge(*sg.last("mix_dve"))
    v.tensor_tensor(pm[:, 0:P], pm[:, 0:P], m["tri"][:], ALU.mult).then_inc(*sg.inc("mix_out_dve", also=[("pm", n)]))


def mlstm_pe(pe, m, b, sg, one):
    pe.wait_ge(*sg.event("mix_small", "pw"))
    for gi in range(4):
        pe.wait_ge(*sg.event("pooled", gi))
        pe.matmul(b[4 + gi][:], m["pw"][:, gi, :], m["pl"][:, gi % 2, :], start=True, stop=True).then_inc(*sg.inc("mix_pe", also=[("mixed", gi), ("ps_used", gi)]))
    pe.wait_ge(*sg.event("free", MIX_FIRST["u", 1] + 1))
    pe.wait_ge(*sg.event("row_nm"))
    pe.wait_ge(*sg.event("row_em"))
    pe.wait_ge(*sg.event("yp", 3))
    pe.wait_ge(*sg.event("qk_done", 7))
    for h in range(MH):
        sel = m["sel4"][0:4, h * P:(h + 1) * P]
        if h:
            pe.wait_ge(*sg.event("e1", 4 * h - 1))
        pe.matmul(b[0][:], sel, m["row"][0:4, 5, :], start=True, stop=True).then_inc(*sg.inc("mix_pe", also=[("nmb", h)]))
        for s in range(4):
            n = 4 * h + s
            if n >= 2:
                pe.wait_ge(*sg.event("pm", n - 2))
            w = (4 - s) * P
            pe.matmul(b[2 + s % 2][:, 0:w], m["qk"][:, 4 + h, s * P:(s + 1) * P], m["qk"][:, h, s * P:S], start=True, stop=True).then_inc(*sg.inc("mix_pe", also=[("sc", n)]))
            if s:
                numden(pe, m, b, sg, one, h, s - 1)
        if h:
            pe.wait_ge(*sg.event("hm", h - 1))
        pe.matmul(b[1][:], sel, m["row"][0:4, 2, :], start=True, stop=True)
        numden(pe, m, b, sg, one, h, 3)
    for h in range(MH):
        pe.wait_ge(*sg.event("hm", h))
        if h == 0:
            pe.wait_ge(*sg.event("hm", 3))
        pe.matmul(b[4 + h][:], one, m["hm"][:, h, :], start=True, stop=True).then_inc(*sg.inc("mix_pe", also=[("mean", h)]))
    for h in range(MH):
        pe.wait_ge(*sg.event("hsq", h))
        pe.wait_ge(*sg.event("pm", 15))
        pe.matmul(b[h][:], one, m["sq"][:, h % 2, :], start=True, stop=True).then_inc(*sg.inc("mix_pe", also=[("var", h)]))
    pe.wait_ge(*sg.event("yml", 3))
    pe.wait_ge(*sg.event("ypl", 3))
    pe.wait_ge(*sg.event("hroot", 3))


def numden(pe, m, b, sg, one, h, s):
    w = (4 - s) * P
    pe.wait_ge(*sg.event("pm", 4 * h + s))
    pm = m["pm"][:, T_AT[s]:T_AT[s] + w]
    pe.matmul(b[4 + 2 * (h % 2)][:, s * P:S], m["v2"][:, s, h * P:(h + 1) * P], pm, start=(s == 0), stop=(s == 3))
    ins = pe.matmul(b[5 + 2 * (h % 2)][:, s * P:S], one, pm, start=(s == 0), stop=(s == 3))
    if s == 3:
        ins.then_inc(*sg.inc("mix_pe", also=[("numden", h)]))


def mix_tensors(at, tail):
    at("qk", 128, [P, KD, S])
    at("hr", 128, [P, MH, S])
    at("v2", 144, [P, NT, MH * MD])
    at("tho", 152, [P, MH, S])
    at("row", 160, [P, 7, S])
    at("yp", 174, [P, 4, S])
    at("hm", 174, [P, MH, S])
    at("stm", 182, [P, 2, S])
    at("upad", 182, [P, 2, S + 16])
    at("spad", 186.25, [P, 2, S + 16])
    at("dec", 182, [P, 2, S])
    at("pm", 186, [P, 1280])
    at("dn", 192, [P, S])
    at("pw", 194, [P, 4, P])
    at("pl", 198.125, [P, 2, S])
    o = tail
    for name, shape in (("vec2", [P, NV2]), ("tri", [P, P]), ("inv", [P, 16]), ("gcol", [P, 16]), ("sel4", [4, MH * P])):
        at(name, o / KB, shape)
        size = 4
        for n in shape[1:]:
            size *= n
        o += (size + 31) // 32 * 32
    return o

ROUTE_SIGNALS = """ro_small ro_bias ro_act ro_dve ro_pe ro_pool ro_store ro_step"""
NB = MAXB + 1
MOE_SLOTS = 12
FIRST_CHUNKS = 7
MOE_CHUNKS = [(w, f, a) for f in range(2) for w in ("gate", "up") for a in range(2)] + \
             [("down", 0, 0), ("down", 1, 0), ("down", 0, 1), ("down", 1, 1)]
MOE_SIGNALS = "mo_gain mo_last mo_low mo_act mo_dve mo_pe mo_idx mo_x mo_y " + " ".join(f"mo_raw{c}" for c in range(MOE_SLOTS))
MOE_SEEDED = ("mo_low", "mo_act", "mo_dve", "mo_pe", "mo_x", "mo_y")


class LoopSignals(Signals):

    def total(self, sem):
        return self.known.get(("total", sem), ("", 1))[1]

    def close(self):
        for sem, count in self.count.items():
            self.at["total", sem] = (sem, count)

    def event(self, name, number=None, loop=None, back=0):
        if not self.known:
            return self.sem["mo_pe"], loop + 1
        sem, value = self.known[name, number]
        total = self.total(sem)
        return self.sem[sem], loop * total + (value + total * ((sem in MOE_SEEDED) - back))


def route_program(engine, who, sg, m, b, W, mo):
    K, X, vec = m["K"], m["X"], m["vec2"]
    one = K[:, K_ONE:K_ONE + P]
    ident = K[:, K_ID:K_ID + P]

    if who == "sp":
        sp = engine
        for dst, src in ((m["wr"][:], W["w_router_2"][0].rearrange("(k p) e -> p k e", p=P)),
                         (m["brow"][:], W["b_router_2"]),
                         (m["lt"][:], W["consts"][:, K_LT:K_LT + P]), (m["i32"][:], W["consts"][:, K_I32:K_I32 + EXPERTS]),
                         (m["i48"][:], W["consts"][:, K_I48:K_I48 + NB + 1]), (m["i128"][:], W["consts"][:, K_I128:K_I128 + P])):
            sp.dma_start(dst, src).then_inc(*sg.inc("ro_small", also=[("rsmall", None)], n=16))
        for j in range(3):
            for i, name in enumerate(("b_gate_2", "b_up_2", "b_down_2")):
                sp.dma_start(m["bf"][32 * j:32 * j + 32, i * D:(i + 1) * D], W[name][0]).then_inc(*sg.inc("ro_bias", also=[("bias", None)], n=16))
        for t in range(NT):
            sp.wait_ge(*sg.event("evac", 2 * t + 1))
            sp.dma_start(W["h2tok"][t * P:(t + 1) * P, :], m["h2t"][:, t, :]).then_inc(*sg.inc("ro_store", also=[("stored", None)], n=16))
        sp.wait_ge(*sg.event("bei"))
        return

    if who == "act":
        act = engine
        for k in range(KD):
            if k >= 2:
                act.wait_ge(*sg.event("sq_used", k - 2))
            act.activation(m["sqm"][:, k % 2, :], X[:, k, :], ACT.Square).then_inc(*sg.inc("ro_act", k, also=[("sq", k)]))
        act.wait_ge(*sg.event("stat"))
        act.activation(m["rstdm"][:], b[4][:], ACT.Sqrt, bias=K[:, K_E5:K_E5 + 1], scale=1.0 / D).then_inc(*sg.inc("ro_act", "root", also=[("root", None)]))
        for g in range(16):
            act.wait_ge(*sg.event("tg", g))
            dst = m["h2t" if g < 8 else "x2t"][:, g % 8 // 2, (g % 2) * 512:(g % 2 + 1) * 512]
            act.activation(dst, b[g % 4][:], ACT.Copy).then_inc(*sg.inc("ro_act", ("evac", g), also=[("evac", g)]))
            if g == 7:
                act.wait_ge(*sg.event("nmx"))
                for t in range(NT):
                    ins = act.activation(m["gates"][:, 4 * t:4 * t + 4], m["mxm"][:, 8 * t:8 * t + 4], ACT.Exp,
                                         bias=m["nmx"][:, t:t + 1], accum_out=m["gs"][:, t:t + 1])
                ins.then_inc(*sg.inc("ro_act", "gexp", also=[("gexp", None)]))

        for half in range(2):
            act.wait_ge(*sg.event("tx0", half))
            act.activation(m["xTh"][:, 4 * half:4 * half + 4, :], b[7 - half][:], ACT.Copy).then_inc(*sg.inc("ro_act", also=[("x0h", half)]))
        act.drain().then_inc(mo.sem["mo_act"], mo.total("mo_act"))

    if who == "dve":
        v = engine
        v.nop().then_inc(mo.sem["mo_low"], FIRST_CHUNKS)

        v.wait_ge(*sg.event("root"))
        v.reciprocal(m["rstdm"][:], m["rstdm"][:]).then_inc(*sg.inc("ro_step"))
        v.wait_ge(*sg.last("ro_step"))
        for k in range(KD):
            v.scalar_tensor_tensor(m["h2T"][:, k, :], X[:, k, :], vec[:, V2_N2 + k:V2_N2 + k + 1], m["rstdm"][:],
                                        ALU.mult, ALU.mult).then_inc(*sg.inc("ro_dve", also=[("h2", k)]))
        v.wait_ge(*sg.event("logits"))
        L, mx, mi = m["L"], m["mxm"], m["mi"]
        v.tensor_copy(L[:], b[5][:, 0:P]).then_inc(*sg.inc("ro_step"))
        v.wait_ge(*sg.last("ro_step"))
        for t in range(NT):
            ins = v.max(mx[:, 8 * t:8 * t + 8], L[:, 32 * t:32 * t + 32])
        ins.then_inc(*sg.inc("ro_step"))
        v.wait_ge(*sg.last("ro_step"))
        for t in range(NT):
            v.max_index(mi[:, 8 * t:8 * t + 8], mx[:, 8 * t:8 * t + 8], L[:, 32 * t:32 * t + 32])
        v.tensor_scalar(m["nmx"][:], mx[:].rearrange("p (t k) -> p t k", k=8)[:, :, 0], -1.0, None, ALU.mult).then_inc(*sg.inc("ro_step"))
        v.wait_ge(*sg.last("ro_step"))
        v.tensor_copy(m["mif"][:], mi[:]).then_inc(*sg.inc("ro_dve", also=[("nmx", None)]))
        v.wait_ge(*sg.event("rsmall"))
        v.wait_ge(*sg.event("nmx"))
        oh = m["oh"]
        for k in range(TOP):
            for t in range(NT):
                ins = v.tensor_scalar(oh[:, k, t * 32:t * 32 + 32], m["i32"][:], m["mif"][:, 8 * t + k:8 * t + k + 1], None, ALU.is_equal)
        ins.then_inc(*sg.inc("ro_step"))
        v.wait_ge(*sg.last("ro_step"))
        v.tensor_tensor(m["M"][:], oh[:, 0, :], oh[:, 1, :], ALU.add).then_inc(*sg.inc("ro_step"))
        v.wait_ge(*sg.last("ro_step"))
        v.tensor_tensor(m["M"][:], m["M"][:], oh[:, 2, :], ALU.add).then_inc(*sg.inc("ro_step"))
        v.wait_ge(*sg.last("ro_step"))
        v.tensor_tensor(m["M"][:], m["M"][:], oh[:, 3, :], ALU.add).then_inc(*sg.inc("ro_dve", also=[("M", None)]))
        v.wait_ge(*sg.event("ranks"))
        cnt, nb, incl, excl, be = m["cnt"][:], m["nb"][:], m["incl"][:], m["excl"][:], m["bef"][:]
        rk, rb, sr, pr = m["rk"][:], m["rb"][:], m["sr"][:], m["pr"][:]
        v.tensor_copy(m["cntc"][:], b[6][0:32, 160:161]).then_inc(*sg.inc("ro_step"))
        v.wait_ge(*sg.last("ro_step"))
        v.tensor_scalar(m["nbc"][:], m["cntc"][:], 0.0, None, ALU.is_gt).then_inc(*sg.inc("ro_step"))
        v.wait_ge(*sg.last("ro_step"))
        for j in range(1, NT):
            v.scalar_tensor_tensor(m["nbc"][:], m["cntc"][:], float(P * j), m["nbc"][:], ALU.is_gt, ALU.add).then_inc(*sg.inc("ro_step"))
            v.wait_ge(*sg.last("ro_step"))
        v.tensor_copy(m["nbf"][:], m["nbc"][:]).then_inc(*sg.inc("ro_dve", also=[("nbc", None)]))
        v.tensor_copy(rk, b[6][:, 0:P])
        v.tensor_copy(cnt, b[6][:, P:P + 32]).then_inc(*sg.inc("ro_step"))
        v.wait_ge(*sg.last("ro_step"))
        v.tensor_scalar(nb, cnt, 0.0, None, ALU.is_gt).then_inc(*sg.inc("ro_step"))
        v.wait_ge(*sg.last("ro_step"))
        for j in range(1, NT):
            v.scalar_tensor_tensor(nb, cnt, float(P * j), nb, ALU.is_gt, ALU.add).then_inc(*sg.inc("ro_step"))
            v.wait_ge(*sg.last("ro_step"))
        v.tensor_tensor_scan(incl, one[:, 0:32], nb, 0.0, ALU.mult, ALU.add).then_inc(*sg.inc("ro_step"))
        v.wait_ge(*sg.last("ro_step"))
        v.wait_ge(*sg.event("inclc"))
        v.tensor_copy(m["nbc"][:], b[5][0:32, 200:201]).then_inc(*sg.inc("ro_step"))
        v.wait_ge(*sg.last("ro_step"))
        v.tensor_scalar(m["cmp"][:], m["i48"][0:32, :], m["nbc"][:], None, ALU.is_ge).then_inc(*sg.inc("ro_dve", also=[("cmp", None)]))
        v.wait_ge(*sg.event("bep"))
        v.tensor_scalar(be, b[5][:, 256:256 + NB + 1], float(EXPERTS - 1), None, ALU.min).then_inc(*sg.inc("ro_step"))
        v.wait_ge(*sg.last("ro_step"))
        v.tensor_copy(m["bei"][:, 0:NB], be[0:1, 0:NB])
        v.memset(m["fresh"][:, 0:1], 1)
        v.tensor_tensor(m["fresh"][:, 1:NB], be[0:1, 1:NB], be[0:1, 0:NB - 1], ALU.not_equal)
        v.tensor_copy(m["bei"][:, NB:NB + 1], incl[0:1, 31:32]).then_inc(*sg.inc("ro_dve", also=[("bei", None)]))
        v.tensor_tensor(excl, incl, nb, ALU.subtract).then_inc(*sg.inc("ro_step"))
        v.wait_ge(*sg.last("ro_step"))
        v.tensor_scalar(rb, rk, float(P), None, ALU.is_ge).then_inc(*sg.inc("ro_step"))
        v.wait_ge(*sg.last("ro_step"))
        for j in range(2, NT):
            v.scalar_tensor_tensor(rb, rk, float(P * j), rb, ALU.is_ge, ALU.add).then_inc(*sg.inc("ro_step"))
            v.wait_ge(*sg.last("ro_step"))
        v.scalar_tensor_tensor(rk, rb, -float(P), rk, ALU.mult, ALU.add).then_inc(*sg.inc("ro_step"))
        v.wait_ge(*sg.last("ro_step"))
        for t in range(NT):
            ins = v.tensor_tensor(sr[:, t * 32:t * 32 + 32], rb[:, t * 32:t * 32 + 32], excl, ALU.add)
        ins.then_inc(*sg.inc("ro_step"))
        v.wait_ge(*sg.last("ro_step"))
        for k in range(TOP):
            for src, dst in ((sr, "bk"), (rk, "pk")):
                v.tensor_tensor(pr, oh[:, k, :], src, ALU.mult).then_inc(*sg.inc("ro_step"))
                v.wait_ge(*sg.last("ro_step"))
                v.tensor_reduce(m[dst][:, 4 * k:4 * k + 4], pr.rearrange("p (t e) -> p t e", e=32), AX.X, ALU.add).then_inc(*sg.inc("ro_step"))
                v.wait_ge(*sg.last("ro_step"))
        v.scalar_tensor_tensor(m["df"][:], m["bk"][:], float(P), m["pk"][:], ALU.mult, ALU.add).then_inc(*sg.inc("ro_step"))
        v.wait_ge(*sg.last("ro_step"))
        v.tensor_scalar(m["dest"][:], m["df"][:], float(P), None, ALU.add)
        for n in range(16):
            t = n % 4
            if n >= 2:
                v.wait_ge(*sg.event("ohp_used", n - 2))
            v.tensor_scalar(m["ohp"][:, n % 2, :], m["i128"][:], m["pk"][:, n:n + 1], None, ALU.is_equal)
            v.tensor_scalar(m["ohb"][:, n % 2, :], m["i48"][:], m["bk"][:, n:n + 1], vec[:, V2_TOK + t:V2_TOK + t + 1],
                                 ALU.is_equal, ALU.mult).then_inc(*sg.inc("ro_dve", also=[("ohp", n)]))
        v.wait_ge(*sg.event("tokens"))
        v.tensor_copy(m["tokcol"][:], b[7][:, 0:NB + 1]).then_inc(*sg.inc("ro_dve", also=[("tokcol", None)]))
        v.wait_ge(*sg.event("gexp"))
        v.reciprocal(m["gs"][:], m["gs"][:]).then_inc(*sg.inc("ro_step"))
        v.wait_ge(*sg.last("ro_step"))
        for t in range(NT):
            v.tensor_scalar(m["gates"][:, 4 * t:4 * t + 4], m["gates"][:, 4 * t:4 * t + 4], m["gs"][:, t:t + 1], None, ALU.mult)
        v.wait_ge(*sg.event("bp"))
        v.tensor_scalar(m["pmb"][:], one[0:96, :], vec[0:96, V2_PM:V2_PM + 1], None, ALU.mult).then_inc(*sg.inc("ro_step"))
        v.wait_ge(*sg.last("ro_step"))
        v.tensor_scalar(m["sel"][:], m["pmb"][:], m["bef"][0:96, 0:1], None, ALU.is_equal)
        v.wait_ge(*sg.event("x0"))
        v.nop().then_inc(mo.sem["mo_low"], MOE_SLOTS - FIRST_CHUNKS)
        for half in range(2):
            v.wait_ge(*sg.event("x0h", half))
            v.tensor_tensor(m["xTl"][:, 4 * half:4 * half + 4, :], b[7 - half][:].rearrange("p (k n) -> p k n", k=4),
                            m["xTh"][:, 4 * half:4 * half + 4, :].bitcast(F32), ALU.subtract)
        v.drain().then_inc(mo.sem["mo_dve"], mo.total("mo_dve"))

    if who == "pe":
        pe = engine
        pe.nop().then_inc(mo.sem["mo_pe"], mo.total("mo_pe"))

        for k in range(KD):
            pe.wait_ge(*sg.event("sq", k))
            ins = pe.matmul(b[4][:], one, m["sqm"][:, k % 2, :], start=(k == 0), stop=(k == KD - 1))
            ins.then_inc(*sg.inc("ro_pe", also=[("sq_used", k), *([("stat", None)] if k == KD - 1 else [])]))
        pe.wait_ge(*sg.event("rsmall"))
        for t in range(NT):
            o = b[5][:, t * 32:t * 32 + 32]
            pe.matmul(o, one[0:1, :], m["brow"][:], start=True, stop=False)
            for k in range(KD):
                pe.wait_ge(*sg.event("h2", k))
                ins = pe.matmul(o, m["h2T"][:, k, t * P:(t + 1) * P], m["wr"][:, k, :], start=False, stop=(k == KD - 1))
        ins.then_inc(*sg.inc("ro_pe", also=[("logits", None)]))

        def turn(g):
            src = m["h2T"] if g < 8 else X
            if g >= 4:
                pe.wait_ge(*sg.event("evac", g - 4))
            t = g % 8 // 2
            for j in range(4):
                k = (g % 2) * 4 + j
                ins = pe.transpose(b[g % 4][:, j * P:(j + 1) * P], src[:, k, t * P:(t + 1) * P], ident)
            ins.then_inc(*sg.inc("ro_pe", also=[("tg", g)]))

        for g in range(8):
            turn(g)
        pe.wait_ge(*sg.event("M"))
        M = lambda t: m["M"][:, t * 32:t * 32 + 32]
        for t in range(NT):
            o = b[6][:, t * 32:t * 32 + 32]
            for u in range(t):
                pe.matmul(o, one, M(u), start=(u == 0), stop=False)
            pe.matmul(o, m["lt"][:], M(t), start=(t == 0), stop=True)
        for t in range(NT):
            pe.matmul(b[6][:, P:P + 32], one, M(t), start=(t == 0), stop=(t == NT - 1))
        for t in range(NT):
            ins = pe.matmul(b[6][0:32, 160:161], M(t), one[:, 0:1], start=(t == 0), stop=(t == NT - 1))
        ins.then_inc(*sg.inc("ro_pe", also=[("ranks", None)]))
        pe.wait_ge(*sg.event("nbc"))
        pe.matmul(b[5][0:32, 200:201], m["tri"][0:32, 0:32], m["nbf"][:], start=True, stop=True).then_inc(*sg.inc("ro_pe", also=[("inclc", None)]))
        pe.wait_ge(*sg.event("cmp"))
        pe.matmul(b[5][:, 256:256 + NB + 1], one[0:32, :], m["cmp"][:], start=True, stop=True).then_inc(*sg.inc("ro_pe", also=[("bep", None)]))
        for g in range(8, 16):
            turn(g)
        for n in range(16):
            pe.wait_ge(*sg.event("ohp", n))
            ins = pe.matmul(b[7][:, 0:NB + 1], m["ohp"][:, n % 2, :], m["ohb"][:, n % 2, :], start=(n == 0), stop=(n == 15))
            ins.then_inc(*sg.inc("ro_pe", also=[("ohp_used", n), *([("tokens", None)] if n == 15 else [])]))
        pe.wait_ge(*sg.event("evac", 15))
        pe.wait_ge(*sg.event("tokcol"))
        pe.wait_ge(*sg.event("x0"))
        for half in range(2):
            for j in range(4):
                ins = pe.transpose(b[7 - half][:, j * P:(j + 1) * P], m["xg"][:, (4 * half + j) * P:(4 * half + j + 1) * P], ident)
            ins.then_inc(*sg.inc("ro_pe", also=[("tx0", half)]))
        pe.wait_ge(*sg.event("bp"))

    if who == "pool":
        pool = engine
        bf, br, bp = m["bf"], m["br"], m["bp"]

        pool.wait_ge(*sg.event("bias"))
        pool.tensor_copy(bp[:], bf[:]).then_inc(*sg.inc("ro_pool", also=[("bp", None)]))
        pool.wait_ge(*sg.last("ro_pool"))
        pool.tensor_tensor(br[:], bf[:], bp[:], ALU.subtract).then_inc(*sg.inc("ro_pool", also=[("bp", None)]))
        pool.wait_ge(*sg.last("ro_pool"))
        pool.tensor_copy(bp[32:64, :], br[32:64, :])
        pool.tensor_copy(bp[64:96, :], br[64:96, :]).then_inc(*sg.inc("ro_pool", also=[("bp", None)]))
        pool.wait_ge(*sg.last("ro_pool"))
        pool.tensor_tensor(br[64:96, :], br[64:96, :], bp[64:96, :], ALU.subtract).then_inc(*sg.inc("ro_pool", also=[("bp", None)]))
        pool.wait_ge(*sg.last("ro_pool"))
        pool.tensor_copy(bp[64:96, :], br[64:96, :]).then_inc(*sg.inc("ro_pool", also=[("bp", None)]))
        pool.wait_ge(*sg.last("ro_pool"))
        pool.wait_ge(*sg.event("tokcol"))
        pool.wait_ge(*sg.event("stored"))
        pool.wait_ge(*sg.event("tg", 15))
        pool.indirect_dma_start(m["xg"][:], None, W["h2tok"][:, :],
                                bass.IndirectOffsetOnAxis(m["tokcol"][:, 0:1], 0)).then_inc(mo.sem["mo_x"], 16)
        pool.wait_ge(mo.sem["mo_x"], 16)
        pool.nop().then_inc(*sg.inc("ro_pool", "x0", also=[("x0", None)]))
        pool.wait_ge(*sg.event("tx0", 1))


def moe_sp(sp, sg, m, W, count):
    with sp.Fori(0, count) as b:
        e = sp.value_load(m["bei"][0:1, bass.ds(b, 1)], min_val=0, max_val=EXPERTS - 1)
        fresh = sp.value_load(m["fresh"][0:1, bass.ds(b, 1)], min_val=0, max_val=1)
        with sp.If(fresh == 1):
            for c, (kind, f, a) in enumerate(MOE_CHUNKS):
                w = W[f"w_{kind}_2"][0][e].rearrange("(k p) n -> p k n", p=P)
                sp.wait_ge(*sg.event("raw_used", c, loop=b, back=1))
                sp.dma_start(m["ring"][:, c, :].rearrange("p (k n) -> p k n", k=4),
                             w[:, 4 * a:4 * a + 4, f * 512:(f + 1) * 512]).then_inc(*sg.inc(f"mo_raw{c}", also=[("raw", c)], n=16))
        with sp.If(fresh == 0):
            for c in range(MOE_SLOTS):
                sp.wait_ge(*sg.event("raw_used", c, loop=b, back=1)).then_inc(sg.sem[f"mo_raw{c}"], 16)
    sp.wait_ge(sg.sem["mo_y"], count * 16 + 32)
    sp.dma_start(m["gf"][:], W["normf_g_2"].rearrange("(o d) -> o d", o=1).broadcast_to([P, D])).then_inc(sg.sem["mo_gain"], 16)


def moe_act(act, sg, m, b, W, count):
    act.nop().then_inc(sg.sem["mo_y"], 16)
    with act.Fori(0, count) as i:
        def high(c):
            act.wait_ge(*sg.event("raw", c, loop=i))
            act.wait_ge(*sg.event("w_used", (c - 3) % MOE_SLOTS, loop=i, back=int(c < 3)))
            act.activation(m["mhi"][:, c % 3, :], m["ring"][:, c, :], ACT.Copy).then_inc(*sg.inc("mo_act", also=[("high", c)]))

        def gate(f):
            act.wait_ge(*sg.event("gc", f, loop=i))
            act.activation(m["th"][:], m["gc"][:], ACT.Tanh, scale=SWIGLU_ALPHA / 2).then_inc(*sg.inc("mo_act", also=[("th", f)]))

        def turned(f):
            act.wait_ge(*sg.event("th_t", f, loop=i))
            act.activation(m["hTh"][:, 4 * f:4 * f + 4, :], b[6][:], ACT.Copy, scale=0.5).then_inc(*sg.inc("mo_act", also=[("hTh", f)]))

        def tokens(half):
            act.wait_ge(*sg.event("tx", half, loop=i))
            act.activation(m["xTh"][:, 4 * half:4 * half + 4, :], b[7][:], ACT.Copy).then_inc(*sg.inc("mo_act", also=[("xTh", half)]))

        for c in range(3):
            high(c)
        for o in range(2):
            act.wait_ge(*sg.event("y", o, loop=i, back=1))
            act.activation(m["ysb"][:, o * 512:(o + 1) * 512], b[4 + o][:], ACT.Copy).then_inc(*sg.inc("mo_act", also=[("ycopy", o)]))
        act.wait_ge(*sg.event("ycopy", 1, loop=i))
        act.dma_start(W["ybuf"][bass.ds(i * P, P), :], m["ysb"][:]).then_inc(*sg.inc("mo_y", also=[("stored", None)], n=16))
        high(3)
        high(4)
        gate(0)
        for c in range(5, 9):
            high(c)
        gate(1)
        turned(0)
        high(9)
        tokens(0)
        high(10)
        high(11)
        turned(1)
        tokens(1)
    for o in range(2):
        act.wait_ge(*sg.event("y", o, loop=count, back=1))
        act.activation(m["ysb"][:, o * 512:(o + 1) * 512], b[4 + o][:], ACT.Copy).then_inc(sg.sem["mo_last"], 1)
    act.wait_ge(sg.sem["mo_last"], 2)
    act.dma_start(W["ybuf"][bass.ds(count * P, P), :], m["ysb"][:]).then_inc(sg.sem["mo_y"], 16)


def moe_dve(v, sg, m, b, count):
    f32 = lambda t: t.bitcast(F32)
    with v.Fori(0, count) as i:
        def low(c):
            v.wait_ge(*sg.event("high", c, loop=i))
            v.tensor_tensor(m["mlo"][:, c % 3, :], m["ring"][:, c, :], f32(m["mhi"])[:, c % 3, :],
                            ALU.subtract).then_inc(*sg.inc("mo_low", also=[("raw_used", c), ("low", c)]))

        def gate(f):
            v.wait_ge(*sg.event("g", f, loop=i))
            v.tensor_scalar(m["gc"][:], b[2 * f][:], SWIGLU_LIMIT, None, ALU.min).then_inc(*sg.inc("mo_dve", also=[("gc", f)]))

        def hidden(f):
            gc, uc, th, hh = m["gc"][:], m["uc"][:], m["th"][:], m["hh"][:, f, :]
            v.wait_ge(*sg.event("u", f, loop=i))
            v.tensor_scalar(uc, b[2 * f + 1][:], SWIGLU_LIMIT, -SWIGLU_LIMIT, ALU.min, ALU.max).then_inc(*sg.inc("mo_dve", also=[("uc", f)]))
            v.wait_ge(*sg.event("uc", f, loop=i))
            v.scalar_tensor_tensor(uc, uc, 1.0, gc, ALU.add, ALU.mult).then_inc(*sg.inc("mo_dve", also=[("up", f)]))
            v.wait_ge(*sg.event("up", f, loop=i))
            v.wait_ge(*sg.event("th", f, loop=i))
            v.scalar_tensor_tensor(hh, th, 1.0, uc, ALU.add, ALU.mult).then_inc(*sg.inc("mo_dve", also=[("hh", f)]))

        def turned(f):
            v.wait_ge(*sg.event("hTh", f, loop=i))
            v.scalar_tensor_tensor(m["hTl"][:, 4 * f:4 * f + 4, :], b[6][:].rearrange("p (k n) -> p k n", k=4), 0.5, f32(m["hTh"])[:, 4 * f:4 * f + 4, :],
                                   ALU.mult, ALU.subtract).then_inc(*sg.inc("mo_dve", also=[("hT", f)]))

        def tokens(half):
            v.wait_ge(*sg.event("xTh", half, loop=i))
            v.tensor_tensor(m["xTl"][:, 4 * half:4 * half + 4, :], b[7][:].rearrange("p (k n) -> p k n", k=4), f32(m["xTh"])[:, 4 * half:4 * half + 4, :],
                            ALU.subtract).then_inc(*sg.inc("mo_dve", also=[("xT", half)]))

        for c in range(4):
            low(c)
        gate(0)
        low(4)
        low(5)
        hidden(0)
        low(6)
        low(7)
        gate(1)
        low(8)
        turned(0)
        low(9)
        hidden(1)
        tokens(0)
        low(10)
        turned(1)
        low(11)
        tokens(1)
        v.wait_ge(*sg.event("bias_used", None, loop=i))
        v.tensor_scalar(m["sel"][:], m["pmb"][:], m["bef"][0:96, bass.ds(i + 1, 1)], None,
                        ALU.is_equal).then_inc(*sg.inc("mo_dve", also=[("sel", None)]))


def moe_pe(pe, sg, m, b, count):
    ident = m["K"][:, K_ID:K_ID + P]
    with pe.Fori(0, count) as i:
        def chunk(c, out, xh, xl, *keys):
            kind, f, a = MOE_CHUNKS[c]
            if a == 0:
                ins = pe.matmul(out, m["sel"][:], m["bp"][:, {"gate": 0, "up": D, "down": 2 * D}[kind] + f * 512:][:, 0:512],
                                start=True, stop=False)
                if c == 9:
                    ins.then_inc(*sg.inc("mo_pe", also=[("bias_used", None)]))
            pe.wait_ge(*sg.event("low", c, loop=i))
            for k in range(4):
                w = slice(k * 512, (k + 1) * 512)
                ins = split3(pe, out, xh[:, 4 * a + k, :], xl[:, 4 * a + k, :], m["mhi"][:, c % 3, w], m["mlo"][:, c % 3, w],
                             False, a == 1 and k == 3)
            ins.then_inc(*sg.inc("mo_pe", also=[("w_used", c), *keys]))

        def turn(out, src, *keys):
            for k in range(4):
                ins = pe.transpose(out[:, k * P:(k + 1) * P], src[:, k * P:(k + 1) * P], ident)
            ins.then_inc(*sg.inc("mo_pe", also=[*keys]))

        pe.wait_ge(*sg.event("sel", loop=i, back=1))
        pe.wait_ge(*sg.event("xT", 1, loop=i, back=1))
        x, h = (m["xTh"], m["xTl"]), (m["hTh"], m["hTl"])
        pe.wait_ge(*sg.event("gc", 0, loop=i, back=1))
        chunk(0, b[0][:], *x)
        chunk(1, b[0][:], *x, ("g", 0))
        pe.wait_ge(*sg.event("uc", 0, loop=i, back=1))
        chunk(2, b[1][:], *x)
        chunk(3, b[1][:], *x, ("u", 0))
        pe.wait_ge(*sg.event("gc", 1, loop=i, back=1))
        chunk(4, b[2][:], *x)
        chunk(5, b[2][:], *x, ("g", 1))
        pe.wait_ge(*sg.event("hh", 0, loop=i))
        pe.wait_ge(*sg.event("hT", 1, loop=i, back=1))
        turn(b[6], m["hh"][:, 0, :], ("th_t", 0))
        pe.wait_ge(*sg.event("uc", 1, loop=i, back=1))
        chunk(6, b[3][:], *x)
        chunk(7, b[3][:], *x, ("u", 1))
        pe.wait_ge(*sg.event("gathered", loop=i))
        turn(b[7], m["xg"][:, 0:512], ("tx", 0))
        pe.wait_ge(*sg.event("ycopy", 1, loop=i))
        pe.wait_ge(*sg.event("hT", 0, loop=i))
        chunk(8, b[4][:], *h)
        chunk(9, b[5][:], *h)
        pe.wait_ge(*sg.event("hh", 1, loop=i))
        turn(b[6], m["hh"][:, 1, :], ("th_t", 1))
        pe.wait_ge(*sg.event("xT", 0, loop=i))
        turn(b[7], m["xg"][:, 512:1024], ("tx", 1))
        pe.wait_ge(*sg.event("hT", 1, loop=i))
        chunk(10, b[4][:], *h, ("y", 0))
        chunk(11, b[5][:], *h, ("y", 1))


def moe_pool(pool, sg, m, W, count):
    with pool.Fori(0, count) as i:
        pool.wait_ge(*sg.event("stored", loop=i))
        pool.tensor_copy(m["idx"][:], m["tokcol"][:, bass.ds(i + 1, 1)]).then_inc(sg.sem["mo_idx"], 1)
        pool.wait_ge(sg.sem["mo_idx"], 1)
        pool.indirect_dma_start(m["xg"][:], None, W["h2tok"][:, :], bass.IndirectOffsetOnAxis(m["idx"][:, 0:1], 0)).then_inc(*sg.inc("mo_x", also=[("gathered", None)], n=16))
        pool.sem_clear(sg.sem["mo_idx"])


FINAL_SIGNALS = "fi_g0 fi_g1 fi_g2 fi_g3  fi_dve fi_act fi_out fi_step"


def final_program(engine, who, sg, m, W, mo):
    if who == "sp":
        for t in range(NT):
            engine.wait_ge(*sg.event("done", t))
            engine.dma_start(W["out"][0, t * P:(t + 1) * P, :], m["ot"][:, t, :]).then_inc(sg.sem["fi_out"], 16)
        engine.wait_ge(sg.sem["fi_out"], 16 * NT)
    if who == "pool":
        for t in range(NT):
            for k in range(TOP):
                engine.indirect_dma_start(m["fy"][:, 4 * t + k, :], None, W["ybuf"][:, :],
                                                  bass.IndirectOffsetOnAxis(m["dest"][:, 4 * k + t:4 * k + t + 1], 0)).then_inc(*sg.inc(f"fi_g{t}", also=[("fy", t)], n=16))
    if who == "dve":
        v = engine

        def norm(t):
            v.wait_ge(*sg.event("root", t))
            v.reciprocal(m["fs"][:, t:t + 1], m["fs"][:, t:t + 1]).then_inc(*sg.inc("fi_step"))
            v.wait_ge(*sg.last("fi_step"))
            v.scalar_tensor_tensor(m["ot"][:, t, :], m["x2t"][:, t, :], m["fs"][:, t:t + 1], m["gf"][:], ALU.mult, ALU.mult).then_inc(*sg.inc("fi_dve", ("done", t), also=[("done", t)]))

        v.wait_ge(mo.sem["mo_gain"], 16)
        for t in range(NT):
            x = m["x2t"][:, t, :]
            v.wait_ge(*sg.event("fy", t))
            for k in range(TOP):
                ins = v.scalar_tensor_tensor(x, m["fy"][:, 4 * t + k, :], m["gates"][:, 4 * t + k:4 * t + k + 1], x, ALU.mult, ALU.add)
                if k < TOP - 1:
                    ins.then_inc(*sg.inc("fi_step"))
                    v.wait_ge(*sg.last("fi_step"))
            ins.then_inc(*sg.inc("fi_dve", ("sum", t), also=[("sum", t)]))
            if t:
                norm(t - 1)
        norm(NT - 1)
    if who == "act":
        for t in range(NT):
            engine.wait_ge(*sg.event("sum", t))
            engine.activation(m["fq"][:, t % 2, :], m["x2t"][:, t, :], ACT.Square, accum_out=m["fs"][:, t:t + 1]).then_inc(*sg.inc("fi_act", ("fsq", t), also=[("fsq", t)]))
            engine.wait_ge(*sg.event("fsq", t))
            engine.activation(m["fs"][:, t:t + 1], m["fs"][:, t:t + 1], ACT.Sqrt, bias=m["K"][:, K_E5:K_E5 + 1], scale=1.0 / D).then_inc(*sg.inc("fi_act", ("root", t), also=[("root", t)]))


SWIGLU_LIMIT, SWIGLU_ALPHA = 7.0, 1.702


def moe_tensors(at):
    at("x2t", 16, [P, NT, D])
    at("h2T", 32, [P, KD, S])
    at("sqm", 48, [P, 2, S])
    at("h2t", 48, [P, NT, D])
    at("wr", 60, [P, KD, EXPERTS])
    at("bf", 64, [96, 3 * D])
    at("br", 76, [96, 3 * D])
    at("bp", 94, [96, 3 * D], BF16)
    for base, names in ((88, (("oh", [P, TOP, P]), ("L", [P, P]), ("M", [P, P]), ("sr", [P, P]), ("pr", [P, P]), ("rk", [P, P]),
                              ("rb", [P, P]), ("i128", [P, P]), ("lt", [P, P]))),
                        (196, (("rstdm", [P, S]),)),
                        (198, (("mxm", [P, 32]), ("mi", [P, 32], U32), ("mif", [P, 32]), ("nmx", [P, 4]), ("gs", [P, 4]),
                               ("pk", [P, 16]), ("bk", [P, 16]), ("df", [P, 16]), ("dest", [P, 16], U32), ("gates", [P, 16]),
                               ("cnt", [P, 32]), ("nb", [P, 32]), ("incl", [P, 32]), ("excl", [P, 32]), ("i32", [P, 32]),
                               ("bef", [P, NB + 1]), ("bei", [1, NB + 1], I32), ("fresh", [1, NB + 1], I32), ("i48", [P, NB + 1]), ("brow", [1, 32]),
                               ("ohp", [P, 2, P]), ("ohb", [P, 2, NB + 1]), ("tokcol", [P, NB + 1], U32), ("idx", [P, 1], U32),
                               ("fs", [P, 4])))):
        o = base * KB
        for name, shape, *dt in names:
            at(name, o / KB, shape, *dt)
            size = 4
            for n in shape[1:]:
                size *= n
            o += (size + 31) // 32 * 32
        assert o <= {88: 94, 196: 198, 198: 202.125}[base] * KB, (base, o / KB)
    at("ring", 100, [P, MOE_SLOTS, SLOT])
    at("xg", 0, [P, D])
    at("ysb", 0, [P, D])
    at("xTh", 4, [P, KD, P], F32R)
    at("xTl", 8, [P, KD, P], F32R)
    at("hTh", 12, [P, KD, P], F32R)
    at("hTl", 32, [P, KD, P], F32R)
    at("gc", 36, [P, S])
    at("th", 38, [P, S])
    at("uc", 40, [P, S])
    at("hh", 42, [P, 2, S])
    at("mhi", 46, [P, 3, SLOT], F32R)
    at("mlo", 70, [P, 3, SLOT], F32R)
    at("cntc", 197, [32, 1])
    at("nbc", 197.125, [32, 1])
    at("nbf", 197.25, [32, 1])
    at("cmp", 197.375, [32, NB + 1])
    at("sel", 196, [96, P], BF16)
    at("pmb", 196.5, [96, P], BF16)
    at("fy", 100, [P, 16, D])
    at("gf", 48, [P, D])
    at("ot", 168, [P, NT, D])
    at("fq", 184, [P, 2, D])


AS_THEY_ARE = ["x", "positions", "w_ada", "w_in", "lru_wa", "lru_wx", "w_uq", "w_ukv", "w_out", "w_ffn_in", "w_ffn_out",
               "w_in_2", "w_out_2", "pool_w_2", "w_router_2", "b_router_2", "w_gate_2", "b_gate_2", "w_up_2", "b_up_2",
               "w_down_2", "b_down_2", "normf_g_2"]


def kernel(**inputs):
    import concourse.bacc as _bacc
    from concourse.bass_utils import run_bass_kernel_spmd as _run

    arrays = {n: np.ascontiguousarray(inputs[n]) for n in AS_THEY_ARE}
    arrays["c_cols"] = columns(inputs["c"])
    arrays["vecs"] = np.stack([layer_vectors(inputs, l) for l in range(DEPTH)])
    arrays["vecs2"] = block_vectors(inputs)
    arrays["consts"], arrays["sel4"] = constants(), head_selectors()

    at = {}
    for _ in range(2):
        nc = _bacc.Bacc("TRN2", target_bir_lowering=False, num_devices=1)
        W = {n: nc.dram_tensor(n, a.shape, mybir.dt.from_np(a.dtype), kind="ExternalInput").ap() for n, a in arrays.items()}
        W["out"] = nc.dram_tensor("out", (1, S, D), F32, kind="ExternalOutput").ap()
        program(nc, W, at)
    r = _run(nc, [arrays], core_ids=[0])
    return r.results[0]["out"]
```
